# Optimizing a Trainium2 kernel written in Bass

```python
import math
import jax, jax.numpy as jnp
from jax import lax
import numpy as np

D_MODEL = 1024
BATCH = 1
SEQ = 256
DEPTH = 2

N_META = 16
N_HEADS = 16
N_KV_HEADS = 4
HEAD_DIM = 64
GROUP = N_HEADS // N_KV_HEADS
WINDOW = 128
BLOCK = 128
ATTN_SCALE = 1.0 / math.sqrt(HEAD_DIM)
Q_DIM = N_HEADS * HEAD_DIM
KV_DIM = N_KV_HEADS * HEAD_DIM
QKV_DIM = Q_DIM + 2 * KV_DIM
NEG_INF = -1e30
NUM_BUCKETS = 32
MAX_EXACT = NUM_BUCKETS // 2
MAX_DISTANCE = 128
RWKV_HEAD = 64
RWKV_HEADS = D_MODEL // RWKV_HEAD
D_DECAY_LORA = 64
D_AAA_LORA = 64
D_GATE_LORA = 160
GN_EPS = 64e-5
D_FF = int(round(8 * D_MODEL / 3 / 256)) * 256
N_EXPERTS = 8
TOP_K = 2
D_FF_EXPERT = 7 * D_MODEL // 2
ALPHA = (2 * DEPTH) ** 0.25
BETA = (8 * DEPTH) ** -0.25
LN_EPS = 1e-5
N_ATTN = (DEPTH + 1) // 2
N_RWKV = DEPTH // 2

kernel_name = "hybrid_swa_sink_rwkv7_moe_deepnorm"

def layer_norm(x, g, b):
    xf = x.astype(jnp.float32)
    mu = jnp.mean(xf, axis=-1, keepdims=True)
    var = jnp.mean(jnp.square(xf - mu), axis=-1, keepdims=True)
    y = (xf - mu) * lax.rsqrt(var + LN_EPS) * g.astype(jnp.float32) + b.astype(jnp.float32)
    return y.astype(x.dtype)

def t5_bucket(dist):
    n = jnp.maximum(dist, 0)
    is_small = n < MAX_EXACT
    nf = jnp.maximum(n, 1).astype(jnp.float32)
    large = MAX_EXACT + (jnp.log(nf / MAX_EXACT) / math.log(MAX_DISTANCE / MAX_EXACT)
                         * (NUM_BUCKETS - MAX_EXACT)).astype(jnp.int32)
    large = jnp.minimum(large, NUM_BUCKETS - 1)
    return jnp.where(is_small, n, large)

def sliding_window_attention(x, w_qkv, b_qkv, sinks, rel_bias, w_o):
    B, L, _ = x.shape
    pad = BLOCK - N_META
    qkv = jnp.einsum('bld,de->ble', x, w_qkv) + b_qkv
    qkv = jnp.pad(qkv, ((0, 0), (pad, 0), (0, 0)))
    Lp = L + pad
    nb = Lp // BLOCK
    q = qkv[..., :Q_DIM].reshape(B, nb, BLOCK, N_KV_HEADS, GROUP, HEAD_DIM) * ATTN_SCALE
    k = qkv[..., Q_DIM:Q_DIM + KV_DIM].reshape(B, nb, BLOCK, N_KV_HEADS, HEAD_DIM)
    v = qkv[..., Q_DIM + KV_DIM:].reshape(B, nb, BLOCK, N_KV_HEADS, HEAD_DIM)

    def band(t):
        prev = jnp.concatenate([jnp.zeros_like(t[:, :1]), t[:, :-1]], axis=1)
        return jnp.concatenate([prev, t], axis=2)

    k_band, v_band = band(k), band(v)
    k_meta = k[:, 0, pad:]
    v_meta = v[:, 0, pad:]

    s_band = jnp.einsum('bnqhgd,bnkhd->bnhgqk', q, k_band).astype(jnp.float32)
    s_meta = jnp.einsum('bnqhgd,bmhd->bnhgqm', q, k_meta).astype(jnp.float32)

    blk = jnp.arange(nb)[:, None]
    q_pos = blk * BLOCK + jnp.arange(BLOCK)[None, :] - pad
    kb_pos = (blk - 1) * BLOCK + jnp.arange(2 * BLOCK)[None, :] - pad
    d_band = BLOCK + jnp.arange(BLOCK)[:, None] - jnp.arange(2 * BLOCK)[None, :]
    ok_band = ((d_band >= 0) & (d_band < WINDOW))[None] & (kb_pos[:, None, :] >= 0)
    d_meta = q_pos[:, :, None] - jnp.arange(N_META)[None, None, :]
    ok_meta = d_meta >= WINDOW

    rb = rel_bias.astype(jnp.float32)
    bias_band = rb[t5_bucket(d_band)].transpose(2, 0, 1).reshape(N_KV_HEADS, GROUP, BLOCK, 2 * BLOCK)
    bias_meta = rb[t5_bucket(d_meta)].transpose(0, 3, 1, 2).reshape(nb, N_KV_HEADS, GROUP, BLOCK, N_META)

    s_band = jnp.where(ok_band[None, :, None, None], s_band + bias_band, NEG_INF)
    s_meta = jnp.where(ok_meta[None, :, None, None], s_meta + bias_meta[None], NEG_INF)

    sink = sinks.astype(jnp.float32).reshape(N_KV_HEADS, GROUP)[None, None, :, :, None]
    m = jnp.maximum(jnp.maximum(jnp.max(s_band, -1), jnp.max(s_meta, -1)), sink)
    p_band = jnp.exp(s_band - m[..., None])
    p_meta = jnp.exp(s_meta - m[..., None])
    denom = p_band.sum(-1) + p_meta.sum(-1) + jnp.exp(sink - m)
    o = (jnp.einsum('bnhgqk,bnkhd->bnqhgd', p_band, v_band.astype(jnp.float32))
         + jnp.einsum('bnhgqm,bmhd->bnqhgd', p_meta, v_meta.astype(jnp.float32)))
    o = o / denom.transpose(0, 1, 4, 2, 3)[..., None]
    o = o.reshape(B, Lp, Q_DIM)[:, pad:].astype(x.dtype)
    return jnp.einsum('ble,ed->bld', o, w_o)

def wkv7_scan(r, w, k, v, a, b):
    B, L, H, N = r.shape
    xs = tuple(t.astype(jnp.float32).transpose(1, 0, 2, 3) for t in (r, w, k, v, a, b))

    def step(S, inp):
        r_t, w_t, k_t, v_t, a_t, b_t = inp
        sa = jnp.einsum('bhij,bhj->bhi', S, a_t)
        S = S * w_t[:, :, None, :] + sa[..., None] * b_t[:, :, None, :] + v_t[..., None] * k_t[:, :, None, :]
        y = jnp.einsum('bhij,bhj->bhi', S, r_t)
        return S, y

    S0 = jnp.zeros((B, H, N, N), jnp.float32)
    _, ys = lax.scan(step, S0, xs)
    return ys.transpose(1, 0, 2, 3)

def rwkv7_time_mix(x, mu, w0, w1, w2, a0, a1, a2, g1, g2, k_k, k_a, r_k, w_rkv, lnx_g, lnx_b, w_o):
    B, L, D = x.shape
    H, N = RWKV_HEADS, RWKV_HEAD
    xx = jnp.pad(x, ((0, 0), (1, 0), (0, 0)))[:, :-1] - x
    xr = x + xx * mu[0]
    xw = x + xx * mu[1]
    xk = x + xx * mu[2]
    xv = x + xx * mu[3]
    xa = x + xx * mu[4]
    xg = x + xx * mu[5]
    r = xr @ w_rkv[0]
    k = xk @ w_rkv[1]
    v = xv @ w_rkv[2]
    w = -jax.nn.softplus(-(w0 + jnp.tanh(xw @ w1) @ w2).astype(jnp.float32)) - 0.5
    a = jax.nn.sigmoid((a0 + (xa @ a1) @ a2).astype(jnp.float32))
    g = jax.nn.sigmoid(xg @ g1) @ g2

    r = r.astype(jnp.float32).reshape(B, L, H, N)
    k = k.astype(jnp.float32)
    v = v.astype(jnp.float32).reshape(B, L, H, N)
    kk = (k * k_k.astype(jnp.float32)).reshape(B, L, H, N)
    kk = kk / jnp.maximum(jnp.sqrt(jnp.sum(kk * kk, -1, keepdims=True)), 1e-12)
    k = (k * (1.0 + (a - 1.0) * k_a.astype(jnp.float32))).reshape(B, L, H, N)
    a = a.reshape(B, L, H, N)
    decay = jnp.exp(-jnp.exp(w)).reshape(B, L, H, N)

    y = wkv7_scan(r, decay, k, v, -kk, kk * a)
    mu_y = jnp.mean(y, -1, keepdims=True)
    var_y = jnp.mean(jnp.square(y - mu_y), -1, keepdims=True)
    y = ((y - mu_y) * lax.rsqrt(var_y + GN_EPS)).reshape(B, L, D)
    y = y * lnx_g.astype(jnp.float32) + lnx_b.astype(jnp.float32)
    bonus = jnp.sum(r * k * r_k.astype(jnp.float32), -1, keepdims=True) * v
    y = (y + bonus.reshape(B, L, D)).astype(x.dtype)
    return (y * g) @ w_o

def swiglu(t, w_gu, w_down):
    gu = t @ w_gu
    gate, up = jnp.split(gu, 2, axis=-1)
    return (jax.nn.silu(gate) * up) @ w_down

def moe_swiglu(x, w_router, w_gu, w_down):
    B, L, D = x.shape
    t = x.reshape(B * L, D)
    logits = (t @ w_router).astype(jnp.float32)
    top_v, top_i = lax.top_k(logits, TOP_K)
    top_w = jax.nn.softmax(top_v, axis=-1)
    gates = jnp.sum(jax.nn.one_hot(top_i, N_EXPERTS, dtype=jnp.float32) * top_w[..., None], axis=1)
    out = jnp.zeros_like(t)
    for e in range(N_EXPERTS):
        out = out + gates[:, e:e + 1].astype(t.dtype) * swiglu(t, w_gu[e], w_down[e])
    return out.reshape(B, L, D)

def setup_inputs(seed: int = 0) -> dict:
    key = jax.random.key(seed)
    ks = iter(jax.random.split(key, 48))
    f32 = jnp.float32

    def nrm(shape, scale):
        return jax.random.normal(next(ks), shape, f32) * scale

    D = D_MODEL
    return {
        "x": nrm((BATCH, SEQ, D), 1.0),
        "meta_tokens": nrm((N_META, D), 1.0),
        "rel_bias": nrm((NUM_BUCKETS, N_HEADS), 0.5),
        "ln_mix_g": 1.0 + nrm((DEPTH, D), 0.02),
        "ln_mix_b": nrm((DEPTH, D), 0.02),
        "ln_ffn_g": 1.0 + nrm((DEPTH, D), 0.02),
        "ln_ffn_b": nrm((DEPTH, D), 0.02),
        "attn_w_qkv": nrm((N_ATTN, D, QKV_DIM), D ** -0.5),
        "attn_b_qkv": nrm((N_ATTN, QKV_DIM), 0.02),
        "attn_sinks": nrm((N_ATTN, N_HEADS), 0.5),
        "attn_w_o": nrm((N_ATTN, Q_DIM, D), Q_DIM ** -0.5 * BETA),
        "rwkv_mu": jax.random.uniform(next(ks), (N_RWKV, 6, D), f32),
        "rwkv_w0": jax.random.uniform(next(ks), (N_RWKV, D), f32, minval=-6.5, maxval=-1.5),
        "rwkv_w1": nrm((N_RWKV, D, D_DECAY_LORA), D ** -0.5),
        "rwkv_w2": nrm((N_RWKV, D_DECAY_LORA, D), 0.1 * D_DECAY_LORA ** -0.5),
        "rwkv_a0": nrm((N_RWKV, D), 0.1),
        "rwkv_a1": nrm((N_RWKV, D, D_AAA_LORA), D ** -0.5),
        "rwkv_a2": nrm((N_RWKV, D_AAA_LORA, D), 0.1 * D_AAA_LORA ** -0.5),
        "rwkv_g1": nrm((N_RWKV, D, D_GATE_LORA), D ** -0.5),
        "rwkv_g2": nrm((N_RWKV, D_GATE_LORA, D), D_GATE_LORA ** -0.5),
        "rwkv_k_k": 0.85 + nrm((N_RWKV, D), 0.02),
        "rwkv_k_a": 1.0 + nrm((N_RWKV, D), 0.02),
        "rwkv_r_k": -0.04 + nrm((N_RWKV, RWKV_HEADS, RWKV_HEAD), 0.1),
        "rwkv_w_rkv": nrm((N_RWKV, 3, D, D), D ** -0.5),
        "rwkv_lnx_g": 1.0 + nrm((N_RWKV, D), 0.02),
        "rwkv_lnx_b": nrm((N_RWKV, D), 0.02),
        "rwkv_w_o": nrm((N_RWKV, D, D), D ** -0.5 * BETA),
        "ffn_w_gu": nrm((N_ATTN, D, 2 * D_FF), D ** -0.5),
        "ffn_w_down": nrm((N_ATTN, D_FF, D), D_FF ** -0.5 * BETA),
        "moe_router": nrm((N_RWKV, D, N_EXPERTS), D ** -0.5),
        "moe_w_gu": nrm((N_RWKV, N_EXPERTS, D, 2 * D_FF_EXPERT), D ** -0.5),
        "moe_w_down": nrm((N_RWKV, N_EXPERTS, D_FF_EXPERT, D), D_FF_EXPERT ** -0.5 * BETA),
    }

def reference(x, meta_tokens, rel_bias, ln_mix_g, ln_mix_b, ln_ffn_g, ln_ffn_b,
              attn_w_qkv, attn_b_qkv, attn_sinks, attn_w_o,
              rwkv_mu, rwkv_w0, rwkv_w1, rwkv_w2, rwkv_a0, rwkv_a1, rwkv_a2,
              rwkv_g1, rwkv_g2, rwkv_k_k, rwkv_k_a, rwkv_r_k, rwkv_w_rkv,
              rwkv_lnx_g, rwkv_lnx_b, rwkv_w_o,
              ffn_w_gu, ffn_w_down, moe_router, moe_w_gu, moe_w_down):
    B = x.shape[0]
    meta = jnp.broadcast_to(meta_tokens.astype(x.dtype)[None], (B, N_META, D_MODEL))
    h = jnp.concatenate([meta, x], axis=1)
    for i in range(DEPTH):
        j = i // 2
        if i % 2 == 0:
            y = sliding_window_attention(h, attn_w_qkv[j], attn_b_qkv[j], attn_sinks[j], rel_bias, attn_w_o[j])
        else:
            y = rwkv7_time_mix(h, rwkv_mu[j], rwkv_w0[j], rwkv_w1[j], rwkv_w2[j], rwkv_a0[j], rwkv_a1[j],
                               rwkv_a2[j], rwkv_g1[j], rwkv_g2[j], rwkv_k_k[j], rwkv_k_a[j], rwkv_r_k[j],
                               rwkv_w_rkv[j], rwkv_lnx_g[j], rwkv_lnx_b[j], rwkv_w_o[j])
        h = layer_norm(ALPHA * h + y, ln_mix_g[i], ln_mix_b[i])
        if i % 2 == 0:
            y = swiglu(h, ffn_w_gu[j], ffn_w_down[j])
        else:
            y = moe_swiglu(h, moe_router[j], moe_w_gu[j], moe_w_down[j])
        h = layer_norm(ALPHA * h + y, ln_ffn_g[i], ln_ffn_b[i])
    return h[:, N_META:]


_drawn_inputs = setup_inputs


def setup_inputs(seed=0):
    import zlib

    import numpy as np

    out = dict(_drawn_inputs(seed))
    spreads = {}
    factors = {'attn_b_qkv': 4.871,
     'attn_sinks': 8.0,
     'rwkv_w1': 8.0,
     'rwkv_w2': 8.0,
     'rwkv_a0': 5.306,
     'rwkv_a1': 4.41,
     'rwkv_a2': 4.172,
     'rwkv_k_k': 16.672,
     'rwkv_k_a': 7.293,
     'rwkv_lnx_g': 15.24,
     'rwkv_lnx_b': 13.818}
    for name, (base, spread) in spreads.items():
        noise = np.random.default_rng([zlib.crc32(name.encode()), seed]).standard_normal(out[name].shape)
        drawn = base * np.exp(spread * noise) if base else spread * noise
        out[name] = __import__('jax').numpy.asarray(drawn.astype(out[name].dtype))
    for name, factor in factors.items():
        out[name] = (out[name] * factor).astype(out[name].dtype)
    return out
```

```python
from contextlib import ExitStack

import numpy as np

import concourse.bass as bass
from concourse import mybir
from concourse.alu_op_type import AluOpType as ALU

F32 = mybir.dt.float32
ACT = mybir.ActivationFunctionType
AX = mybir.AxisListType

P = 128
D = 1024
KC = D // P
N_META, SEQ = 16, 256
T = N_META + SEQ
HEADS, KV_HEADS, HD = 16, 4, 64
WINDOW = 128
D_FF, D_FFE, EXPERTS = 2816, 3584, 8
FT, FTE = D_FF // P, D_FFE // P
ALPHA = 4 ** 0.25
LN_EPS, GN_EPS = 1e-5, 64e-5
DECAY = float(np.exp(-0.5))
NEG = -1e30

TILES = 16
SLOTS = 7
SL_QK, SL_V, SL_WO = 0, 5, 6
SL_GU = SL_WO + 4
SL_DN = SL_GU + FT
SL_RKV = SL_DN + FT * KC // TILES
SL_O2 = SL_RKV + 12
SL_MOE = SL_O2 + 4
SL_EXPERT = FTE + FTE * KC // TILES
N_SLABS = SL_MOE + EXPERTS * SL_EXPERT

Q_TILES = [(0, 96, 96), (96, 96, 192), (192, 80, 272)]
KN_AT = [0, 96, 288]
KN_ALL = 560
Q_MAX = 96
LINE = 2 * T - 1

CH = 64
N_CH = -(-T // CH)
TP = N_CH * CH
LEVELS = [2, 4, 8, 16, 32]

VECS = ["g0", "b0", "g1", "b1", "g2", "b2", "g3", "b3", "mu_r", "mu_k", "mu_v", "mu_w", "mu_a", "mu_g",
        "w0", "a0", "k_k", "k_a", "r_k", "lnx_g", "lnx_b", "b_q"]
VCOL = {n: KC * i for i, n in enumerate(VECS)}
VCOL["b_k"] = KC * len(VECS)
N_VEC = KC * len(VECS) + 2
PRE_BONUS, PRE_LAST = 9, 14
CD_IN = 6
CD_MASKED = CD_IN + 11
CD = CD_MASKED + 4 * len(LEVELS) + 5
CP = 8 + 3 * len(LEVELS) + 4
PRE_ST = 0
RT_EXP, RT_GATES = 12, 16
HB = 2 * FT
MASKS = ["low2", "low2T", "upper", "upper_eq"] + [f"off{b}" for b in LEVELS] + ["eye64"]


def build(nc, A, OUT):
    ctx = ExitStack()
    with ctx:
        def sb(name, shape):
            return ctx.enter_context(nc.sbuf_tensor(name, shape, F32))

        def sem(name):
            return ctx.enter_context(nc.semaphore(name))

        ring = sb("ring", [P, SLOTS, TILES * P])
        h = sb("h", [P, KC, T])
        z = sb("z", [P, KC, T])
        sq = sb("sq", [P, KC, T])
        rstd = sb("rstd", [P, T])
        eye = sb("eye", [P, P])
        ones_d = sb("ones_d", [P, P])
        same_head = sb("same_head", [P, P])
        mean_head = sb("mean_head", [P, P])
        masks = sb("masks", [P, len(MASKS), CH])
        vec = sb("vec", [P, N_VEC])
        arena = sb("arena", [P, 28800])
        PS = ctx.enter_context(nc.psum_tensor("PS", [P, 8, 512], F32))
        scratch = nc.dram_tensor("bias_lines", (HEADS, Q_MAX, 2 * LINE), F32, kind="Internal").ap()

        def carve(start, *shape):
            n = int(np.prod(shape))
            assert start + n <= 28800, (start, shape)
            v = arena[:, start:start + n]
            if len(shape) == 1:
                return v
            names = "abcd"[:len(shape)]
            return v.rearrange(f"p ({' '.join(names)}) -> p {' '.join(names)}", **dict(zip(names, shape)))

        def v_of(name, m):
            return vec[:, VCOL[name] + m:VCOL[name] + m + 1]

        def v_all(name, n=T):
            return vec[:, VCOL[name]:VCOL[name] + KC].unsqueeze(2).broadcast_to([P, KC, n])

        qk = carve(0, 10, T)
        vn = carve(2720, 3, 256)
        bias = carve(3488, HEADS * KN_ALL)
        sb_ = carve(12448, 2, 2, T + 1)
        pr = carve(13540, 2, 2, T + 1)
        prT = carve(14632, 2, 2, 3, 96)
        oT = carve(15784, KC, T)
        line = carve(17960, 2 * LINE)
        onehot = carve(19046, 2 * LINE)
        rbias = carve(20132, HEADS)
        bv = carve(20148, 256)
        sinks = carve(20404, HEADS)
        mx = carve(20420, 2)
        negm = carve(20422, 2, 2)
        den = carve(20426, 2, 2)
        rden = carve(20430, 2)
        ones_row = carve(20432, P)

        def bias_of(t):
            qn, kn = Q_TILES[t][1:]
            s = HEADS * KN_AT[t]
            return bias[:, s:s + HEADS * kn].rearrange("p (h k) -> p h k", h=HEADS)

        hid = carve(0, FTE, T)
        sg = carve(7616, T)
        gu = carve(7888, T)
        gate_b = carve(8160, EXPERTS, T)
        router = carve(10336, KC, EXPERTS)
        lg = carve(10400, 3, EXPERTS)
        cmp_a = carve(10424, 3, EXPERTS, EXPERTS)
        cmp_b = carve(10616, 3, EXPERTS, EXPERTS)
        before = carve(10808, EXPERTS, EXPERTS)
        sel = carve(10872, 3, EXPERTS)
        ex = carve(10896, 3, EXPERTS)
        top = carve(10920, 3)
        gates = carve(10923, 3, EXPERTS)

        r_ = carve(0, KC, TP)
        k_ = carve(2560, KC, TP)
        kk = carve(5120, KC, TP)
        a_ = carve(7680, KC, TP)
        v_ = carve(10240, KC, TP)
        cum = carve(12800, KC, TP)
        g_ = carve(15360, KC, T)
        OV = 17536
        mix = carve(OV, 2, KC, T)
        lora1 = carve(OV + 4352, KC, 288)
        lora2 = carve(OV + 6656, 4, D)
        (e1, em, rt, at, bt, kt, vc, ltm, tm, ttm, um, otm, mak, mrb, mrk, vnat, bnat, knat, xm, sam, st) = [
            carve(OV + 512 * i, KC, CH) for i in range(21)]
        low, lowT = vc, ltm

        def bank(b):
            return PS[:, b, :].rearrange("p (m t) -> p m t", m=KC)

        def mask(name):
            i = MASKS.index(name)
            return masks[:, i:i + 1, :].broadcast_to([P, KC, CH])

        loaded = [sem(f"slab_loaded{j}") for j in range(SLOTS)]
        slab_begun = sem("slab_begun")
        s_const = sem("consts_loaded")
        s_attn = sem("attn_consts_loaded")
        s_h0 = sem("h0_loaded")
        s_lora = sem("lora_loaded")
        s_router = sem("router_loaded")
        s_line_ps = sem("bias_line_in_psum")
        s_line = sem("bias_line_kept")
        s_line_out = sem("bias_line_stored")
        s_bias = sem("bias_loaded")
        s_ones = sem("ones_row_set")
        qkv_ps, qkv_kept = sem("qkv_in_psum"), sem("qkv_kept")
        sc_ps, sc_dve = sem("scores_in_psum"), sem("scores_dve_steps")
        sc_exp, sc_norm = sem("probs_exponentiated"), sem("probs_normalised")
        nrm = sem("norm_steps")
        pT_ps, pT_kept = sem("probs_T_in_psum"), sem("probs_T_kept")
        o_ps, o_kept = sem("attn_out_in_psum"), sem("attn_out_kept")
        y_ps = [sem(f"sublayer{i}_out_in_psum") for i in range(4)]
        zsum = [sem(f"residual{i}_added") for i in range(4)]
        ln_pe = [sem(f"ln{i}_sums") for i in range(4)]
        ln_dve = [sem(f"ln{i}_vector_steps") for i in range(4)]
        ln_act = [sem(f"ln{i}_scalar_steps") for i in range(4)]
        gu_ps, gu_sig, hid_dve = sem("gate_up_in_psum"), sem("gate_sigmoid"), sem("hidden_steps")
        mixed, xx_steps = sem("mixed"), sem("shift_steps")
        rkv_ps, rkv_kept = sem("rkv_in_psum"), sem("rkv_kept")
        l1_ps, l1_kept = sem("lora_in_psum"), sem("lora_kept")
        l2_ps, l2_kept = sem("lora_out_in_psum"), sem("lora_out_kept")
        pads = sem("pads_cleared")
        pre_dve, pre_act, pre_pe = sem("prep_vector_steps"), sem("prep_scalar_steps"), sem("prep_sums")
        c_dve, c_act, c_pe = sem("chunk_vector_steps"), sem("chunk_scalar_steps"), sem("chunk_products")
        gn_dve, gn_act, gn_pe = sem("gn_vector_steps"), sem("gn_scalar_steps"), sem("gn_sums")
        rt_pe, rt_dve, rt_act = sem("router_products"), sem("router_vector_steps"), sem("router_scalar_steps")
        s_out = sem("out_stored")

        block = ctx.enter_context(nc.Block())

        @block.sync
        def _(sp):
            sp.dma_start(h[:, :, :], A["h0"]).then_inc(s_h0, 16)
            for j in range(SLOTS):
                sp.dma_start(ring[:, j, :], A["slabs"][j, :, :]).then_inc(loaded[j], 16)
            with sp.Fori(1, N_SLABS // SLOTS) as i:
                for j in range(SLOTS):
                    sp.wait_ge(slab_begun, SLOTS * i + (j - SLOTS + 2))
                    sp.dma_start(ring[:, j:j + 1, :],
                                 A["slabs"][bass.ds(SLOTS * i + j, 1), :, :].rearrange("s p c -> p s c"))\
                      .then_inc(loaded[j], 16)
            for n in range(N_SLABS // SLOTS * SLOTS, N_SLABS):
                sp.wait_ge(slab_begun, n - SLOTS + 2)
                sp.dma_start(ring[:, n % SLOTS, :], A["slabs"][n, :, :]).then_inc(loaded[n % SLOTS], 16)
            sp.wait_ge(ln_act[3], 10)
            sp.dma_start(OUT, h[:, :, N_META:T]).then_inc(s_out, 16)
            sp.wait_ge(s_out, 16)

        @block.gpsimd
        def _(pool):
            pool.dma_start(onehot[0:33, :], A["onehot"]).then_inc(s_attn, 16)
            pool.dma_start(rbias[0:33, :], A["rel_bias"]).then_inc(s_attn, 16)
            pool.dma_start(bv[0:1, :], A["b_v"]).then_inc(s_attn, 16)
            pool.dma_start(sinks[:, :], A["sinks"].broadcast_to([P, HEADS])).then_inc(s_attn, 16)
            pool.dma_start(vec[:, :], A["vecs"]).then_inc(s_const, 16)
            pool.dma_start(eye[:, :], A["squares"][:, 0:P]).then_inc(s_const, 16)
            pool.dma_start(ones_d[:, :], A["squares"][:, P:2 * P]).then_inc(s_const, 16)
            pool.dma_start(same_head[:, :], A["squares"][:, 2 * P:3 * P]).then_inc(s_const, 16)
            pool.dma_start(mean_head[:, :], A["squares"][:, 3 * P:4 * P]).then_inc(s_const, 16)
            pool.dma_start(masks[:, :, :], A["masks"]).then_inc(s_const, 16)
            pool.memset(ones_row[0:1, :], 1.0).then_inc(s_ones, 1)
            pool.wait_ge(s_line, 3)
            pool.dma_start(scratch, line[0:HEADS, :].unsqueeze(1).broadcast_to([HEADS, Q_MAX, 2 * LINE]))\
                .then_inc(s_line_out, 16)
            pool.wait_ge(s_line_out, 16)
            for t, (q0, qn, kn) in enumerate(Q_TILES):
                for s, k0, k1 in ((0, 0, N_META), (1, N_META, kn)):
                    src = bass.AP(tensor=scratch.tensor, offset=s * LINE + T - 1 - q0 + k0,
                                  ap=[[2 * LINE - 1, qn], [Q_MAX * 2 * LINE, HEADS], [1, k1 - k0]])
                    pool.dma_start(bias_of(t)[0:qn, :, k0:k1], src).then_inc(s_bias, 16)
            pool.wait_ge(ln_act[1], 10)
            pool.wait_ge(y_ps[1], 8)
            pool.dma_start(lora1[:, :, :], A["lora1"]).then_inc(s_lora, 16)
            pool.dma_start(lora2[:, :, :], A["lora2"]).then_inc(s_lora, 16)
            pool.wait_ge(ln_act[2], 10)
            pool.dma_start(router[:, :, :], A["router"]).then_inc(s_router, 16)
            pool.dma_start(before[:, :, :], A["before"]).then_inc(s_router, 16)

        @block.tensor
        def _(pe):
            def arrived(n):
                pe.wait_ge(loaded[n % SLOTS], 16 * (n // SLOTS + 1))

            def tile(n, t):
                return ring[:, n % SLOTS, t * P:(t + 1) * P]

            def linear(base, outs, chunks, x, out, done, kept=None, banks=8, before_out=0):
                for m in range(outs):
                    if kept is not None and m + before_out >= banks:
                        pe.wait_ge(kept, m + before_out - banks + 1)
                    for k in range(chunks):
                        n, t = base + (m * chunks + k) // TILES, (m * chunks + k) % TILES
                        if t == 0:
                            arrived(n)
                        mm = pe.matmul(out(m), tile(n, t), x(k), start=k == 0, stop=k == chunks - 1)
                        if t == 0:
                            mm.then_inc(slab_begun, 1)
                    mm.then_inc(done, 1)

            def layer_norm(l):
                pe.wait_ge(zsum[l], 8 if l < 3 else 8 * EXPERTS + 1)
                for k in range(KC):
                    mm = pe.matmul(PS[:, 0, 0:T], ones_d[:, :], z[:, k, :], start=k == 0, stop=k == KC - 1)
                mm.then_inc(ln_pe[l], 1)
                pe.wait_ge(ln_act[l], 1)
                for k in range(KC):
                    mm = pe.matmul(PS[:, 1, 0:T], ones_d[:, :], sq[:, k, :], start=k == 0, stop=k == KC - 1)
                mm.then_inc(ln_pe[l], 1)

            pe.wait_ge(s_attn, 64)
            for i in range(3):
                n = min(512, 2 * LINE - 512 * i)
                pe.matmul(PS[0:HEADS, i, 0:n], rbias[0:33, :], onehot[0:33, 512 * i:512 * i + n],
                          start=True, stop=True).then_inc(s_line_ps, 1)
            pe.wait_ge(s_line, 3)
            pe.wait_ge(s_h0, 16)
            linear(SL_QK, 10, KC, lambda k: h[:, k, :], lambda m: PS[:, m % 8, 0:T], qkv_ps, qkv_kept)
            arrived(SL_V)
            pe.wait_ge(s_ones, 1)
            for t in range(3):
                n = min(P, T - P * t)
                pe.wait_ge(qkv_kept, 10 + t - 7)
                for k in range(KC):
                    mm = pe.matmul(PS[0:n, (10 + t) % 8, 0:256], h[:, k, P * t:P * t + n],
                                   ring[:, SL_V % SLOTS, 256 * k:256 * k + 256], start=k == 0, stop=False)
                    if t == 0 and k == 0:
                        mm.then_inc(slab_begun, 1)
                pe.matmul(PS[0:n, (10 + t) % 8, 0:256], ones_row[0:1, 0:n], bv[0:1, :],
                          start=False, stop=True).then_inc(qkv_ps, 1)
            pe.wait_ge(qkv_kept, 13)
            pe.wait_ge(s_const, 96)

            units = [(t, m) for t in range(3) for m in range(8)]

            def scores(u):
                t, m = units[u]
                q0, qn, kn = Q_TILES[t]
                if u >= 2:
                    pe.wait_ge(sc_dve, 4 * (u - 1))
                for p in range(2):
                    o = slice(64 * p, 64 * p + 64)
                    mm = pe.matmul(PS[0:qn, 2 * (u % 2) + p, 0:kn], qk[o, m, q0:q0 + qn],
                                   qk[o, 8 + m // 4, 0:kn], start=True, stop=True)
                mm.then_inc(sc_ps, 1)

            scores(0)
            for u, (t, m) in enumerate(units):
                q0, qn, kn = Q_TILES[t]
                if u + 1 < len(units):
                    scores(u + 1)
                pe.wait_ge(sc_norm, u + 1)
                pe.wait_ge(pT_kept, u) if u else None
                parts = [(i, min(P, kn - P * i)) for i in range(-(-kn // P))]
                for p in range(2):
                    for i, n in parts:
                        mm = pe.transpose(PS[0:n, 4 + p, 96 * i:96 * i + qn], pr[0:qn, u % 2, p, P * i:P * i + n],
                                          eye[0:qn, 0:qn])
                mm.then_inc(pT_ps, 1)
                pe.wait_ge(pT_kept, u + 1)
                if u >= 2:
                    pe.wait_ge(o_kept, u - 1)
                for p in range(2):
                    g = 2 * (m // 4) + p
                    for i, n in parts:
                        mm = pe.matmul(PS[64 * p:64 * p + 64, 6 + u % 2, 0:qn], vn[0:n, i, 64 * g:64 * g + 64],
                                       prT[0:n, u % 2, p, i, 0:qn], start=i == 0, stop=i == len(parts) - 1)
                mm.then_inc(o_ps, 1)
            pe.wait_ge(o_kept, len(units))
            linear(SL_WO, 8, KC, lambda k: oT[:, k, :], lambda m: PS[:, m, 0:T], y_ps[0])
            layer_norm(0)

            pe.wait_ge(ln_act[0], 10)
            for f in range(FT):
                n = SL_GU + f
                if f >= 4:
                    pe.wait_ge(hid_dve, 2 * (f - 3))
                arrived(n)
                for t in range(TILES):
                    mm = pe.matmul(PS[:, 2 * (f % 4) + t // 8, 0:T], tile(n, t), h[:, t % 8, :],
                                   start=t % 8 == 0, stop=t % 8 == 7)
                    if t == 0:
                        mm.then_inc(slab_begun, 1)
                mm.then_inc(gu_ps, 1)
            pe.wait_ge(hid_dve, 2 * FT)
            linear(SL_DN, 8, FT, lambda k: hid[:, k, :], lambda m: PS[:, m, 0:T], y_ps[1])
            layer_norm(1)

            for i in range(3):
                pe.wait_ge(mixed, 8 * (i + 1))
                linear(SL_RKV + 4 * i, 8, KC, lambda k: mix[:, i % 2, k, :], lambda m: PS[:, m, 0:T],
                       rkv_ps, rkv_kept, before_out=8 * i)
            pe.wait_ge(s_lora, 32)
            pe.wait_ge(rkv_kept, 24)
            for i, c0, n, b in ((3, 0, 64, 0), (4, 64, 64, 1), (5, 128, 128, 2), (5, 256, 32, 3)):
                pe.wait_ge(mixed, 8 * (i + 1))
                for k in range(KC):
                    mm = pe.matmul(PS[0:n, b, 0:T], lora1[:, k, c0:c0 + n], mix[:, i % 2, k, :],
                                   start=k == 0, stop=k == KC - 1)
                mm.then_inc(l1_ps, 1)
            pe.wait_ge(l1_kept, 4)
            for i in range(24):
                j, m = i // 8, i % 8
                if i >= 8:
                    pe.wait_ge(l2_kept, i - 7)
                if j < 2:
                    mm = pe.matmul(PS[:, i % 8, 0:T], lora2[0:64, j, m * P:(m + 1) * P], sq[0:64, j, :],
                                   start=True, stop=True)
                else:
                    pe.matmul(PS[:, i % 8, 0:T], lora2[:, 2, m * P:(m + 1) * P], sq[:, 2, :],
                              start=True, stop=False)
                    mm = pe.matmul(PS[:, i % 8, 0:T], lora2[0:32, 3, m * P:(m + 1) * P], sq[0:32, 3, :],
                                   start=False, stop=True)
                mm.then_inc(l2_ps, 1)

            def head_sums(square, x, wait, value, done):
                pe.wait_ge(wait, value)
                for m in range(KC):
                    mm = pe.matmul(PS[:, m, 0:T], square, x(m), start=True, stop=True)
                mm.then_inc(done, 1)

            pe.wait_ge(l2_kept, 24)
            head_sums(same_head[:, :], lambda m: sq[:, m, :], pre_act, 1, pre_pe)
            head_sums(same_head[:, :], lambda m: sq[:, m, :], pre_dve, PRE_BONUS, pre_pe)

            def per_head(out, lhsT, rhs, first=True, last=True):
                for m in range(KC):
                    for p in range(2):
                        o = slice(64 * p, 64 * p + 64)
                        mm = pe.matmul(out[o, m, :], lhsT[o, m, :] if lhsT is not None else masks[o, EYE, :],
                                       rhs[o, m, :] if rhs is not None else masks[o, EYE, :],
                                       start=first, stop=last)
                return mm

            def grouped(out, pairs):
                for m in range(KC):
                    for p in range(2):
                        o = slice(64 * p, 64 * p + 64)
                        for i, (lhsT, rhs) in enumerate(pairs):
                            mm = pe.matmul(out[o, m, :], lhsT[o, m, :], rhs[o, m, :],
                                           start=i == 0, stop=i == len(pairs) - 1)
                return mm

            EYE = MASKS.index("eye64")
            pe.wait_ge(pre_dve, PRE_LAST)
            for c in range(N_CH):
                def dv(n):
                    pe.wait_ge(c_dve, CD * c + n)
                dv(CD_IN)
                for b, (l, r) in enumerate(((bt, at), (at, bt), (kt, at), (bt, rt), (kt, rt))):
                    per_head(bank(b), l, r).then_inc(c_pe, 1)
                for b, x in enumerate((vc, bt, kt)):
                    per_head(bank(5 + b), x, None).then_inc(c_pe, 1)
                for i, b in enumerate(LEVELS):
                    dv(CD_MASKED + 4 * i + 1)
                    per_head(bank(0), otm, tm).then_inc(c_pe, 1)
                    dv(CD_MASKED + 4 * i + 2)
                    per_head(bank(1), ttm, um).then_inc(c_pe, 1)
                    per_head(bank(2), um, ttm).then_inc(c_pe, 1)
                dv(CD_MASKED + 4 * len(LEVELS))
                grouped(bank(3), ((mak, vnat), (at, st))).then_inc(c_pe, 1)
                dv(CD_MASKED + 4 * len(LEVELS) + 1)
                grouped(bank(4), ((ttm, xm),)).then_inc(c_pe, 1)
                dv(CD_MASKED + 4 * len(LEVELS) + 2)
                grouped(bank(5), ((st, rt), (sam, mrb), (vnat, mrk))).then_inc(c_pe, 1)
                grouped(bank(6), ((bnat, sam), (knat, vnat))).then_inc(c_pe, 1)

            head_sums(mean_head[:, :], lambda m: r_[:, m, 0:T], c_dve, CD * N_CH + PRE_ST, gn_pe)
            head_sums(mean_head[:, :], lambda m: sq[:, m, :], gn_act, 1, gn_pe)
            pe.wait_ge(gn_dve, 8)
            linear(SL_O2, 8, KC, lambda k: r_[:, k, 0:T], lambda m: PS[:, m, 0:T], y_ps[2])
            layer_norm(2)

            pe.wait_ge(ln_act[2], 10)
            pe.wait_ge(s_router, 32)
            for t in range(3):
                n = min(P, T - P * t)
                for k in range(KC):
                    mm = pe.matmul(PS[0:n, t, 0:EXPERTS], h[:, k, P * t:P * t + n],
                                   router[:, k, :], start=k == 0, stop=k == KC - 1)
            mm.then_inc(rt_pe, 1)
            pe.wait_ge(rt_dve, RT_GATES)
            for e in range(EXPERTS):
                for t in range(3):
                    n = min(P, T - P * t)
                    mm = pe.matmul(PS[:, e, P * t:P * t + n], gates[0:n, t, e:e + 1].broadcast_to([n, P]),
                                   eye[0:n, 0:n], start=True, stop=True)
            mm.then_inc(rt_pe, 1)
            pe.wait_ge(rt_act, 2)

            with pe.Fori(0, EXPERTS) as e:
                with pe.Fori(0, FTE // SLOTS) as j:
                    for k in range(SLOTS):
                        n = SL_MOE + k
                        if k == 0:
                            pe.wait_ge(zsum[3], 8 * e + 1)
                        pe.wait_ge(hid_dve, HB + 3 * (FTE * e + SLOTS * j + (k - 2)))
                        pe.wait_ge(loaded[n % SLOTS], 16 * (6 * e + j + (n // SLOTS + 1)))
                        for t in range(TILES):
                            mm = pe.matmul(PS[:, 2 * (k % 4) + t // 8, 0:T], tile(n, t), h[:, t % 8, :],
                                           start=t % 8 == 0, stop=t % 8 == 7)
                            if t == 0:
                                mm.then_inc(slab_begun, 1)
                        mm.then_inc(gu_ps, 1)
                with pe.Fori(0, 2) as j:
                    for g in range(4 * FTE):
                        m, k = g // FTE, g % FTE
                        n, t = SL_MOE + FTE + g // TILES, g % TILES
                        if k == 0 and m == 0:
                            pe.wait_ge(hid_dve, HB + 3 * FTE * (e + 1))
                            pe.wait_ge(zsum[3], 8 * e + 4 * j + 1)
                        if t == 0:
                            pe.wait_ge(loaded[n % SLOTS], 16 * (6 * e + j + (n // SLOTS + 1)))
                        mm = pe.matmul(PS[:, m, 0:T], tile(n, t), hid[:, k, :], start=k == 0, stop=k == FTE - 1)
                        if t == 0:
                            mm.then_inc(slab_begun, 1)
                        if k == FTE - 1:
                            mm.then_inc(y_ps[3], 1)
            layer_norm(3)

        @block.scalar
        def _(act):
            def layer_norm(l):
                act.wait_ge(ln_dve[l], 1)
                act.activation(sq[:, :, :], z[:, :, :], ACT.Square).then_inc(ln_act[l], 1)
                act.wait_ge(ln_dve[l], 2)
                act.activation(rstd[:, :], rstd[:, :], ACT.Sqrt).then_inc(ln_act[l], 1)
                for k in range(KC):
                    act.wait_ge(ln_dve[l], 4 + k)
                    act.activation(h[:, k, :], z[:, k, :], ACT.Identity, bias=v_of(f"b{l}", k))\
                       .then_inc(ln_act[l], 1)

            act.wait_ge(s_const, 96)
            for m in range(10):
                act.wait_ge(qkv_ps, m + 1)
                b = v_of("b_q", m) if m < 8 else v_of("b_k", m - 8)
                act.activation(qk[:, m, :], PS[:, m % 8, 0:T], ACT.Identity, bias=b).then_inc(qkv_kept, 1)
            for t in range(3):
                n = min(P, T - P * t)
                act.wait_ge(qkv_ps, 11 + t)
                act.activation(vn[0:n, t, :], PS[0:n, (10 + t) % 8, 0:256], ACT.Copy).then_inc(qkv_kept, 1)

            units = [(t, m) for t in range(3) for m in range(8)]

            def exps(u):
                q0, qn, kn = Q_TILES[units[u][0]]
                act.wait_ge(sc_dve, 4 * (u + 1))
                for p in range(2):
                    a = act.activation(pr[0:qn, u % 2, p, 0:kn + 1], sb_[0:qn, u % 2, p, 0:kn + 1], ACT.Exp,
                                       bias=negm[0:qn, u % 2, p:p + 1], accum_out=den[0:qn, u % 2, p:p + 1])
                a.then_inc(sc_exp, 1)

            def keep_out(u):
                t, m = units[u]
                q0, qn, kn = Q_TILES[t]
                act.wait_ge(o_ps, u + 1)
                act.activation(oT[:, m, q0:q0 + qn], PS[:, 6 + u % 2, 0:qn], ACT.Copy).then_inc(o_kept, 1)

            exps(0)
            for u, (t, m) in enumerate(units):
                q0, qn, kn = Q_TILES[t]
                if u + 1 < len(units):
                    exps(u + 1)
                act.wait_ge(pT_ps, u + 1)
                full, part = kn // P, kn % P
                src = PS[:, 4:6, 0:288].rearrange("p b (i q) -> p b i q", i=3)
                if full:
                    a = act.activation(prT[:, u % 2, :, 0:full, 0:qn], src[:, :, 0:full, 0:qn], ACT.Copy)
                if part:
                    a = act.activation(prT[0:part, u % 2, :, full, 0:qn], src[0:part, :, full, 0:qn], ACT.Copy)
                a.then_inc(pT_kept, 1)
                if u >= 1:
                    keep_out(u - 1)
            keep_out(len(units) - 1)
            layer_norm(0)

            for f in range(FT):
                act.wait_ge(gu_ps, f + 1)
                if f:
                    act.wait_ge(hid_dve, 2 * f)
                act.activation(sg[:, :], PS[:, 2 * (f % 4), 0:T], ACT.Sigmoid).then_inc(gu_sig, 1)
            layer_norm(1)

            for i in range(24):
                act.wait_ge(rkv_ps, i + 1)
                dst = (r_, k_, v_)[i // 8]
                act.activation(dst[:, i % 8, 0:T], PS[:, i % 8, 0:T], ACT.Copy).then_inc(rkv_kept, 1)
            for i, (n, f) in enumerate(((64, ACT.Tanh), (64, ACT.Copy), (128, ACT.Sigmoid), (32, ACT.Sigmoid))):
                act.wait_ge(l1_ps, i + 1)
                act.activation(sq[0:n, i, :], PS[0:n, i, 0:T], f).then_inc(l1_kept, 1)
            for i in range(24):
                j, m = i // 8, i % 8
                act.wait_ge(l2_ps, i + 1)
                if j < 2:
                    a = act.activation((cum, a_)[j][:, m, 0:T], PS[:, m, 0:T], ACT.Sigmoid,
                                       bias=v_of(("w0", "a0")[j], m))
                else:
                    a = act.activation(g_[:, m, :], PS[:, m, 0:T], ACT.Copy)
                a.then_inc(l2_kept, 1)
            act.wait_ge(pre_dve, 1)
            act.activation(sq[:, :, :], kk[:, :, 0:T], ACT.Square).then_inc(pre_act, 1)
            act.wait_ge(pre_dve, 2)
            act.activation(sq[:, :, :], sq[:, :, :], ACT.Sqrt).then_inc(pre_act, 1)

            act.wait_ge(pre_dve, PRE_LAST)
            for c in range(N_CH):
                act.wait_ge(c_pe, CP * c + 0)
                act.wait_ge(c_dve, CD * c + PRE_ST)
                cc = cum[:, :, slice(CH * c, CH * c + CH)]
                act.activation(e1[:, :, :], cc, ACT.Exp, scale=-DECAY).then_inc(c_act, 1)
                act.activation(em[:, :, :], cc, ACT.Exp, scale=DECAY).then_inc(c_act, 1)

            act.wait_ge(gn_dve, 1)
            act.activation(sq[:, :, :], r_[:, :, 0:T], ACT.Square).then_inc(gn_act, 1)
            act.wait_ge(gn_dve, 2)
            act.activation(sq[:, :, :], sq[:, :, :], ACT.Sqrt).then_inc(gn_act, 1)
            layer_norm(2)
            act.wait_ge(rt_dve, RT_EXP)
            act.activation(ex[:, :, :], ex[:, :, :], ACT.Exp).then_inc(rt_act, 1)
            act.wait_ge(rt_pe, 2)
            act.activation(gate_b[:, :, :], PS[:, :, 0:T], ACT.Copy).then_inc(rt_act, 1)
            with act.Fori(0, EXPERTS) as e:
                with act.Fori(0, FTE // SLOTS) as j:
                    for k in range(SLOTS):
                        act.wait_ge(gu_ps, FT + FTE * e + SLOTS * j + (k + 1))
                        act.wait_ge(hid_dve, HB + 3 * (FTE * e + SLOTS * j + k))
                        act.activation(sg[:, :], PS[:, 2 * (k % 4), 0:T], ACT.Sigmoid).then_inc(gu_sig, 1)
            layer_norm(3)

        @block.vector
        def _(dve):
            class Steps:
                def __init__(self, s, n=0):
                    self.s, self.n = s, n

                def step(self, ins):
                    self.n = self.n + 1
                    ins.then_inc(self.s, 1)
                    dve.wait_ge(self.s, self.n)

                def mark(self, ins):
                    self.n = self.n + 1
                    ins.then_inc(self.s, 1)

            def residual(l):
                for m in range(KC):
                    dve.wait_ge(y_ps[l], m + 1)
                    dve.scalar_tensor_tensor(out=z[:, m, :], in0=h[:, m, :], scalar=ALPHA, in1=PS[:, m, 0:T],
                                             op0=ALU.mult, op1=ALU.add).then_inc(zsum[l], 1)

            def layer_norm(l):
                s = Steps(ln_dve[l])
                dve.wait_ge(ln_pe[l], 1)
                dve.wait_ge(zsum[l], 8 if l < 3 else 8 * EXPERTS + 1)
                s.step(dve.tensor_tensor(out=z[:, :, :], in0=z[:, :, :],
                                         in1=PS[:, 0:1, 0:T].broadcast_to([P, KC, T]), op=ALU.subtract))
                dve.wait_ge(ln_pe[l], 2)
                s.mark(dve.tensor_scalar(rstd[:, :], PS[:, 1, 0:T], LN_EPS, None, ALU.add))
                dve.wait_ge(ln_act[l], 2)
                s.step(dve.reciprocal(rstd[:, :], rstd[:, :]))
                for k in range(KC):
                    s.mark(dve.scalar_tensor_tensor(out=z[:, k, :], in0=z[:, k, :], scalar=v_of(f"g{l}", k),
                                                    in1=rstd[:, :], op0=ALU.mult, op1=ALU.mult))

            for i in range(3):
                n = min(512, 2 * LINE - 512 * i)
                dve.wait_ge(s_line_ps, i + 1)
                dve.tensor_copy(line[0:HEADS, 512 * i:512 * i + n], PS[0:HEADS, i, 0:n]).then_inc(s_line, 1)

            units = [(t, m) for t in range(3) for m in range(8)]
            sc, nr = Steps(sc_dve), Steps(nrm)

            def biased(u):
                t, m = units[u]
                q0, qn, kn = Q_TILES[t]
                dve.wait_ge(sc_ps, u + 1)
                if u >= 2:
                    dve.wait_ge(sc_exp, u - 1)
                sc.mark(dve.scalar_tensor_tensor(
                    out=sb_[0:qn, u % 2, :, 0:kn], in0=PS[0:qn, 2 * (u % 2):2 * (u % 2) + 2, 0:kn],
                    scalar=HD ** -0.5, in1=bias_of(t)[0:qn, 2 * m:2 * m + 2, :], op0=ALU.mult, op1=ALU.add))
                sc.step(dve.tensor_copy(sb_[0:qn, u % 2, :, kn:kn + 1],
                                        sinks[0:qn, 2 * m:2 * m + 2].unsqueeze(2)))
                sc.step(dve.tensor_reduce(out=mx[0:qn, :], in_=sb_[0:qn, u % 2, :, 0:kn + 1], axis=AX.X, op=ALU.max))
                sc.mark(dve.tensor_scalar(negm[0:qn, u % 2, :], mx[0:qn, :], -1.0, None, ALU.mult))

            dve.wait_ge(s_attn, 64)
            dve.wait_ge(s_bias, 96)
            biased(0)
            for u, (t, m) in enumerate(units):
                q0, qn, kn = Q_TILES[t]
                if u + 1 < len(units):
                    biased(u + 1)
                dve.wait_ge(sc_exp, u + 1)
                if u:
                    dve.wait_ge(sc_norm, u)
                nr.step(dve.reciprocal(rden[0:qn, :], den[0:qn, u % 2, :]))
                for p in range(2):
                    i = dve.tensor_scalar(pr[0:qn, u % 2, p, 0:kn], pr[0:qn, u % 2, p, 0:kn],
                                          rden[0:qn, p:p + 1], None, ALU.mult)
                i.then_inc(sc_norm, 1)
            residual(0)
            layer_norm(0)

            s = Steps(hid_dve)
            for f in range(FT):
                dve.wait_ge(gu_sig, f + 1)
                s.step(dve.tensor_tensor(out=gu[:, :], in0=sg[:, :], in1=PS[:, 2 * (f % 4), 0:T], op=ALU.mult))
                s.step(dve.tensor_tensor(out=hid[:, f, :], in0=gu[:, :], in1=PS[:, 2 * (f % 4) + 1, 0:T],
                                         op=ALU.mult))
            residual(1)
            layer_norm(1)

            dve.wait_ge(ln_act[1], 10)
            s = Steps(xx_steps)
            s.mark(dve.tensor_tensor(out=z[:, :, 1:T], in0=h[:, :, 0:T - 1], in1=h[:, :, 1:T], op=ALU.subtract))
            s.step(dve.tensor_scalar(z[:, :, 0:1], h[:, :, 0:1], -1.0, None, ALU.mult))
            for x in (r_, k_, kk, a_, v_, cum):
                i = dve.memset(x[:, :, T:TP], 0.0)
            i.then_inc(pads, 1)
            for i, name in enumerate(("mu_r", "mu_k", "mu_v", "mu_w", "mu_a", "mu_g")):
                if 2 <= i < 5:
                    dve.wait_ge(rkv_ps, 8 * (i - 1))
                if i == 5:
                    dve.wait_ge(l1_ps, 1)
                for k in range(KC):
                    dve.scalar_tensor_tensor(out=mix[:, i % 2, k, :], in0=z[:, k, :], scalar=v_of(name, k),
                                             in1=h[:, k, :], op0=ALU.mult, op1=ALU.add).then_inc(mixed, 1)
            s = Steps(pre_dve)
            dve.wait_ge(pads, 1)
            dve.wait_ge(l2_kept, 24)
            s.step(dve.tensor_tensor(out=kk[:, :, 0:T], in0=k_[:, :, 0:T], in1=v_all("k_k"), op=ALU.mult))
            dve.wait_ge(pre_pe, 1)
            s.mark(dve.tensor_scalar(sq[:, :, :], PS[:, :, 0:T], 1e-24, None, ALU.max))
            dve.wait_ge(pre_act, 2)
            s.step(dve.reciprocal(sq[:, :, :], sq[:, :, :]))
            s.step(dve.tensor_tensor(out=kk[:, :, 0:T], in0=kk[:, :, 0:T], in1=sq[:, :, :], op=ALU.mult))
            s.step(dve.scalar_tensor_tensor(out=sq[:, :, :], in0=a_[:, :, 0:T], scalar=-1.0, in1=v_all("k_a"),
                                            op0=ALU.add, op1=ALU.mult))
            s.step(dve.scalar_tensor_tensor(out=k_[:, :, 0:T], in0=sq[:, :, :], scalar=1.0, in1=k_[:, :, 0:T],
                                            op0=ALU.add, op1=ALU.mult))
            s.step(dve.tensor_tensor(out=a_[:, :, 0:T], in0=a_[:, :, 0:T], in1=kk[:, :, 0:T], op=ALU.mult))
            s.step(dve.tensor_tensor(out=sq[:, :, :], in0=r_[:, :, 0:T], in1=k_[:, :, 0:T], op=ALU.mult))
            s.step(dve.tensor_tensor(out=sq[:, :, :], in0=sq[:, :, :], in1=v_all("r_k"), op=ALU.mult))
            assert s.n == PRE_BONUS
            flat = lambda x: x.rearrange("p a b -> p (a b)")
            restart = arena[:, OV:OV + KC * TP]
            s.step(dve.memset(restart, 1.0))
            s.step(dve.memset(restart.rearrange("p (c t) -> p c t", t=CH)[:, :, 0:1], 0.0))
            s.step(dve.tensor_tensor_scan(flat(cum), restart, flat(cum), 0.0, ALU.mult, ALU.add))
            dve.wait_ge(pre_pe, 2)
            s.step(dve.tensor_tensor(out=z[:, :, :], in0=PS[:, :, 0:T], in1=v_[:, :, 0:T], op=ALU.mult))
            s.step(dve.memset(st[:, :, :], 0.0))
            assert s.n == PRE_LAST

            for c in range(N_CH):
                s = Steps(c_dve, CD * c)
                cs = slice(CH * c, CH * c + CH)

                def pw(n):
                    dve.wait_ge(c_pe, CP * c + n)
                tt = lambda o, a, b, op=ALU.mult: dve.tensor_tensor(out=o, in0=a, in1=b, op=op)
                dve.wait_ge(c_act, 2 * c + 2)
                s.step(tt(rt[:, :, :], r_[:, :, cs], e1[:, :, :]))
                s.step(dve.tensor_scalar(at[:, :, 0:1], kk[:, :, slice(CH * c, CH * c + 1)], -1.0, None, ALU.mult))
                s.step(dve.scalar_tensor_tensor(out=at[:, :, 1:CH], in0=kk[:, :, slice(CH * c + 1, CH * c + CH)],
                                                scalar=-1.0, in1=e1[:, :, 0:CH - 1], op0=ALU.mult, op1=ALU.mult))
                s.step(tt(bt[:, :, :], a_[:, :, cs], em[:, :, :]))
                s.step(tt(kt[:, :, :], k_[:, :, cs], em[:, :, :]))
                s.step(dve.tensor_copy(vc[:, :, :], v_[:, :, cs]))
                pw(1)
                s.step(tt(ltm[:, :, :], bank(0), mask("upper")))
                s.step(tt(ttm[:, :, :], ltm[:, :, :], mask("low2T")))
                s.step(tt(ttm[:, :, :], ttm[:, :, :], mask("eye64"), ALU.add))
                pw(2)
                s.step(tt(tm[:, :, :], bank(1), mask("low2")))
                s.step(tt(tm[:, :, :], tm[:, :, :], mask("eye64"), ALU.add))
                pw(3)
                s.step(tt(mak[:, :, :], bank(2), mask("upper")))
                pw(4)
                s.step(tt(mrb[:, :, :], bank(3), mask("upper_eq")))
                pw(5)
                s.step(tt(mrk[:, :, :], bank(4), mask("upper_eq")))
                for i, x in enumerate((vnat, bnat, knat)):
                    pw(6 + i)
                    s.step(dve.tensor_copy(x[:, :, :], bank(5 + i)))
                for i, b in enumerate(LEVELS):
                    s.step(tt(otm[:, :, :], ltm[:, :, :], mask(f"off{b}")))
                    pw(8 + 3 * i + 1)
                    s.step(dve.tensor_copy(um[:, :, :], bank(0)))
                    pw(8 + 3 * i + 3)
                    s.step(tt(tm[:, :, :], tm[:, :, :], bank(1), ALU.add))
                    s.step(tt(ttm[:, :, :], ttm[:, :, :], bank(2), ALU.add))
                n = 8 + 3 * len(LEVELS)
                pw(n + 1)
                s.step(dve.tensor_copy(xm[:, :, :], bank(3)))
                pw(n + 2)
                s.step(dve.tensor_copy(sam[:, :, :], bank(4)))
                pw(n + 4)
                s.step(dve.tensor_copy(r_[:, :, cs], bank(5)))
                s.step(tt(st[:, :, :], st[:, :, :], bank(6), ALU.add))
                s.step(tt(st[:, :, :], st[:, :, :], e1[:, :, CH - 1:CH].broadcast_to([P, KC, CH])))

            s = Steps(gn_dve)
            y = r_[:, :, 0:T]
            dve.wait_ge(gn_pe, 1)
            s.step(tt(y, y, PS[:, :, 0:T], ALU.subtract))
            dve.wait_ge(gn_pe, 2)
            s.mark(dve.tensor_scalar(sq[:, :, :], PS[:, :, 0:T], GN_EPS, None, ALU.add))
            dve.wait_ge(gn_act, 2)
            s.step(dve.reciprocal(sq[:, :, :], sq[:, :, :]))
            s.step(tt(y, y, sq[:, :, :]))
            s.step(tt(y, y, v_all("lnx_g")))
            s.step(tt(y, y, v_all("lnx_b"), ALU.add))
            s.step(tt(y, y, z[:, :, :], ALU.add))
            s.step(tt(y, y, g_[:, :, :]))
            residual(2)
            layer_norm(2)

            dve.wait_ge(ln_act[2], 10)
            dve.wait_ge(s_router, 32)
            dve.wait_ge(rt_pe, 1)
            s = Steps(rt_dve)
            s.step(dve.memset(lg[:, :, :], 0.0))
            for t in range(3):
                n = min(P, T - P * t)
                s.step(dve.tensor_copy(lg[0:n, t, :], PS[0:n, t, 0:EXPERTS]))
            four = [P, 3, EXPERTS, EXPERTS]
            other, own = lg[:, :, :].unsqueeze(2).broadcast_to(four), lg[:, :, :].unsqueeze(3).broadcast_to(four)
            s.step(tt(cmp_a[:, :, :, :], other, own, ALU.is_gt))
            s.step(tt(cmp_b[:, :, :, :], other, own, ALU.is_equal))
            s.step(tt(cmp_b[:, :, :, :], cmp_b[:, :, :, :], before[:, :, :].unsqueeze(1).broadcast_to(four)))
            s.step(tt(cmp_a[:, :, :, :], cmp_a[:, :, :, :], cmp_b[:, :, :, :], ALU.add))
            s.step(dve.tensor_reduce(out=sel[:, :, :], in_=cmp_a[:, :, :, :], axis=AX.X, op=ALU.add))
            s.step(dve.tensor_scalar(sel[:, :, :], sel[:, :, :], 2.0, None, ALU.is_lt))
            s.step(dve.tensor_reduce(out=top[:, :], in_=lg[:, :, :], axis=AX.X, op=ALU.max))
            s.step(tt(ex[:, :, :], lg[:, :, :], top[:, :].unsqueeze(2).broadcast_to([P, 3, EXPERTS]), ALU.subtract))
            assert s.n == RT_EXP
            dve.wait_ge(rt_act, 1)
            s.step(tt(gates[:, :, :], ex[:, :, :], sel[:, :, :]))
            s.step(dve.tensor_reduce(out=top[:, :], in_=gates[:, :, :], axis=AX.X, op=ALU.add))
            s.step(dve.reciprocal(top[:, :], top[:, :]))
            s.step(tt(gates[:, :, :], gates[:, :, :], top[:, :].unsqueeze(2).broadcast_to([P, 3, EXPERTS])))
            assert s.n == RT_GATES
            dve.tensor_scalar(z[:, :, :], h[:, :, :], ALPHA, None, ALU.mult).then_inc(zsum[3], 1)
            dve.wait_ge(rt_act, 2)
            dve.wait_ge(zsum[3], 1)
            with dve.Fori(0, EXPERTS) as e:
                with dve.Fori(0, FTE // SLOTS) as j:
                    s = Steps(hid_dve, HB + 3 * FTE * e + 3 * SLOTS * j)
                    for k in range(SLOTS):
                        dve.wait_ge(gu_sig, FT + FTE * e + SLOTS * j + (k + 1))
                        b = 2 * (k % 4)
                        s.step(tt(gu[:, :], sg[:, :], PS[:, b, 0:T]))
                        s.step(tt(gu[:, :], gu[:, :], PS[:, b + 1, 0:T]))
                        s.step(tt(hid[:, bass.ds(SLOTS * j + k, 1), :], gu[:, :].unsqueeze(1),
                                  gate_b[:, bass.ds(e, 1), :]))
                with dve.Fori(0, 2) as j:
                    for m in range(4):
                        dve.wait_ge(y_ps[3], 8 * e + 4 * j + (m + 1))
                        zm = z[:, bass.ds(4 * j + m, 1), :]
                        tt(zm, zm, PS[:, m:m + 1, 0:T], ALU.add).then_inc(zsum[3], 1)
            layer_norm(3)


def slabs_of(tiles):
    n = tiles.shape[0] // TILES
    return tiles.reshape(n, TILES, P, P).transpose(0, 2, 1, 3).reshape(n, P, TILES * P)


def tiles_of(w):
    k, m = w.shape
    return w.reshape(k // P, P, m // P, P).transpose(2, 0, 1, 3).reshape(-1, P, P)


def gate_up_tiles(w):
    k, f = w.shape
    t = w.reshape(k // P, P, 2, f // 2 // P, P).transpose(3, 2, 0, 1, 4)
    return t.reshape(-1, P, P)


def chunked(v):
    return v.reshape(-1, P).T


def t5_buckets():
    n = np.arange(T)
    f = np.maximum(n, 1).astype(np.float32)
    large = 16 + (np.log(f / np.float32(16)) / np.float32(np.log(8.0)) * np.float32(16)).astype(np.int32)
    return np.where(n < 16, n, np.minimum(large, 31))


def constants():
    onehot = np.zeros((33, 2, LINE), np.float32)
    buckets = t5_buckets()
    for x in range(LINE):
        d = T - 1 - x
        for s in range(2):
            ok = d >= 0 and (s == 0 or d < WINDOW)
            onehot[buckets[d] if ok else 32, s, x] = 1.0
    i = np.arange(P)
    eye = np.eye(P, dtype=np.float32)
    same = (i[:, None] // 64 == i[None, :] // 64).astype(np.float32)
    squares = np.concatenate([eye, np.full((P, P), 1.0 / D, np.float32), same, same / 64], 1).astype(np.float32)
    r, c = np.arange(CH)[:, None], np.arange(CH)[None, :]
    m = {"low2": (c < r) & (c // 2 == r // 2), "low2T": (r < c) & (c // 2 == r // 2),
         "upper": r < c, "upper_eq": r <= c, "eye64": r == c}
    for b in LEVELS:
        m[f"off{b}"] = (r // b != c // b) & (r // (2 * b) == c // (2 * b)) & (r < c)
    masks = np.stack([np.concatenate([m[n], m[n]], 0) for n in MASKS], 1).astype(np.float32)
    before = np.broadcast_to((np.arange(8)[None, :] < np.arange(8)[:, None]).astype(np.float32), (P, 8, 8))
    return {"onehot": onehot.reshape(33, 2 * LINE), "squares": squares, "masks": masks,
            "before": np.ascontiguousarray(before)}


def head_order():
    return [4 * (2 * (m // 4) + p) + m % 4 for m in range(8) for p in range(2)]


def layout(x, meta_tokens, rel_bias, ln_mix_g, ln_mix_b, ln_ffn_g, ln_ffn_b, attn_w_qkv, attn_b_qkv, attn_sinks,
           attn_w_o, rwkv_mu, rwkv_w0, rwkv_w1, rwkv_w2, rwkv_a0, rwkv_a1, rwkv_a2, rwkv_g1, rwkv_g2, rwkv_k_k,
           rwkv_k_a, rwkv_r_k, rwkv_w_rkv, rwkv_lnx_g, rwkv_lnx_b, rwkv_w_o, ffn_w_gu, ffn_w_down, moe_router,
           moe_w_gu, moe_w_down):
    order = head_order()
    feats = np.concatenate([np.arange(64 * q, 64 * q + 64) for q in order])
    wqkv, bqkv = attn_w_qkv[0], attn_b_qkv[0]
    wq, wk, wv = wqkv[:, :D][:, feats], wqkv[:, D:D + 256], wqkv[:, D + 256:]
    v_slab = wv.reshape(KC, P, 256).transpose(1, 0, 2).reshape(1, P, KC * 256)
    parts = [slabs_of(tiles_of(np.concatenate([wq, wk], 1))), v_slab, slabs_of(tiles_of(attn_w_o[0][feats])),
             slabs_of(gate_up_tiles(ffn_w_gu[0])), slabs_of(tiles_of(ffn_w_down[0]))]
    parts += [slabs_of(tiles_of(rwkv_w_rkv[0, i])) for i in range(3)] + [slabs_of(tiles_of(rwkv_w_o[0]))]
    for e in range(EXPERTS):
        parts += [slabs_of(gate_up_tiles(moe_w_gu[0, e])), slabs_of(tiles_of(moe_w_down[0, e]))]
    vecs = [ln_mix_g[0], ln_mix_b[0], ln_ffn_g[0], ln_ffn_b[0], ln_mix_g[1], ln_mix_b[1], ln_ffn_g[1], ln_ffn_b[1],
            *rwkv_mu[0][[0, 2, 3, 1, 4, 5]], rwkv_w0[0], rwkv_a0[0], rwkv_k_k[0], rwkv_k_a[0],
            rwkv_r_k[0].reshape(-1), rwkv_lnx_g[0], rwkv_lnx_b[0], bqkv[:D][feats], bqkv[D:D + 256]]
    lora1 = np.concatenate([rwkv_w1[0], rwkv_a1[0], rwkv_g1[0]], 1).reshape(KC, P, 288).transpose(1, 0, 2)
    lora2 = np.zeros((P, 4, D), np.float32)
    lora2[0:64, 0], lora2[0:64, 1] = rwkv_w2[0], rwkv_a2[0]
    lora2[:, 2], lora2[0:32, 3] = rwkv_g2[0][0:P], rwkv_g2[0][P:]
    h0 = np.concatenate([meta_tokens, x[0]], 0)
    return {
        "h0": h0.T.reshape(KC, P, T).transpose(1, 0, 2),
        "slabs": np.concatenate(parts, 0),
        "vecs": np.concatenate([chunked(v) for v in vecs], 1),
        "rel_bias": np.concatenate([rel_bias[:, order], np.full((1, HEADS), NEG, np.float32)], 0),
        "b_v": bqkv[None, D + 256:],
        "sinks": attn_sinks[:, order],
        "lora1": lora1, "lora2": lora2,
        "router": moe_router[0].reshape(KC, P, EXPERTS).transpose(1, 0, 2),
        **constants(),
    }


def kernel(**inputs):
    import concourse.bacc as bacc
    from concourse.bass_utils import run_bass_kernel_spmd

    nc = bacc.Bacc("TRN2", target_bir_lowering=False, num_devices=1)
    arrays = {f"in_{n}": np.ascontiguousarray(a) for n, a in
              layout(**{n: np.asarray(a) for n, a in inputs.items()}).items()}
    A = {n[3:]: nc.dram_tensor(n, a.shape, F32, kind="ExternalInput").ap() for n, a in arrays.items()}
    out = nc.dram_tensor("out", (P, KC, SEQ), F32, kind="ExternalOutput").ap()
    build(nc, A, out)
    got = run_bass_kernel_spmd(nc, [arrays], core_ids=[0]).results[0]["out"]
    return np.ascontiguousarray(got.transpose(2, 1, 0).reshape(1, SEQ, D))
```

```python
from contextlib import ExitStack

import numpy as np

import concourse.bass as bass
from concourse import mybir
from concourse.alu_op_type import AluOpType as ALU

F32, I32 = mybir.dt.float32, mybir.dt.int32
ACT = mybir.ActivationFunctionType
AX = mybir.AxisListType

P = 128
D = 1024
KC = D // P
N_META, SEQ = 16, 256
T = N_META + SEQ
HEADS, KV_HEADS, HD = 16, 4, 64
WINDOW = 128
D_FF, D_FFE, EXPERTS = 2816, 3584, 8
FT, FTE = D_FF // P, D_FFE // P
ALPHA = 4 ** 0.25
LN_EPS, GN_EPS = 1e-5, 64e-5
DECAY = float(np.exp(-0.5))
NEG = -1e30

TILES = 16
SLOTS = 7
SL_QK, SL_V, SL_WO = 0, 5, 6
SL_GU = SL_WO + 4
SL_DN = SL_GU + FT
SL_RKV = SL_DN + FT * KC // TILES
SL_O2 = SL_RKV + 12
SL_MOE = SL_O2 + 4
SL_EXPERT = FTE + FTE * KC // TILES
N_SLABS = SL_MOE + EXPERTS * SL_EXPERT

Q_TILES = [(0, 96, 96), (96, 96, 192), (192, 80, 272)]
KN_AT = [0, 96, 288]
KN_ALL = 560
Q_MAX = 96
LINE = 2 * T - 1

CH = 64
N_CH = -(-T // CH)
TP = N_CH * CH
LEVELS = [2, 4, 8, 16, 32]

VECS = ["g0", "b0", "g1", "b1", "g2", "b2", "g3", "b3", "mu_r", "mu_k", "mu_v", "mu_w", "mu_a", "mu_g",
        "w0", "a0", "k_k", "k_a", "r_k", "lnx_g", "lnx_b", "b_q"]
VCOL = {n: KC * i for i, n in enumerate(VECS)}
VCOL["b_k"] = KC * len(VECS)
N_VEC = KC * len(VECS) + 2
PRE_BONUS, PRE_LAST = 9, 14
CD_IN = 6
CD_MASKED = CD_IN + 11
CD = CD_MASKED + 4 * len(LEVELS) + 5
CP = 8 + 3 * len(LEVELS) + 4
PRE_ST = 0
CAP = 96
PASSES = -(-T // CAP)
RT_SEL, RT_EXP, RT_POS, RT_FLAG = 10, 12, 21, 23
MASKS = ["low2", "low2T", "upper", "upper_eq"] + [f"off{b}" for b in LEVELS] + ["eye64"]


def build(nc, A, OUT):
    ctx = ExitStack()
    with ctx:
        def sb(name, shape):
            return ctx.enter_context(nc.sbuf_tensor(name, shape, F32))

        def sem(name):
            return ctx.enter_context(nc.semaphore(name))

        ring = sb("ring", [P, SLOTS, TILES * P])
        h = sb("h", [P, KC, T])
        z = sb("z", [P, KC, T])
        sq = sb("sq", [P, KC, T])
        rstd = sb("rstd", [P, T])
        eye = sb("eye", [P, P])
        ones_d = sb("ones_d", [P, P])
        same_head = sb("same_head", [P, P])
        mean_head = sb("mean_head", [P, P])
        masks = sb("masks", [P, len(MASKS), CH])
        vec = sb("vec", [P, N_VEC])
        arena = sb("arena", [P, 28800])
        PS = ctx.enter_context(nc.psum_tensor("PS", [P, 8, 512], F32))
        scratch = nc.dram_tensor("bias_lines", (HEADS, Q_MAX, 2 * LINE), F32, kind="Internal").ap()

        def carve(start, *shape):
            n = int(np.prod(shape))
            assert start + n <= 28800, (start, shape)
            v = arena[:, start:start + n]
            if len(shape) == 1:
                return v
            names = "abcd"[:len(shape)]
            return v.rearrange(f"p ({' '.join(names)}) -> p {' '.join(names)}", **dict(zip(names, shape)))

        def v_of(name, m):
            return vec[:, VCOL[name] + m:VCOL[name] + m + 1]

        def v_all(name, n=T):
            return vec[:, VCOL[name]:VCOL[name] + KC].unsqueeze(2).broadcast_to([P, KC, n])

        qk = carve(0, 10, T)
        vn = carve(2720, 3, 256)
        bias = carve(3488, HEADS * KN_ALL)
        sb_ = carve(12448, 2, 2, T + 1)
        pr = carve(13540, 2, 2, T + 1)
        prT = carve(14632, 2, 2, 3, 96)
        oT = carve(15784, KC, T)
        line = carve(17960, 2 * LINE)
        onehot = carve(19046, 2 * LINE)
        rbias = carve(20132, HEADS)
        bv = carve(20148, 256)
        sinks = carve(20404, HEADS)
        mx = carve(20420, 2)
        negm = carve(20422, 2, 2)
        den = carve(20426, 2, 2)
        rden = carve(20430, 2)
        ones_row = carve(20432, P)

        def bias_of(t):
            qn, kn = Q_TILES[t][1:]
            s = HEADS * KN_AT[t]
            return bias[:, s:s + HEADS * kn].rearrange("p (h k) -> p h k", h=HEADS)

        hid = carve(0, FTE, T)
        sg = carve(7616, T)
        gu = carve(7888, T)
        gate_b = carve(8160, EXPERTS, T)
        router = carve(10336, KC, EXPERTS)
        lg = carve(10400, 3, EXPERTS)
        cmp_a = carve(10424, 3, EXPERTS, EXPERTS)
        cmp_b = carve(10616, 3, EXPERTS, EXPERTS)
        before = carve(10808, EXPERTS, EXPERTS)
        sel = carve(10872, 3, EXPERTS)
        ex = carve(10896, 3, EXPERTS)
        top = carve(10920, 3)
        gates = carve(10923, 3, EXPERTS)
        place = carve(22271, 3, EXPERTS + 1)
        most = carve(10971, 1)
        place_b = carve(10972, EXPERTS, T)
        hn = carve(13420, 3, D)
        hid_e = carve(16492, FTE, CAP)
        xe = carve(19180, KC, CAP)
        yn = carve(19948, D)
        pick = carve(20972, 3, CAP)
        put = carve(21260, T)
        sge = carve(21532, CAP)
        gue = carve(21628, CAP)
        numbers = carve(21724, PASSES * CAP)
        number_p = carve(21724 + PASSES * CAP, PASSES)
        tri = carve(21724 + PASSES * (CAP + 1), P)
        ones = carve(21724 + PASSES * (CAP + 1) + P, P)
        places = carve(21724, PASSES * (CAP + 1) + 2 * P)
        flag = ctx.enter_context(nc.sbuf_tensor("flag", [P, 1], I32))

        r_ = carve(0, KC, TP)
        k_ = carve(2560, KC, TP)
        kk = carve(5120, KC, TP)
        a_ = carve(7680, KC, TP)
        v_ = carve(10240, KC, TP)
        cum = carve(12800, KC, TP)
        g_ = carve(15360, KC, T)
        OV = 17536
        mix = carve(OV, 2, KC, T)
        lora1 = carve(OV + 4352, KC, 288)
        lora2 = carve(OV + 6656, 4, D)
        (e1, em, rt, at, bt, kt, vc, ltm, tm, ttm, um, otm, mak, mrb, mrk, vnat, bnat, knat, xm, sam, st) = [
            carve(OV + 512 * i, KC, CH) for i in range(21)]
        low, lowT = vc, ltm

        def bank(b):
            return PS[:, b, :].rearrange("p (m t) -> p m t", m=KC)

        def mask(name):
            i = MASKS.index(name)
            return masks[:, i:i + 1, :].broadcast_to([P, KC, CH])

        loaded = [sem(f"slab_loaded{j}") for j in range(SLOTS)]
        slab_begun = sem("slab_begun")
        s_const = sem("consts_loaded")
        s_attn = sem("attn_consts_loaded")
        s_h0 = sem("h0_loaded")
        s_lora = sem("lora_loaded")
        s_router = sem("router_loaded")
        s_line_ps = sem("bias_line_in_psum")
        s_line = sem("bias_line_kept")
        s_line_out = sem("bias_line_stored")
        s_bias = sem("bias_loaded")
        s_ones = sem("ones_row_set")
        qkv_ps, qkv_kept = sem("qkv_in_psum"), sem("qkv_kept")
        sc_ps, sc_dve = sem("scores_in_psum"), sem("scores_dve_steps")
        sc_exp, sc_norm = sem("probs_exponentiated"), sem("probs_normalised")
        nrm = sem("norm_steps")
        pT_ps, pT_kept = sem("probs_T_in_psum"), sem("probs_T_kept")
        o_ps, o_kept = sem("attn_out_in_psum"), sem("attn_out_kept")
        y_ps = [sem(f"sublayer{i}_out_in_psum") for i in range(4)]
        zsum = [sem(f"residual{i}_added") for i in range(4)]
        ln_pe = [sem(f"ln{i}_sums") for i in range(4)]
        ln_dve = [sem(f"ln{i}_vector_steps") for i in range(4)]
        ln_act = [sem(f"ln{i}_scalar_steps") for i in range(4)]
        gu_ps, gu_sig, hid_dve = sem("gate_up_in_psum"), sem("gate_sigmoid"), sem("hidden_steps")
        mixed, xx_steps = sem("mixed"), sem("shift_steps")
        rkv_ps, rkv_kept = sem("rkv_in_psum"), sem("rkv_kept")
        l1_ps, l1_kept = sem("lora_in_psum"), sem("lora_kept")
        l2_ps, l2_kept = sem("lora_out_in_psum"), sem("lora_out_kept")
        pads = sem("pads_cleared")
        pre_dve, pre_act, pre_pe = sem("prep_vector_steps"), sem("prep_scalar_steps"), sem("prep_sums")
        c_dve, c_act, c_pe = sem("chunk_vector_steps"), sem("chunk_scalar_steps"), sem("chunk_products")
        gn_dve, gn_act, gn_pe = sem("gn_vector_steps"), sem("gn_scalar_steps"), sem("gn_sums")
        rt_pe, rt_dve, rt_act = sem("router_products"), sem("router_vector_steps"), sem("router_scalar_steps")
        picked, gathered, xe_kept = sem("picks_built"), sem("gathered_in_psum"), sem("tokens_kept")
        put_dve, dn_ps, yn_kept = sem("puts_built"), sem("expert_out_in_psum"), sem("expert_out_kept")
        z_whole = sem("all_experts_added")
        s_out = sem("out_stored")

        block = ctx.enter_context(nc.Block())

        @block.sync
        def _(sp):
            sp.dma_start(h[:, :, :], A["h0"]).then_inc(s_h0, 16)
            for j in range(SLOTS):
                sp.dma_start(ring[:, j, :], A["slabs"][j, :, :]).then_inc(loaded[j], 16)
            with sp.Fori(1, N_SLABS // SLOTS) as i:
                for j in range(SLOTS):
                    sp.wait_ge(slab_begun, SLOTS * i + (j - SLOTS + 2))
                    sp.dma_start(ring[:, j:j + 1, :],
                                 A["slabs"][bass.ds(SLOTS * i + j, 1), :, :].rearrange("s p c -> p s c"))\
                      .then_inc(loaded[j], 16)
            for n in range(N_SLABS // SLOTS * SLOTS, N_SLABS):
                sp.wait_ge(slab_begun, n - SLOTS + 2)
                sp.dma_start(ring[:, n % SLOTS, :], A["slabs"][n, :, :]).then_inc(loaded[n % SLOTS], 16)
            sp.wait_ge(rt_dve, RT_FLAG)
            with sp.If(sp.value_load(flag[0:1, 0:1]) > 0):
                with sp.Fori(0, PASSES - 1) as i:
                    with sp.Fori(0, EXPERTS * SL_EXPERT // SLOTS) as c:
                        for j in range(SLOTS):
                            n = N_SLABS + j
                            sp.wait_ge(slab_begun, EXPERTS * SL_EXPERT * i + SLOTS * c + (n - SLOTS + 2))
                            sp.dma_start(ring[:, n % SLOTS:n % SLOTS + 1, :],
                                         A["slabs"][bass.ds(SLOTS * c + (SL_MOE + j), 1), :, :]
                                         .rearrange("s p c -> p s c")).then_inc(loaded[n % SLOTS], 16)
            sp.wait_ge(ln_act[3], 10)
            sp.dma_start(OUT, h[:, :, N_META:T]).then_inc(s_out, 16)
            sp.wait_ge(s_out, 16)

        @block.gpsimd
        def _(pool):
            pool.dma_start(onehot[0:33, :], A["onehot"]).then_inc(s_attn, 16)
            pool.dma_start(rbias[0:33, :], A["rel_bias"]).then_inc(s_attn, 16)
            pool.dma_start(bv[0:1, :], A["b_v"]).then_inc(s_attn, 16)
            pool.dma_start(sinks[:, :], A["sinks"].broadcast_to([P, HEADS])).then_inc(s_attn, 16)
            pool.dma_start(vec[:, :], A["vecs"]).then_inc(s_const, 16)
            pool.dma_start(eye[:, :], A["squares"][:, 0:P]).then_inc(s_const, 16)
            pool.dma_start(ones_d[:, :], A["squares"][:, P:2 * P]).then_inc(s_const, 16)
            pool.dma_start(same_head[:, :], A["squares"][:, 2 * P:3 * P]).then_inc(s_const, 16)
            pool.dma_start(mean_head[:, :], A["squares"][:, 3 * P:4 * P]).then_inc(s_const, 16)
            pool.dma_start(masks[:, :, :], A["masks"]).then_inc(s_const, 16)
            pool.memset(ones_row[0:1, :], 1.0).then_inc(s_ones, 1)
            pool.wait_ge(s_line, 3)
            pool.dma_start(scratch, line[0:HEADS, :].unsqueeze(1).broadcast_to([HEADS, Q_MAX, 2 * LINE]))\
                .then_inc(s_line_out, 16)
            pool.wait_ge(s_line_out, 16)
            for t, (q0, qn, kn) in enumerate(Q_TILES):
                for s, k0, k1 in ((0, 0, N_META), (1, N_META, kn)):
                    src = bass.AP(tensor=scratch.tensor, offset=s * LINE + T - 1 - q0 + k0,
                                  ap=[[2 * LINE - 1, qn], [Q_MAX * 2 * LINE, HEADS], [1, k1 - k0]])
                    pool.dma_start(bias_of(t)[0:qn, :, k0:k1], src).then_inc(s_bias, 16)
            pool.wait_ge(ln_act[1], 10)
            pool.wait_ge(y_ps[1], 8)
            pool.dma_start(lora1[:, :, :], A["lora1"]).then_inc(s_lora, 16)
            pool.dma_start(lora2[:, :, :], A["lora2"]).then_inc(s_lora, 16)
            pool.wait_ge(ln_act[2], 10)
            pool.dma_start(router[:, :, :], A["router"]).then_inc(s_router, 16)
            pool.dma_start(before[:, :, :], A["before"]).then_inc(s_router, 16)
            pool.dma_start(places, A["places"]).then_inc(s_router, 16)

        @block.tensor
        def _(pe):
            def arrived(n):
                pe.wait_ge(loaded[n % SLOTS], 16 * (n // SLOTS + 1))

            def tile(n, t):
                return ring[:, n % SLOTS, t * P:(t + 1) * P]

            def linear(base, outs, chunks, x, out, done, kept=None, banks=8, before_out=0):
                for m in range(outs):
                    if kept is not None and m + before_out >= banks:
                        pe.wait_ge(kept, m + before_out - banks + 1)
                    for k in range(chunks):
                        n, t = base + (m * chunks + k) // TILES, (m * chunks + k) % TILES
                        if t == 0:
                            arrived(n)
                        mm = pe.matmul(out(m), tile(n, t), x(k), start=k == 0, stop=k == chunks - 1)
                        if t == 0:
                            mm.then_inc(slab_begun, 1)
                    mm.then_inc(done, 1)

            def layer_norm(l):
                pe.wait_ge(zsum[l] if l < 3 else z_whole, 8 if l < 3 else 1)
                for k in range(KC):
                    mm = pe.matmul(PS[:, 0, 0:T], ones_d[:, :], z[:, k, :], start=k == 0, stop=k == KC - 1)
                mm.then_inc(ln_pe[l], 1)
                pe.wait_ge(ln_act[l], 1)
                for k in range(KC):
                    mm = pe.matmul(PS[:, 1, 0:T], ones_d[:, :], sq[:, k, :], start=k == 0, stop=k == KC - 1)
                mm.then_inc(ln_pe[l], 1)

            pe.wait_ge(s_attn, 64)
            for i in range(3):
                n = min(512, 2 * LINE - 512 * i)
                pe.matmul(PS[0:HEADS, i, 0:n], rbias[0:33, :], onehot[0:33, 512 * i:512 * i + n],
                          start=True, stop=True).then_inc(s_line_ps, 1)
            pe.wait_ge(s_line, 3)
            pe.wait_ge(s_h0, 16)
            linear(SL_QK, 10, KC, lambda k: h[:, k, :], lambda m: PS[:, m % 8, 0:T], qkv_ps, qkv_kept)
            arrived(SL_V)
            pe.wait_ge(s_ones, 1)
            for t in range(3):
                n = min(P, T - P * t)
                pe.wait_ge(qkv_kept, 10 + t - 7)
                for k in range(KC):
                    mm = pe.matmul(PS[0:n, (10 + t) % 8, 0:256], h[:, k, P * t:P * t + n],
                                   ring[:, SL_V % SLOTS, 256 * k:256 * k + 256], start=k == 0, stop=False)
                    if t == 0 and k == 0:
                        mm.then_inc(slab_begun, 1)
                pe.matmul(PS[0:n, (10 + t) % 8, 0:256], ones_row[0:1, 0:n], bv[0:1, :],
                          start=False, stop=True).then_inc(qkv_ps, 1)
            pe.wait_ge(qkv_kept, 13)
            pe.wait_ge(s_const, 96)

            units = [(t, m) for t in range(3) for m in range(8)]

            def scores(u):
                t, m = units[u]
                q0, qn, kn = Q_TILES[t]
                if u >= 2:
                    pe.wait_ge(sc_dve, 4 * (u - 1))
                for p in range(2):
                    o = slice(64 * p, 64 * p + 64)
                    mm = pe.matmul(PS[0:qn, 2 * (u % 2) + p, 0:kn], qk[o, m, q0:q0 + qn],
                                   qk[o, 8 + m // 4, 0:kn], start=True, stop=True)
                mm.then_inc(sc_ps, 1)

            scores(0)
            for u, (t, m) in enumerate(units):
                q0, qn, kn = Q_TILES[t]
                if u + 1 < len(units):
                    scores(u + 1)
                pe.wait_ge(sc_norm, u + 1)
                pe.wait_ge(pT_kept, u) if u else None
                parts = [(i, min(P, kn - P * i)) for i in range(-(-kn // P))]
                for p in range(2):
                    for i, n in parts:
                        mm = pe.transpose(PS[0:n, 4 + p, 96 * i:96 * i + qn], pr[0:qn, u % 2, p, P * i:P * i + n],
                                          eye[0:qn, 0:qn])
                mm.then_inc(pT_ps, 1)
                pe.wait_ge(pT_kept, u + 1)
                if u >= 2:
                    pe.wait_ge(o_kept, u - 1)
                for p in range(2):
                    g = 2 * (m // 4) + p
                    for i, n in parts:
                        mm = pe.matmul(PS[64 * p:64 * p + 64, 6 + u % 2, 0:qn], vn[0:n, i, 64 * g:64 * g + 64],
                                       prT[0:n, u % 2, p, i, 0:qn], start=i == 0, stop=i == len(parts) - 1)
                mm.then_inc(o_ps, 1)
            pe.wait_ge(o_kept, len(units))
            linear(SL_WO, 8, KC, lambda k: oT[:, k, :], lambda m: PS[:, m, 0:T], y_ps[0])
            layer_norm(0)

            pe.wait_ge(ln_act[0], 10)
            for f in range(FT):
                n = SL_GU + f
                if f >= 4:
                    pe.wait_ge(hid_dve, 2 * (f - 3))
                arrived(n)
                for t in range(TILES):
                    mm = pe.matmul(PS[:, 2 * (f % 4) + t // 8, 0:T], tile(n, t), h[:, t % 8, :],
                                   start=t % 8 == 0, stop=t % 8 == 7)
                    if t == 0:
                        mm.then_inc(slab_begun, 1)
                mm.then_inc(gu_ps, 1)
            pe.wait_ge(hid_dve, 2 * FT)
            linear(SL_DN, 8, FT, lambda k: hid[:, k, :], lambda m: PS[:, m, 0:T], y_ps[1])
            layer_norm(1)

            for i in range(3):
                pe.wait_ge(mixed, 8 * (i + 1))
                linear(SL_RKV + 4 * i, 8, KC, lambda k: mix[:, i % 2, k, :], lambda m: PS[:, m, 0:T],
                       rkv_ps, rkv_kept, before_out=8 * i)
            pe.wait_ge(s_lora, 32)
            pe.wait_ge(rkv_kept, 24)
            for i, c0, n, b in ((3, 0, 64, 0), (4, 64, 64, 1), (5, 128, 128, 2), (5, 256, 32, 3)):
                pe.wait_ge(mixed, 8 * (i + 1))
                for k in range(KC):
                    mm = pe.matmul(PS[0:n, b, 0:T], lora1[:, k, c0:c0 + n], mix[:, i % 2, k, :],
                                   start=k == 0, stop=k == KC - 1)
                mm.then_inc(l1_ps, 1)
            pe.wait_ge(l1_kept, 4)
            for i in range(24):
                j, m = i // 8, i % 8
                if i >= 8:
                    pe.wait_ge(l2_kept, i - 7)
                if j < 2:
                    mm = pe.matmul(PS[:, i % 8, 0:T], lora2[0:64, j, m * P:(m + 1) * P], sq[0:64, j, :],
                                   start=True, stop=True)
                else:
                    pe.matmul(PS[:, i % 8, 0:T], lora2[:, 2, m * P:(m + 1) * P], sq[:, 2, :],
                              start=True, stop=False)
                    mm = pe.matmul(PS[:, i % 8, 0:T], lora2[0:32, 3, m * P:(m + 1) * P], sq[0:32, 3, :],
                                   start=False, stop=True)
                mm.then_inc(l2_ps, 1)

            def head_sums(square, x, wait, value, done):
                pe.wait_ge(wait, value)
                for m in range(KC):
                    mm = pe.matmul(PS[:, m, 0:T], square, x(m), start=True, stop=True)
                mm.then_inc(done, 1)

            pe.wait_ge(l2_kept, 24)
            head_sums(same_head[:, :], lambda m: sq[:, m, :], pre_act, 1, pre_pe)
            head_sums(same_head[:, :], lambda m: sq[:, m, :], pre_dve, PRE_BONUS, pre_pe)

            def per_head(out, lhsT, rhs, first=True, last=True):
                for m in range(KC):
                    for p in range(2):
                        o = slice(64 * p, 64 * p + 64)
                        mm = pe.matmul(out[o, m, :], lhsT[o, m, :] if lhsT is not None else masks[o, EYE, :],
                                       rhs[o, m, :] if rhs is not None else masks[o, EYE, :],
                                       start=first, stop=last)
                return mm

            def grouped(out, pairs):
                for m in range(KC):
                    for p in range(2):
                        o = slice(64 * p, 64 * p + 64)
                        for i, (lhsT, rhs) in enumerate(pairs):
                            mm = pe.matmul(out[o, m, :], lhsT[o, m, :], rhs[o, m, :],
                                           start=i == 0, stop=i == len(pairs) - 1)
                return mm

            EYE = MASKS.index("eye64")
            pe.wait_ge(pre_dve, PRE_LAST)
            for c in range(N_CH):
                def dv(n):
                    pe.wait_ge(c_dve, CD * c + n)
                dv(CD_IN)
                for b, (l, r) in enumerate(((bt, at), (at, bt), (kt, at), (bt, rt), (kt, rt))):
                    per_head(bank(b), l, r).then_inc(c_pe, 1)
                for b, x in enumerate((vc, bt, kt)):
                    per_head(bank(5 + b), x, None).then_inc(c_pe, 1)
                for i, b in enumerate(LEVELS):
                    dv(CD_MASKED + 4 * i + 1)
                    per_head(bank(0), otm, tm).then_inc(c_pe, 1)
                    dv(CD_MASKED + 4 * i + 2)
                    per_head(bank(1), ttm, um).then_inc(c_pe, 1)
                    per_head(bank(2), um, ttm).then_inc(c_pe, 1)
                dv(CD_MASKED + 4 * len(LEVELS))
                grouped(bank(3), ((mak, vnat), (at, st))).then_inc(c_pe, 1)
                dv(CD_MASKED + 4 * len(LEVELS) + 1)
                grouped(bank(4), ((ttm, xm),)).then_inc(c_pe, 1)
                dv(CD_MASKED + 4 * len(LEVELS) + 2)
                grouped(bank(5), ((st, rt), (sam, mrb), (vnat, mrk))).then_inc(c_pe, 1)
                grouped(bank(6), ((bnat, sam), (knat, vnat))).then_inc(c_pe, 1)

            head_sums(mean_head[:, :], lambda m: r_[:, m, 0:T], c_dve, CD * N_CH + PRE_ST, gn_pe)
            head_sums(mean_head[:, :], lambda m: sq[:, m, :], gn_act, 1, gn_pe)
            pe.wait_ge(gn_dve, 8)
            linear(SL_O2, 8, KC, lambda k: r_[:, k, 0:T], lambda m: PS[:, m, 0:T], y_ps[2])
            layer_norm(2)

            pe.wait_ge(ln_act[2], 10)
            pe.wait_ge(s_router, 48)
            tokens = [(t, min(P, T - P * t)) for t in range(3)]
            for t, n in tokens:
                for k in range(KC):
                    mm = pe.matmul(PS[0:n, 6, EXPERTS * t:EXPERTS * (t + 1)], h[:, k, P * t:P * t + n],
                                   router[:, k, :], start=k == 0, stop=k == KC - 1)
            mm.then_inc(rt_pe, 1)
            for t, n in tokens:
                for k in range(KC):
                    mm = pe.transpose(PS[0:n, 2 * t + k // 4, P * (k % 4):P * (k % 4) + P],
                                      h[:, k, P * t:P * t + n], eye[:, :])
            mm.then_inc(rt_pe, 1)
            pe.wait_ge(rt_dve, RT_SEL)
            for t, n in tokens:
                for i in range(t + 1):
                    k = tokens[i][1]
                    mm = pe.matmul(PS[0:n, 7, EXPERTS * t:EXPERTS * (t + 1)], (ones if i < t else tri)[0:k, 0:n],
                                   sel[0:k, i, :], start=i == 0, stop=i == t)
            mm.then_inc(rt_pe, 1)
            for x, dve_step, act_step in ((gates, RT_POS, 2), (place, RT_POS, 3)):
                pe.wait_ge(rt_dve, dve_step)
                pe.wait_ge(rt_act, act_step)
                for e in range(EXPERTS):
                    for t, n in tokens:
                        mm = pe.matmul(PS[:, e, P * t:P * t + n], x[0:n, t, e:e + 1].broadcast_to([n, P]),
                                       eye[0:n, 0:n], start=True, stop=True)
                mm.then_inc(rt_pe, 1)
            pe.wait_ge(rt_act, 4)

            def gather(o, first=False):
                pe.wait_ge(picked, 3 * o + 3)
                if not first:
                    pe.wait_ge(xe_kept, o)
                for k in range(KC):
                    for t, n in tokens:
                        mm = pe.matmul(PS[:, 6 + k // 4, CAP * (k % 4):CAP * (k % 4 + 1)],
                                       hn[0:n, t, P * k:P * k + P], pick[0:n, t, :], start=t == 0, stop=t == 2)
                mm.then_inc(gathered, 1)

            def expert(q, o):
                with pe.Fori(0, FTE // SLOTS) as j:
                    for k in range(SLOTS):
                        n = SL_MOE + k
                        if k == 0:
                            pe.wait_ge(xe_kept, o + 1)
                            pe.wait_ge(zsum[3], 8 * q + 1)
                        pe.wait_ge(hid_dve, 2 * FTE * q + 2 * SLOTS * j + (2 * (FT + k - 2)))
                        pe.wait_ge(loaded[n % SLOTS], 96 * q + 16 * j + 16 * (n // SLOTS + 1))
                        b = k % 3 if k < 6 else 3
                        for t in range(TILES):
                            mm = pe.matmul(PS[:, b, CAP * (t // 8):CAP * (t // 8 + 1)], tile(n, t), xe[:, t % 8, :],
                                           start=t % 8 == 0, stop=t % 8 == 7)
                            if t == 0:
                                mm.then_inc(slab_begun, 1)
                        mm.then_inc(gu_ps, 1)
                for f in range(FTE):
                    n = SL_MOE + FTE + f // 2
                    if f == 0:
                        pe.wait_ge(hid_dve, 2 * FTE * q + 2 * (FT + FTE))
                    if f % 2 == 0:
                        pe.wait_ge(loaded[n % SLOTS], 96 * q + 16 * (n // SLOTS + 1))
                    for i in range(2):
                        c = D * (f % 2) + 512 * i
                        mm = pe.matmul(PS[0:CAP, 4 + i, :], hid_e[:, f, :], ring[:, n % SLOTS, c:c + 512],
                                       start=f == 0, stop=f == FTE - 1)
                        if c == 0:
                            mm.then_inc(slab_begun, 1)
                        if f == FTE - 1:
                            mm.then_inc(dn_ps, 1)

            def scatter(q):
                pe.wait_ge(put_dve, 2 * q + 2)
                for m in range(KC):
                    if m % 4 == 0:
                        pe.wait_ge(yn_kept, 2 * q + 1 + m // 4)
                    if m >= 4:
                        pe.wait_ge(zsum[3], 8 * q + (m - 2))
                    pe.matmul(PS[:, m % 4, 0:T], yn[0:CAP, P * m:P * m + P], put[0:CAP, :],
                              start=True, stop=True).then_inc(y_ps[3], 1)

            gather(0, first=True)
            with pe.Fori(0, EXPERTS) as e:
                expert(e, e)
                gather(e + 1)
                scatter(e)
            with pe.If(pe.value_load(flag[0:1, 0:1]) > 0):
                with pe.Fori(1, PASSES) as i:
                    with pe.Fori(0, EXPERTS) as e:
                        q = EXPERTS * i + e
                        gather(q + 1)
                        expert(q, q + 1)
                        scatter(q)
            layer_norm(3)

        @block.scalar
        def _(act):
            def layer_norm(l):
                act.wait_ge(ln_dve[l], 1)
                act.activation(sq[:, :, :], z[:, :, :], ACT.Square).then_inc(ln_act[l], 1)
                act.wait_ge(ln_dve[l], 2)
                act.activation(rstd[:, :], rstd[:, :], ACT.Sqrt).then_inc(ln_act[l], 1)
                for k in range(KC):
                    act.wait_ge(ln_dve[l], 4 + k)
                    act.activation(h[:, k, :], z[:, k, :], ACT.Identity, bias=v_of(f"b{l}", k))\
                       .then_inc(ln_act[l], 1)

            act.wait_ge(s_const, 96)
            for m in range(10):
                act.wait_ge(qkv_ps, m + 1)
                b = v_of("b_q", m) if m < 8 else v_of("b_k", m - 8)
                act.activation(qk[:, m, :], PS[:, m % 8, 0:T], ACT.Identity, bias=b).then_inc(qkv_kept, 1)
            for t in range(3):
                n = min(P, T - P * t)
                act.wait_ge(qkv_ps, 11 + t)
                act.activation(vn[0:n, t, :], PS[0:n, (10 + t) % 8, 0:256], ACT.Copy).then_inc(qkv_kept, 1)

            units = [(t, m) for t in range(3) for m in range(8)]

            def exps(u):
                q0, qn, kn = Q_TILES[units[u][0]]
                act.wait_ge(sc_dve, 4 * (u + 1))
                for p in range(2):
                    a = act.activation(pr[0:qn, u % 2, p, 0:kn + 1], sb_[0:qn, u % 2, p, 0:kn + 1], ACT.Exp,
                                       bias=negm[0:qn, u % 2, p:p + 1], accum_out=den[0:qn, u % 2, p:p + 1])
                a.then_inc(sc_exp, 1)

            def keep_out(u):
                t, m = units[u]
                q0, qn, kn = Q_TILES[t]
                act.wait_ge(o_ps, u + 1)
                act.activation(oT[:, m, q0:q0 + qn], PS[:, 6 + u % 2, 0:qn], ACT.Copy).then_inc(o_kept, 1)

            exps(0)
            for u, (t, m) in enumerate(units):
                q0, qn, kn = Q_TILES[t]
                if u + 1 < len(units):
                    exps(u + 1)
                act.wait_ge(pT_ps, u + 1)
                full, part = kn // P, kn % P
                src = PS[:, 4:6, 0:288].rearrange("p b (i q) -> p b i q", i=3)
                if full:
                    a = act.activation(prT[:, u % 2, :, 0:full, 0:qn], src[:, :, 0:full, 0:qn], ACT.Copy)
                if part:
                    a = act.activation(prT[0:part, u % 2, :, full, 0:qn], src[0:part, :, full, 0:qn], ACT.Copy)
                a.then_inc(pT_kept, 1)
                if u >= 1:
                    keep_out(u - 1)
            keep_out(len(units) - 1)
            layer_norm(0)

            for f in range(FT):
                act.wait_ge(gu_ps, f + 1)
                if f:
                    act.wait_ge(hid_dve, 2 * f)
                act.activation(sg[:, :], PS[:, 2 * (f % 4), 0:T], ACT.Sigmoid).then_inc(gu_sig, 1)
            layer_norm(1)

            for i in range(24):
                act.wait_ge(rkv_ps, i + 1)
                dst = (r_, k_, v_)[i // 8]
                act.activation(dst[:, i % 8, 0:T], PS[:, i % 8, 0:T], ACT.Copy).then_inc(rkv_kept, 1)
            for i, (n, f) in enumerate(((64, ACT.Tanh), (64, ACT.Copy), (128, ACT.Sigmoid), (32, ACT.Sigmoid))):
                act.wait_ge(l1_ps, i + 1)
                act.activation(sq[0:n, i, :], PS[0:n, i, 0:T], f).then_inc(l1_kept, 1)
            for i in range(24):
                j, m = i // 8, i % 8
                act.wait_ge(l2_ps, i + 1)
                if j < 2:
                    a = act.activation((cum, a_)[j][:, m, 0:T], PS[:, m, 0:T], ACT.Sigmoid,
                                       bias=v_of(("w0", "a0")[j], m))
                else:
                    a = act.activation(g_[:, m, :], PS[:, m, 0:T], ACT.Copy)
                a.then_inc(l2_kept, 1)
            act.wait_ge(pre_dve, 1)
            act.activation(sq[:, :, :], kk[:, :, 0:T], ACT.Square).then_inc(pre_act, 1)
            act.wait_ge(pre_dve, 2)
            act.activation(sq[:, :, :], sq[:, :, :], ACT.Sqrt).then_inc(pre_act, 1)

            act.wait_ge(pre_dve, PRE_LAST)
            for c in range(N_CH):
                act.wait_ge(c_pe, CP * c + 0)
                act.wait_ge(c_dve, CD * c + PRE_ST)
                cc = cum[:, :, slice(CH * c, CH * c + CH)]
                act.activation(e1[:, :, :], cc, ACT.Exp, scale=-DECAY).then_inc(c_act, 1)
                act.activation(em[:, :, :], cc, ACT.Exp, scale=DECAY).then_inc(c_act, 1)

            act.wait_ge(gn_dve, 1)
            act.activation(sq[:, :, :], r_[:, :, 0:T], ACT.Square).then_inc(gn_act, 1)
            act.wait_ge(gn_dve, 2)
            act.activation(sq[:, :, :], sq[:, :, :], ACT.Sqrt).then_inc(gn_act, 1)
            layer_norm(2)
            act.wait_ge(rt_pe, 2)
            for t in range(3):
                n = min(P, T - P * t)
                a = act.activation(hn[0:n, t, :].rearrange("p (b c) -> p b c", b=2), PS[0:n, 2 * t:2 * t + 2, :],
                                   ACT.Copy)
            a.then_inc(rt_act, 1)
            act.wait_ge(rt_dve, RT_EXP)
            act.activation(ex[:, :, :], ex[:, :, :], ACT.Exp).then_inc(rt_act, 1)
            act.wait_ge(rt_pe, 4)
            act.activation(gate_b[:, :, :], PS[:, :, 0:T], ACT.Copy).then_inc(rt_act, 1)
            act.wait_ge(rt_pe, 5)
            act.activation(place_b[:, 0:EXPERTS, :], PS[:, :, 0:T], ACT.Copy).then_inc(rt_act, 1)

            def keep_tokens(o):
                act.wait_ge(gathered, o + 1)
                for i in range(2):
                    a = act.activation(xe[:, 4 * i:4 * i + 4, :],
                                       PS[:, 6 + i, 0:4 * CAP].rearrange("p (k c) -> p k c", k=4), ACT.Copy)
                a.then_inc(xe_kept, 1)

            def expert(q):
                with act.Fori(0, FTE // SLOTS) as j:
                    for k in range(SLOTS):
                        act.wait_ge(gu_ps, FTE * q + SLOTS * j + (FT + k + 1))
                        act.wait_ge(hid_dve, 2 * FTE * q + 2 * SLOTS * j + 2 * (FT + k))
                        act.activation(sge[:, :], PS[:, k % 3 if k < 6 else 3, 0:CAP], ACT.Sigmoid)\
                           .then_inc(gu_sig, 1)
                for i in range(2):
                    act.wait_ge(dn_ps, 2 * q + 1 + i)
                    act.activation(yn[0:CAP, 512 * i:512 * i + 512], PS[0:CAP, 4 + i, :], ACT.Copy)\
                       .then_inc(yn_kept, 1)

            keep_tokens(0)
            with act.Fori(0, EXPERTS) as e:
                expert(e)
                keep_tokens(e + 1)
            act.wait_ge(rt_dve, RT_FLAG)
            with act.If(act.value_load(flag[0:1, 0:1]) > 0):
                with act.Fori(1, PASSES) as i:
                    with act.Fori(0, EXPERTS) as e:
                        q = EXPERTS * i + e
                        keep_tokens(q + 1)
                        expert(q)
            layer_norm(3)

        @block.vector
        def _(dve):
            class Steps:
                def __init__(self, s, n=0):
                    self.s, self.n = s, n

                def step(self, ins):
                    self.n = self.n + 1
                    ins.then_inc(self.s, 1)
                    dve.wait_ge(self.s, self.n)

                def mark(self, ins):
                    self.n = self.n + 1
                    ins.then_inc(self.s, 1)

            def residual(l):
                for m in range(KC):
                    dve.wait_ge(y_ps[l], m + 1)
                    dve.scalar_tensor_tensor(out=z[:, m, :], in0=h[:, m, :], scalar=ALPHA, in1=PS[:, m, 0:T],
                                             op0=ALU.mult, op1=ALU.add).then_inc(zsum[l], 1)

            def layer_norm(l):
                s = Steps(ln_dve[l])
                dve.wait_ge(ln_pe[l], 1)
                dve.wait_ge(zsum[l] if l < 3 else z_whole, 8 if l < 3 else 1)
                s.step(dve.tensor_tensor(out=z[:, :, :], in0=z[:, :, :],
                                         in1=PS[:, 0:1, 0:T].broadcast_to([P, KC, T]), op=ALU.subtract))
                dve.wait_ge(ln_pe[l], 2)
                s.mark(dve.tensor_scalar(rstd[:, :], PS[:, 1, 0:T], LN_EPS, None, ALU.add))
                dve.wait_ge(ln_act[l], 2)
                s.step(dve.reciprocal(rstd[:, :], rstd[:, :]))
                for k in range(KC):
                    s.mark(dve.scalar_tensor_tensor(out=z[:, k, :], in0=z[:, k, :], scalar=v_of(f"g{l}", k),
                                                    in1=rstd[:, :], op0=ALU.mult, op1=ALU.mult))

            for i in range(3):
                n = min(512, 2 * LINE - 512 * i)
                dve.wait_ge(s_line_ps, i + 1)
                dve.tensor_copy(line[0:HEADS, 512 * i:512 * i + n], PS[0:HEADS, i, 0:n]).then_inc(s_line, 1)

            units = [(t, m) for t in range(3) for m in range(8)]
            sc, nr = Steps(sc_dve), Steps(nrm)

            def biased(u):
                t, m = units[u]
                q0, qn, kn = Q_TILES[t]
                dve.wait_ge(sc_ps, u + 1)
                if u >= 2:
                    dve.wait_ge(sc_exp, u - 1)
                sc.mark(dve.scalar_tensor_tensor(
                    out=sb_[0:qn, u % 2, :, 0:kn], in0=PS[0:qn, 2 * (u % 2):2 * (u % 2) + 2, 0:kn],
                    scalar=HD ** -0.5, in1=bias_of(t)[0:qn, 2 * m:2 * m + 2, :], op0=ALU.mult, op1=ALU.add))
                sc.step(dve.tensor_copy(sb_[0:qn, u % 2, :, kn:kn + 1],
                                        sinks[0:qn, 2 * m:2 * m + 2].unsqueeze(2)))
                sc.step(dve.tensor_reduce(out=mx[0:qn, :], in_=sb_[0:qn, u % 2, :, 0:kn + 1], axis=AX.X, op=ALU.max))
                sc.mark(dve.tensor_scalar(negm[0:qn, u % 2, :], mx[0:qn, :], -1.0, None, ALU.mult))

            dve.wait_ge(s_attn, 64)
            dve.wait_ge(s_bias, 96)
            biased(0)
            for u, (t, m) in enumerate(units):
                q0, qn, kn = Q_TILES[t]
                if u + 1 < len(units):
                    biased(u + 1)
                dve.wait_ge(sc_exp, u + 1)
                if u:
                    dve.wait_ge(sc_norm, u)
                nr.step(dve.reciprocal(rden[0:qn, :], den[0:qn, u % 2, :]))
                for p in range(2):
                    i = dve.tensor_scalar(pr[0:qn, u % 2, p, 0:kn], pr[0:qn, u % 2, p, 0:kn],
                                          rden[0:qn, p:p + 1], None, ALU.mult)
                i.then_inc(sc_norm, 1)
            residual(0)
            layer_norm(0)

            s = Steps(hid_dve)
            for f in range(FT):
                dve.wait_ge(gu_sig, f + 1)
                s.step(dve.tensor_tensor(out=gu[:, :], in0=sg[:, :], in1=PS[:, 2 * (f % 4), 0:T], op=ALU.mult))
                s.step(dve.tensor_tensor(out=hid[:, f, :], in0=gu[:, :], in1=PS[:, 2 * (f % 4) + 1, 0:T],
                                         op=ALU.mult))
            residual(1)
            layer_norm(1)

            dve.wait_ge(ln_act[1], 10)
            s = Steps(xx_steps)
            s.mark(dve.tensor_tensor(out=z[:, :, 1:T], in0=h[:, :, 0:T - 1], in1=h[:, :, 1:T], op=ALU.subtract))
            s.step(dve.tensor_scalar(z[:, :, 0:1], h[:, :, 0:1], -1.0, None, ALU.mult))
            for x in (r_, k_, kk, a_, v_, cum):
                i = dve.memset(x[:, :, T:TP], 0.0)
            i.then_inc(pads, 1)
            for i, name in enumerate(("mu_r", "mu_k", "mu_v", "mu_w", "mu_a", "mu_g")):
                if 2 <= i < 5:
                    dve.wait_ge(rkv_ps, 8 * (i - 1))
                if i == 5:
                    dve.wait_ge(l1_ps, 1)
                for k in range(KC):
                    dve.scalar_tensor_tensor(out=mix[:, i % 2, k, :], in0=z[:, k, :], scalar=v_of(name, k),
                                             in1=h[:, k, :], op0=ALU.mult, op1=ALU.add).then_inc(mixed, 1)
            s = Steps(pre_dve)
            dve.wait_ge(pads, 1)
            dve.wait_ge(l2_kept, 24)
            s.step(dve.tensor_tensor(out=kk[:, :, 0:T], in0=k_[:, :, 0:T], in1=v_all("k_k"), op=ALU.mult))
            dve.wait_ge(pre_pe, 1)
            s.mark(dve.tensor_scalar(sq[:, :, :], PS[:, :, 0:T], 1e-24, None, ALU.max))
            dve.wait_ge(pre_act, 2)
            s.step(dve.reciprocal(sq[:, :, :], sq[:, :, :]))
            s.step(dve.tensor_tensor(out=kk[:, :, 0:T], in0=kk[:, :, 0:T], in1=sq[:, :, :], op=ALU.mult))
            s.step(dve.scalar_tensor_tensor(out=sq[:, :, :], in0=a_[:, :, 0:T], scalar=-1.0, in1=v_all("k_a"),
                                            op0=ALU.add, op1=ALU.mult))
            s.step(dve.scalar_tensor_tensor(out=k_[:, :, 0:T], in0=sq[:, :, :], scalar=1.0, in1=k_[:, :, 0:T],
                                            op0=ALU.add, op1=ALU.mult))
            s.step(dve.tensor_tensor(out=a_[:, :, 0:T], in0=a_[:, :, 0:T], in1=kk[:, :, 0:T], op=ALU.mult))
            s.step(dve.tensor_tensor(out=sq[:, :, :], in0=r_[:, :, 0:T], in1=k_[:, :, 0:T], op=ALU.mult))
            s.step(dve.tensor_tensor(out=sq[:, :, :], in0=sq[:, :, :], in1=v_all("r_k"), op=ALU.mult))
            assert s.n == PRE_BONUS
            flat = lambda x: x.rearrange("p a b -> p (a b)")
            restart = arena[:, OV:OV + KC * TP]
            s.step(dve.memset(restart, 1.0))
            s.step(dve.memset(restart.rearrange("p (c t) -> p c t", t=CH)[:, :, 0:1], 0.0))
            s.step(dve.tensor_tensor_scan(flat(cum), restart, flat(cum), 0.0, ALU.mult, ALU.add))
            dve.wait_ge(pre_pe, 2)
            s.step(dve.tensor_tensor(out=z[:, :, :], in0=PS[:, :, 0:T], in1=v_[:, :, 0:T], op=ALU.mult))
            s.step(dve.memset(st[:, :, :], 0.0))
            assert s.n == PRE_LAST

            for c in range(N_CH):
                s = Steps(c_dve, CD * c)
                cs = slice(CH * c, CH * c + CH)

                def pw(n):
                    dve.wait_ge(c_pe, CP * c + n)
                tt = lambda o, a, b, op=ALU.mult: dve.tensor_tensor(out=o, in0=a, in1=b, op=op)
                dve.wait_ge(c_act, 2 * c + 2)
                s.step(tt(rt[:, :, :], r_[:, :, cs], e1[:, :, :]))
                s.step(dve.tensor_scalar(at[:, :, 0:1], kk[:, :, slice(CH * c, CH * c + 1)], -1.0, None, ALU.mult))
                s.step(dve.scalar_tensor_tensor(out=at[:, :, 1:CH], in0=kk[:, :, slice(CH * c + 1, CH * c + CH)],
                                                scalar=-1.0, in1=e1[:, :, 0:CH - 1], op0=ALU.mult, op1=ALU.mult))
                s.step(tt(bt[:, :, :], a_[:, :, cs], em[:, :, :]))
                s.step(tt(kt[:, :, :], k_[:, :, cs], em[:, :, :]))
                s.step(dve.tensor_copy(vc[:, :, :], v_[:, :, cs]))
                pw(1)
                s.step(tt(ltm[:, :, :], bank(0), mask("upper")))
                s.step(tt(ttm[:, :, :], ltm[:, :, :], mask("low2T")))
                s.step(tt(ttm[:, :, :], ttm[:, :, :], mask("eye64"), ALU.add))
                pw(2)
                s.step(tt(tm[:, :, :], bank(1), mask("low2")))
                s.step(tt(tm[:, :, :], tm[:, :, :], mask("eye64"), ALU.add))
                pw(3)
                s.step(tt(mak[:, :, :], bank(2), mask("upper")))
                pw(4)
                s.step(tt(mrb[:, :, :], bank(3), mask("upper_eq")))
                pw(5)
                s.step(tt(mrk[:, :, :], bank(4), mask("upper_eq")))
                for i, x in enumerate((vnat, bnat, knat)):
                    pw(6 + i)
                    s.step(dve.tensor_copy(x[:, :, :], bank(5 + i)))
                for i, b in enumerate(LEVELS):
                    s.step(tt(otm[:, :, :], ltm[:, :, :], mask(f"off{b}")))
                    pw(8 + 3 * i + 1)
                    s.step(dve.tensor_copy(um[:, :, :], bank(0)))
                    pw(8 + 3 * i + 3)
                    s.step(tt(tm[:, :, :], tm[:, :, :], bank(1), ALU.add))
                    s.step(tt(ttm[:, :, :], ttm[:, :, :], bank(2), ALU.add))
                n = 8 + 3 * len(LEVELS)
                pw(n + 1)
                s.step(dve.tensor_copy(xm[:, :, :], bank(3)))
                pw(n + 2)
                s.step(dve.tensor_copy(sam[:, :, :], bank(4)))
                pw(n + 4)
                s.step(dve.tensor_copy(r_[:, :, cs], bank(5)))
                s.step(tt(st[:, :, :], st[:, :, :], bank(6), ALU.add))
                s.step(tt(st[:, :, :], st[:, :, :], e1[:, :, CH - 1:CH].broadcast_to([P, KC, CH])))

            s = Steps(gn_dve)
            y = r_[:, :, 0:T]
            dve.wait_ge(gn_pe, 1)
            s.step(tt(y, y, PS[:, :, 0:T], ALU.subtract))
            dve.wait_ge(gn_pe, 2)
            s.mark(dve.tensor_scalar(sq[:, :, :], PS[:, :, 0:T], GN_EPS, None, ALU.add))
            dve.wait_ge(gn_act, 2)
            s.step(dve.reciprocal(sq[:, :, :], sq[:, :, :]))
            s.step(tt(y, y, sq[:, :, :]))
            s.step(tt(y, y, v_all("lnx_g")))
            s.step(tt(y, y, v_all("lnx_b"), ALU.add))
            s.step(tt(y, y, z[:, :, :], ALU.add))
            s.step(tt(y, y, g_[:, :, :]))
            residual(2)
            layer_norm(2)

            dve.wait_ge(ln_act[2], 10)
            dve.wait_ge(s_router, 48)
            dve.wait_ge(rt_pe, 1)
            s = Steps(rt_dve)
            s.step(dve.memset(lg[:, :, :], 0.0))
            for t in range(3):
                n = min(P, T - P * t)
                s.step(dve.tensor_copy(lg[0:n, t, :], PS[0:n, 6, EXPERTS * t:EXPERTS * (t + 1)]))
            four = [P, 3, EXPERTS, EXPERTS]
            other, own = lg[:, :, :].unsqueeze(2).broadcast_to(four), lg[:, :, :].unsqueeze(3).broadcast_to(four)
            s.step(tt(cmp_a[:, :, :, :], other, own, ALU.is_gt))
            s.step(tt(cmp_b[:, :, :, :], other, own, ALU.is_equal))
            s.step(tt(cmp_b[:, :, :, :], cmp_b[:, :, :, :], before[:, :, :].unsqueeze(1).broadcast_to(four)))
            s.step(tt(cmp_a[:, :, :, :], cmp_a[:, :, :, :], cmp_b[:, :, :, :], ALU.add))
            s.step(dve.tensor_reduce(out=sel[:, :, :], in_=cmp_a[:, :, :, :], axis=AX.X, op=ALU.add))
            s.step(dve.tensor_scalar(sel[:, :, :], sel[:, :, :], 2.0, None, ALU.is_lt))
            assert s.n == RT_SEL
            s.step(dve.tensor_reduce(out=top[:, :], in_=lg[:, :, :], axis=AX.X, op=ALU.max))
            s.step(tt(ex[:, :, :], lg[:, :, :], top[:, :].unsqueeze(2).broadcast_to([P, 3, EXPERTS]), ALU.subtract))
            assert s.n == RT_EXP
            dve.wait_ge(rt_act, 2)
            s.step(tt(gates[:, :, :], ex[:, :, :], sel[:, :, :]))
            s.step(dve.tensor_reduce(out=top[:, :], in_=gates[:, :, :], axis=AX.X, op=ALU.add))
            s.step(dve.reciprocal(top[:, :], top[:, :]))
            s.step(tt(gates[:, :, :], gates[:, :, :], top[:, :].unsqueeze(2).broadcast_to([P, 3, EXPERTS])))
            dve.wait_ge(rt_pe, 3)
            for t in range(3):
                n = min(P, T - P * t)
                s.step(dve.scalar_tensor_tensor(out=place[0:n, t, 0:EXPERTS], in0=PS[0:n, 7, EXPERTS * t:EXPERTS * (t + 1)],
                                                scalar=1.0, in1=sel[0:n, t, :], op0=ALU.add, op1=ALU.mult))
            s.step(dve.tensor_scalar(place[:, 0:2, 0:EXPERTS], place[:, 0:2, 0:EXPERTS], -1.0, None, ALU.add))
            n = T - 2 * P
            s.step(dve.tensor_scalar(place[0:n, 2, 0:EXPERTS], place[0:n, 2, 0:EXPERTS], -1.0, None, ALU.add))
            assert s.n == RT_POS
            dve.memset(place[:, :, EXPERTS:], -1.0).then_inc(pads, 1)
            dve.tensor_scalar(z[:, :, :], h[:, :, :], ALPHA, None, ALU.mult).then_inc(zsum[3], 1)
            dve.wait_ge(rt_act, 4)
            dve.wait_ge(pads, 2)
            s.step(dve.tensor_reduce(out=most[:, :], in_=place_b[:, 0:EXPERTS, :].rearrange("p e t -> p (e t)"),
                                     axis=AX.X, op=ALU.max))
            s.step(dve.tensor_scalar(flag[:, :], most[:, :], float(CAP), None, ALU.is_ge))
            assert s.n == RT_FLAG
            dve.wait_ge(zsum[3], 1)

            def build_pick(e, first):
                for t in range(3):
                    n = min(P, T - P * t)
                    dve.tensor_scalar(pick[0:n, t:t + 1, :], first[0:n].unsqueeze(1), place[0:n, t, bass.ds(e, 1)]
                                      if e is not None else place[0:n, t, 0:1], None, ALU.is_equal)\
                       .then_inc(picked, 1)

            def build_put(q, e, column):
                dve.tensor_scalar(put[:, :].unsqueeze(1), place_b[:, bass.ds(e, 1), :], column, None, ALU.is_equal)\
                   .then_inc(put_dve, 1)
                dve.wait_ge(put_dve, 2 * q + 1)
                tt(put[:, :].unsqueeze(1), put[:, :].unsqueeze(1), gate_b[:, bass.ds(e, 1), :]).then_inc(put_dve, 1)

            def expert(q):
                with dve.Fori(0, FTE // SLOTS) as j:
                    s = Steps(hid_dve, 2 * FTE * q + 2 * SLOTS * j + 2 * FT)
                    for k in range(SLOTS):
                        dve.wait_ge(gu_sig, FTE * q + SLOTS * j + (FT + k + 1))
                        b = k % 3 if k < 6 else 3
                        s.step(tt(gue[:, :], sge[:, :], PS[:, b, 0:CAP]))
                        s.step(tt(hid_e[:, bass.ds(SLOTS * j + k, 1), :], gue[:, :].unsqueeze(1),
                                  PS[:, b:b + 1, CAP:2 * CAP]))
                for m in range(KC):
                    dve.wait_ge(y_ps[3], 8 * q + (m + 1))
                    tt(z[:, m, :], z[:, m, :], PS[:, m % 4, 0:T], ALU.add).then_inc(zsum[3], 1)

            build_pick(None, numbers[:, 0:CAP])
            with dve.Fori(0, EXPERTS) as e:
                dve.wait_ge(gathered, e + 1)
                build_pick(e + 1, numbers[:, 0:CAP])
                build_put(e, e, number_p[:, 0:1])
                expert(e)
            with dve.If(dve.value_load(flag[0:1, 0:1]) > 0):
                with dve.Fori(1, PASSES) as i:
                    with dve.Fori(0, EXPERTS) as e:
                        q = EXPERTS * i + e
                        dve.wait_ge(gathered, q + 1)
                        build_pick(e, numbers[:, bass.ds(CAP * i, CAP)])
                        build_put(q, e, number_p[:, bass.ds(i, 1)])
                        expert(q)
            dve.memset(most[:, :], 0.0).then_inc(z_whole, 1)
            dve.wait_ge(z_whole, 1)
            layer_norm(3)


def slabs_of(tiles):
    n = tiles.shape[0] // TILES
    return tiles.reshape(n, TILES, P, P).transpose(0, 2, 1, 3).reshape(n, P, TILES * P)


def tiles_of(w):
    k, m = w.shape
    return w.reshape(k // P, P, m // P, P).transpose(2, 0, 1, 3).reshape(-1, P, P)


def gate_up_tiles(w):
    k, f = w.shape
    t = w.reshape(k // P, P, 2, f // 2 // P, P).transpose(3, 2, 0, 1, 4)
    return t.reshape(-1, P, P)


def chunked(v):
    return v.reshape(-1, P).T


def t5_buckets():
    n = np.arange(T)
    f = np.maximum(n, 1).astype(np.float32)
    large = 16 + (np.log(f / np.float32(16)) / np.float32(np.log(8.0)) * np.float32(16)).astype(np.int32)
    return np.where(n < 16, n, np.minimum(large, 31))


def constants():
    onehot = np.zeros((33, 2, LINE), np.float32)
    buckets = t5_buckets()
    for x in range(LINE):
        d = T - 1 - x
        for s in range(2):
            ok = d >= 0 and (s == 0 or d < WINDOW)
            onehot[buckets[d] if ok else 32, s, x] = 1.0
    i = np.arange(P)
    eye = np.eye(P, dtype=np.float32)
    same = (i[:, None] // 64 == i[None, :] // 64).astype(np.float32)
    squares = np.concatenate([eye, np.full((P, P), 1.0 / D, np.float32), same, same / 64], 1).astype(np.float32)
    r, c = np.arange(CH)[:, None], np.arange(CH)[None, :]
    m = {"low2": (c < r) & (c // 2 == r // 2), "low2T": (r < c) & (c // 2 == r // 2),
         "upper": r < c, "upper_eq": r <= c, "eye64": r == c}
    for b in LEVELS:
        m[f"off{b}"] = (r // b != c // b) & (r // (2 * b) == c // (2 * b)) & (r < c)
    masks = np.stack([np.concatenate([m[n], m[n]], 0) for n in MASKS], 1).astype(np.float32)
    before = np.broadcast_to((np.arange(8)[None, :] < np.arange(8)[:, None]).astype(np.float32), (P, 8, 8))
    places = np.zeros((P, PASSES * CAP + PASSES + 2 * P), np.float32)
    places[:, :PASSES * CAP] = np.arange(PASSES * CAP)
    places[:, PASSES * CAP:PASSES * CAP + PASSES] = i[:, None] + CAP * np.arange(PASSES)
    places[:, -2 * P:-P] = i[:, None] < i[None, :]
    places[:, -P:] = 1.0
    return {"places": places, "onehot": onehot.reshape(33, 2 * LINE), "squares": squares, "masks": masks,
            "before": np.ascontiguousarray(before)}


def head_order():
    return [4 * (2 * (m // 4) + p) + m % 4 for m in range(8) for p in range(2)]


def layout(x, meta_tokens, rel_bias, ln_mix_g, ln_mix_b, ln_ffn_g, ln_ffn_b, attn_w_qkv, attn_b_qkv, attn_sinks,
           attn_w_o, rwkv_mu, rwkv_w0, rwkv_w1, rwkv_w2, rwkv_a0, rwkv_a1, rwkv_a2, rwkv_g1, rwkv_g2, rwkv_k_k,
           rwkv_k_a, rwkv_r_k, rwkv_w_rkv, rwkv_lnx_g, rwkv_lnx_b, rwkv_w_o, ffn_w_gu, ffn_w_down, moe_router,
           moe_w_gu, moe_w_down):
    order = head_order()
    feats = np.concatenate([np.arange(64 * q, 64 * q + 64) for q in order])
    wqkv, bqkv = attn_w_qkv[0], attn_b_qkv[0]
    wq, wk, wv = wqkv[:, :D][:, feats], wqkv[:, D:D + 256], wqkv[:, D + 256:]
    v_slab = wv.reshape(KC, P, 256).transpose(1, 0, 2).reshape(1, P, KC * 256)
    parts = [slabs_of(tiles_of(np.concatenate([wq, wk], 1))), v_slab, slabs_of(tiles_of(attn_w_o[0][feats])),
             slabs_of(gate_up_tiles(ffn_w_gu[0])), slabs_of(tiles_of(ffn_w_down[0]))]
    parts += [slabs_of(tiles_of(rwkv_w_rkv[0, i])) for i in range(3)] + [slabs_of(tiles_of(rwkv_w_o[0]))]
    for e in range(EXPERTS):
        down = moe_w_down[0, e].reshape(FTE // 2, 2, P, D).transpose(0, 2, 1, 3).reshape(FTE // 2, P, 2 * D)
        parts += [slabs_of(gate_up_tiles(moe_w_gu[0, e])), down]
    vecs = [ln_mix_g[0], ln_mix_b[0], ln_ffn_g[0], ln_ffn_b[0], ln_mix_g[1], ln_mix_b[1], ln_ffn_g[1], ln_ffn_b[1],
            *rwkv_mu[0][[0, 2, 3, 1, 4, 5]], rwkv_w0[0], rwkv_a0[0], rwkv_k_k[0], rwkv_k_a[0],
            rwkv_r_k[0].reshape(-1), rwkv_lnx_g[0], rwkv_lnx_b[0], bqkv[:D][feats], bqkv[D:D + 256]]
    lora1 = np.concatenate([rwkv_w1[0], rwkv_a1[0], rwkv_g1[0]], 1).reshape(KC, P, 288).transpose(1, 0, 2)
    lora2 = np.zeros((P, 4, D), np.float32)
    lora2[0:64, 0], lora2[0:64, 1] = rwkv_w2[0], rwkv_a2[0]
    lora2[:, 2], lora2[0:32, 3] = rwkv_g2[0][0:P], rwkv_g2[0][P:]
    h0 = np.concatenate([meta_tokens, x[0]], 0)
    return {
        "h0": h0.T.reshape(KC, P, T).transpose(1, 0, 2),
        "slabs": np.concatenate(parts, 0),
        "vecs": np.concatenate([chunked(v) for v in vecs], 1),
        "rel_bias": np.concatenate([rel_bias[:, order], np.full((1, HEADS), NEG, np.float32)], 0),
        "b_v": bqkv[None, D + 256:],
        "sinks": attn_sinks[:, order],
        "lora1": lora1, "lora2": lora2,
        "router": moe_router[0].reshape(KC, P, EXPERTS).transpose(1, 0, 2),
        **constants(),
    }


def kernel(**inputs):
    import concourse.bacc as bacc
    from concourse.bass_utils import run_bass_kernel_spmd

    nc = bacc.Bacc("TRN2", target_bir_lowering=False, num_devices=1)
    arrays = {f"in_{n}": np.ascontiguousarray(a) for n, a in
              layout(**{n: np.asarray(a) for n, a in inputs.items()}).items()}
    A = {n[3:]: nc.dram_tensor(n, a.shape, F32, kind="ExternalInput").ap() for n, a in arrays.items()}
    out = nc.dram_tensor("out", (P, KC, SEQ), F32, kind="ExternalOutput").ap()
    build(nc, A, out)
    got = run_bass_kernel_spmd(nc, [arrays], core_ids=[0]).results[0]["out"]
    return np.ascontiguousarray(got.transpose(2, 1, 0).reshape(1, SEQ, D))
```

```python
from contextlib import ExitStack

import numpy as np

import concourse.bass as bass
from concourse import mybir
from concourse.alu_op_type import AluOpType as ALU

F32, I32 = mybir.dt.float32, mybir.dt.int32
F32R = mybir.dt.float32r
ACT = mybir.ActivationFunctionType
AX = mybir.AxisListType

P = 128
D = 1024
KC = D // P
N_META, SEQ = 16, 256
T = N_META + SEQ
HEADS, KV_HEADS, HD = 16, 4, 64
WINDOW = 128
D_FF, D_FFE, EXPERTS = 2816, 3584, 8
FT, FTE = D_FF // P, D_FFE // P
ALPHA = 4 ** 0.25
LN_EPS, GN_EPS = 1e-5, 64e-5
DECAY = float(np.exp(-0.5))
NEG = -1e30

TILES = 16
SLOTS = 7
SL_QK, SL_V, SL_WO = 0, 5, 6
SL_GU = SL_WO + 4
SL_DN = SL_GU + FT
SL_RKV = SL_DN + FT * KC // TILES
SL_O2 = SL_RKV + 12
SL_MOE = SL_O2 + 4
SL_EXPERT = FTE + FTE * KC // TILES
N_SLABS = SL_MOE + EXPERTS * SL_EXPERT

Q_TILES = [(0, 96, 96), (96, 96, 192), (192, 80, 272)]
KN_AT = [0, 96, 288]
KN_ALL = 560
Q_MAX = 96
LINE = 2 * T - 1

CH = 64
N_CH = -(-T // CH)
LEVELS = [2, 4, 8, 16, 32]

VECS = ["g0", "b0", "g1", "b1", "g2", "b2", "g3", "b3", "mu_r", "mu_k", "mu_v", "mu_w", "mu_a", "mu_g",
        "w0", "a0", "k_k", "k_a", "r_k", "lnx_g", "lnx_b", "b_q"]
VCOL = {n: KC * i for i, n in enumerate(VECS)}
VCOL["b_k"] = KC * len(VECS)
N_VEC = KC * len(VECS) + 2


def recurrence_order():
    def halves(names, c, i=0):
        return [(x, c, i, g) for x in names for g in range(2)]

    parts = {}
    for c in range(N_CH):
        more = ["bk"] if c < N_CH - 1 else []
        parts["first", c] = (halves(["b_ra", "k_ra", "l_v"] + more, c),
                             halves(["b_ra", "k_ra", "ttm0", "ttm", "tm0", "tm", "vnat"] + more, c))
        for i in range(len(levels_of(c))):
            parts["level", c, i] = (halves(["u"], c, i) + [(x, c, i, g) for g in range(2) for x in ("tu", "tut")],
                                    halves(["otm", "um", "t+"], c, i))
        parts["x", c] = halves(["x"], c), halves(["xm"], c)
        parts["sa", c] = halves(["sa"], c), halves(["sam"], c)
        parts["y", c] = halves(["y"], c), halves(["y"], c)
        parts["s", c] = halves(["s"], c), halves(["st0", "st"], c)
    order = [("first", 0)] + [("level", 0, i) for i in range(len(levels_of(0)))]
    for c in range(N_CH):
        state = [("x", c), ("sa", c), ("y", c)] + ([("s", c)] if c < N_CH - 1 else [])
        ahead = []
        if c + 1 < N_CH:
            ahead = [("first", c + 1)] + [("level", c + 1, i) for i in range(len(levels_of(c + 1)))]
        while state or ahead:
            if state:
                order.append(state.pop(0))
            if ahead:
                order.append(ahead.pop(0))
    pe = [x for part in order for x in parts[part][0]]
    dve = [x for part in order for x in parts[part][1]]
    return order, {x: n + 1 for n, x in enumerate(pe)}, {x: n + 1 for n, x in enumerate(dve)}


def tokens_of(c):
    return min(CH, T - CH * c)


def levels_of(c):
    return [b for b in LEVELS if b < tokens_of(c)]


PRE_KN, PRE_KK, PRE_SCAN, PRE_LAST = 8, 11, 6, 19
GROUP = 512
GROUPS = D_FFE // GROUP
SL_GROUP = 4
CAP = 96
PASSES = -(-T // CAP)
RT_SEL, RT_EXP, RT_POS, RT_FLAG = 10, 12, 21, 23
GN_OUT = 3
LN_READY = 10
ARENA = 28800
GATHER_AT = 33
PUT_AT = 38
MASKS = ["low2", "low2T", "upper_eq", "upper"] + [f"off{b}" for b in LEVELS] + ["eye64"]


def build(nc, A, OUT):
    ctx = ExitStack()
    with ctx:
        def sb(name, shape, dtype=F32):
            return ctx.enter_context(nc.sbuf_tensor(name, shape, dtype))

        def sem(name):
            return ctx.enter_context(nc.semaphore(name))

        ring = sb("ring", [P, SLOTS, TILES * P])
        h = sb("h", [P, KC, T])
        with nc.sbuf_tensor("z", [P, KC, T], F32) as z, nc.sbuf_tensor("sq", [P, KC, T], F32) as sq:
            pass
        z_r, sq_r = sb("z_rounded", [P, KC, T], F32R), sb("sq_rounded", [P, KC, T], F32R)
        rstd = sb("rstd", [P, T])
        eye = sb("eye", [P, P])
        ones_d = sb("ones_d", [P, P])
        same_head = sb("same_head", [P, P])
        mean_head = sb("mean_head", [P, P])
        masks = sb("masks", [P, len(MASKS), CH])
        vec = sb("vec", [P, N_VEC])
        wc = sb("wc", [P, KC, N_CH])
        to_head = sb("to_head", [P, KC, HEADS])
        from_head = sb("from_head", [HEADS, KC, P])
        with nc.sbuf_tensor("arena", [P, ARENA], F32) as arena:
            pass

        def rounded(name, start, shape):
            with ExitStack() as place:
                if start:
                    place.enter_context(nc.sbuf_tensor(f"before_{name}", [P, start], F32R))
                return place.enter_context(nc.sbuf_tensor(name, shape, F32R))

        PS = ctx.enter_context(nc.psum_tensor("PS", [P, 8, 512], F32))
        scratch = nc.dram_tensor("bias_lines", (HEADS, Q_MAX, 2 * LINE), F32, kind="Internal").ap()

        def carve(start, *shape, memory=arena):
            n = int(np.prod(shape))
            assert start + n <= memory.shape[1], (start, shape)
            v = memory[:, start:start + n]
            if len(shape) == 1:
                return v
            names = "abcd"[:len(shape)]
            return v.rearrange(f"p ({' '.join(names)}) -> p {' '.join(names)}", **dict(zip(names, shape)))

        def v_of(name, m):
            return vec[:, VCOL[name] + m:VCOL[name] + m + 1]

        def v_all(name, n=T):
            return vec[:, VCOL[name]:VCOL[name] + KC].unsqueeze(2).broadcast_to([P, KC, n])

        qk = carve(0, 10, T)
        vn = carve(2720, 3, 256)
        bias = carve(3488, HEADS * KN_ALL)
        sb_ = carve(12448, 2, 2, T + 1)
        pr = carve(13540, 2, 2, T + 1)
        prT = carve(14632, 2, 2, 3, 96)
        o_hi = rounded("o_hi", 15784, [P, KC, T])
        o_lo = rounded("o_lo", 15784 + KC * T, [P, KC, T])
        line = carve(17960, 2 * LINE)
        onehot = carve(19046, 2 * LINE)
        rbias = carve(20132, HEADS)
        bv = carve(20148, 256)
        sinks = carve(20404, HEADS)
        mx = carve(20420, 2)
        negm = carve(20422, 2, 2)
        den = carve(20426, 2, 2)
        rden = carve(20430, 2)
        ones_row = carve(20432, P)

        def bias_of(t):
            qn, kn = Q_TILES[t][1:]
            s = HEADS * KN_AT[t]
            return bias[:, s:s + HEADS * kn].rearrange("p (h k) -> p h k", h=HEADS)

        dh_hi = rounded("dh_hi", 0, [P, FT, T])
        dh_lo = rounded("dh_lo", FT * T, [P, FT, T])
        h_hi = rounded("h_hi", 2 * FT * T, [P, KC, T])
        h_lo = rounded("h_lo", 2 * FT * T + KC * T, [P, KC, T])
        FREE = 2 * (FT + KC) * T
        sg = carve(FREE, T)
        gu = carve(FREE + T, T)
        dh = carve(FREE + 2 * T, 2, T)

        r_ = carve(0, KC, T)
        k_ = carve(2176, KC, T)
        v_ = carve(4352, KC, T)
        kk = carve(6528, KC, T)
        a_ = carve(8704, KC, T)
        cum = carve(10880, KC, T)
        g_ = carve(13056, KC, T)
        OV = 15232
        mix = carve(OV, 2, KC, T)
        mix_hi, mix_lo = sq_r, rounded("mix_lo", 6528, [P, KC, T])
        lora1 = carve(8704, KC, 288)
        lora2 = carve(OV + 5376, 4, D)
        out_hi = rounded("out_hi", 2176, [P, KC, T])
        out_lo = rounded("out_lo", 4352, [P, KC, T])
        t1 = carve(OV, KC, T)
        e1 = carve(OV + T * KC, KC, T)
        em = carve(OV + 2 * T * KC, KC, T)
        restart = z
        slot = [carve(OV + 512 * i, KC, CH) for i in range(7)]
        um, otm, xm, sam, st, *vnat = slot
        pair = [carve(OV + 512 * (7 + 2 * i), 2, KC, CH) for i in range(6)]
        b_ra, k_ra, bk_nat = pair[0:2], pair[2:4], pair[4:6]
        mrb, ltm = [x[:, 0] for x in b_ra], [x[:, 1] for x in b_ra]
        mrk, mak = [x[:, 0] for x in k_ra], [x[:, 1] for x in k_ra]
        bnat, knat = [x[:, 0] for x in bk_nat], [x[:, 1] for x in bk_nat]
        r_kk = arena[:, 0:2 * 6528].rearrange("p (k x) -> p k x", k=2)
        t_both = [carve(OV + 512 * (19 + 2 * i), 2, KC, CH) for i in range(2)]
        tm, ttm = [t[:, 0] for t in t_both], [t[:, 1] for t in t_both]

        x_hi = sb("x_hi", [P, KC, CAP], F32R)
        x_lo = sb("x_lo", [P, KC, CAP], F32R)
        hid_hi = sb("hid_hi", [P, FTE, CAP], F32R)
        hid_lo = sb("hid_lo", [P, FTE, CAP], F32R)
        experts = sb("experts", [P, ARENA - 2 * (2 * TILES * P + (KC + FTE) * CAP)])
        w_hi = sb("w_hi", [P, 2, TILES * P], F32R)
        w_lo = sb("w_lo", [P, 2, TILES * P], F32R)
        taken = [0]

        def next_of(*shape):
            taken[0] += int(np.prod(shape))
            return carve(taken[0] - int(np.prod(shape)), *shape, memory=experts)

        router = next_of(KC, EXPERTS)
        lg = next_of(3, EXPERTS)
        cmp_a = next_of(3, EXPERTS, EXPERTS)
        cmp_b = next_of(3, EXPERTS, EXPERTS)
        before = next_of(EXPERTS, EXPERTS)
        sel = next_of(3, EXPERTS)
        ex = next_of(3, EXPERTS)
        top = next_of(3)
        gates = next_of(3, EXPERTS)
        place = next_of(3, EXPERTS + 1)
        most = next_of(1)
        hn = next_of(3, D)
        yn = next_of(D)
        pick = next_of(3, CAP)
        gated_pick = next_of(3, CAP)
        put = next_of(T)
        sge = next_of(GROUP)
        gue = next_of(GROUP)
        hid_rows = next_of(2, GROUP)
        places = next_of(PASSES * CAP + 2 * P)
        numbers = places[:, 0:PASSES * CAP]
        tri = places[:, PASSES * CAP:PASSES * CAP + P]
        ones = places[:, PASSES * CAP + P:]
        flag = ctx.enter_context(nc.sbuf_tensor("flag", [P, 1], I32))

        loaded = [sem(f"slab_loaded{j}") for j in range(SLOTS)]
        hi_set, slab_taken = sem("slab_rounded"), sem("slab_split")
        hi_free, slab_used = sem("rounded_weights_used"), sem("slab_multiplied")
        h_hi_set, h_split = sem("h_rounded"), sem("h_split")
        dense_sig, dense_gate, gu_free = sem("dense_sigmoid"), sem("dense_gate"), sem("dense_hidden")
        dense_hi, dense_split = sem("dense_hidden_rounded"), sem("dense_hidden_split")
        mix_hi_set, mix_split = sem("mix_rounded"), sem("mix_split")
        out_hi_set, out_split = sem("rwkv_out_rounded"), sem("rwkv_out_split")
        gated = sem("expert_sigmoids")
        rows_set, gate_used = sem("hidden_rows_set"), sem("gate_times_sigmoid")
        hidT_ps, hid_hi_set, hid_split = sem("hidden_T_in_psum"), sem("rounded_hidden_set"), sem("hidden_split")
        x_hi_set, x_split = sem("rounded_tokens_set"), sem("tokens_split")
        s_const = sem("consts_loaded")
        s_attn = sem("attn_consts_loaded")
        s_h0, s_bv, s_sinks = sem("h0_loaded"), sem("value_bias_loaded"), sem("sinks_loaded")
        s_lora = sem("lora_loaded")
        s_router = sem("router_loaded")
        s_line_ps = sem("bias_line_in_psum")
        s_line = sem("bias_line_kept")
        s_line_out = sem("bias_line_stored")
        s_bias = [sem(f"bias{t}_loaded") for t in range(len(Q_TILES))]
        s_ones = sem("ones_row_set")
        qkv_kept = sem("qkv_kept")
        sc_ps, sc_dve = sem("scores_in_psum"), sem("scores_dve_steps")
        sc_exp, sc_norm = sem("probs_exponentiated"), sem("probs_normalised")
        nrm = sem("norm_steps")
        pT_ps, pT_kept = sem("probs_T_in_psum"), sem("probs_T_kept")
        o_ps, o_kept, o_split = sem("attn_out_in_psum"), sem("attn_out_rounded"), sem("attn_out_split")
        scattered = sem("expert_out_scattered")
        zsum = [sem(f"residual{i}_added") for i in range(4)]
        ln_pe = [sem(f"ln{i}_sums") for i in range(4)]
        ln_dve = [sem(f"ln{i}_vector_steps") for i in range(4)]
        ln_act = [sem(f"ln{i}_scalar_steps") for i in range(4)]
        mixed, xx_steps = sem("mixed"), sem("shift_steps")
        rkv_kept = sem("rkv_kept")
        l1_ps, l1_kept = sem("lora_in_psum"), sem("lora_kept")
        l2_ps, l2_kept = sem("lora_out_in_psum"), sem("lora_out_kept")
        pads = sem("pads_cleared")
        pre_dve, pre_act, pre_pe = sem("prep_vector_steps"), sem("prep_scalar_steps"), sem("prep_sums")
        c_dve, c_pe = sem("chunk_vector_steps"), sem("chunk_products")
        gn_dve, gn_act, gn_pe = sem("gn_vector_steps"), sem("gn_scalar_steps"), sem("gn_sums")
        rt_pe, rt_dve, rt_act = sem("router_products"), sem("router_vector_steps"), sem("router_scalar_steps")
        picked, gathered = sem("picks_built"), sem("gathered_in_psum")
        yn_kept = sem("expert_out_kept")
        gated_set, put_ps, put_kept = sem("gated_picks_built"), sem("puts_in_psum"), sem("puts_kept")
        z_whole = sem("all_experts_added")
        s_out = sem("out_stored")

        block = ctx.enter_context(nc.Block())

        @block.sync
        def _(sp):
            sp.dma_start(rbias[0:33, :], A["rel_bias"]).then_inc(s_attn, 16)
            sp.dma_start(onehot[0:33, :], A["onehot"]).then_inc(s_attn, 16)
            sp.dma_start(h[:, :, :], A["h0"]).then_inc(s_h0, 16)
            for j in range(SLOTS):
                sp.dma_start(ring[:, j, :], A["slabs"][j, :, :]).then_inc(loaded[j], 16)
            with sp.Fori(1, N_SLABS // SLOTS) as i:
                for j in range(SLOTS):
                    sp.wait_ge(slab_taken, SLOTS * i + (j - SLOTS + 1))
                    sp.dma_start(ring[:, j:j + 1, :],
                                 A["slabs"][bass.ds(SLOTS * i + j, 1), :, :].rearrange("s p c -> p s c"))\
                      .then_inc(loaded[j], 16)
            for n in range(N_SLABS // SLOTS * SLOTS, N_SLABS):
                sp.wait_ge(slab_taken, n - SLOTS + 1)
                sp.dma_start(ring[:, n % SLOTS, :], A["slabs"][n, :, :]).then_inc(loaded[n % SLOTS], 16)
            sp.wait_ge(rt_dve, RT_FLAG)
            with sp.If(sp.value_load(flag[0:1, 0:1]) > 0):
                with sp.Fori(0, PASSES - 1) as i:
                    with sp.Fori(0, EXPERTS * SL_EXPERT // SLOTS) as c:
                        for j in range(SLOTS):
                            n = N_SLABS + j
                            sp.wait_ge(slab_taken, EXPERTS * SL_EXPERT * i + SLOTS * c + (n - SLOTS + 1))
                            sp.dma_start(ring[:, n % SLOTS:n % SLOTS + 1, :],
                                         A["slabs"][bass.ds(SLOTS * c + (SL_MOE + j), 1), :, :]
                                         .rearrange("s p c -> p s c")).then_inc(loaded[n % SLOTS], 16)
            sp.wait_ge(ln_act[3], LN_READY + 7)
            sp.dma_start(OUT, h[:, :, N_META:T]).then_inc(s_out, 16)
            sp.wait_ge(s_out, 16)

        @block.gpsimd
        def _(pool):
            pool.dma_start(bv[0:1, :], A["b_v"]).then_inc(s_bv, 16)
            pool.dma_start(sinks[:, :], A["sinks"].broadcast_to([P, HEADS])).then_inc(s_sinks, 16)
            pool.dma_start(vec[:, :], A["vecs"]).then_inc(s_const, 16)
            pool.dma_start(eye[:, :], A["squares"][:, 0:P]).then_inc(s_const, 16)
            pool.dma_start(ones_d[:, :], A["squares"][:, P:2 * P]).then_inc(s_const, 16)
            pool.dma_start(same_head[:, :], A["squares"][:, 2 * P:3 * P]).then_inc(s_const, 16)
            pool.dma_start(mean_head[:, :], A["squares"][:, 3 * P:4 * P]).then_inc(s_const, 16)
            pool.dma_start(masks[:, :, :], A["masks"]).then_inc(s_const, 16)
            pool.dma_start(to_head[:, :, :], A["to_head"]).then_inc(s_const, 16)
            pool.dma_start(from_head[:, :, :], A["from_head"]).then_inc(s_const, 16)
            pool.memset(ones_row[0:1, :], 1.0).then_inc(s_ones, 1)
            pool.wait_ge(s_line, 3)
            pool.dma_start(scratch, line[0:HEADS, :].unsqueeze(1).broadcast_to([HEADS, Q_MAX, 2 * LINE]))\
                .then_inc(s_line_out, 16)
            pool.wait_ge(s_line_out, 16)
            for t, (q0, qn, kn) in enumerate(Q_TILES):
                for s, k0, k1 in ((0, 0, N_META), (1, N_META, kn)):
                    src = bass.AP(tensor=scratch.tensor, offset=s * LINE + T - 1 - q0 + k0,
                                  ap=[[2 * LINE - 1, qn], [Q_MAX * 2 * LINE, HEADS], [1, k1 - k0]])
                    pool.dma_start(bias_of(t)[0:qn, :, k0:k1], src).then_inc(s_bias[t], 16)
            pool.wait_ge(ln_act[1], LN_READY + 7)
            pool.wait_ge(slab_used, SL_RKV)
            pool.dma_start(lora1[:, :, :], A["lora1"]).then_inc(s_lora, 16)
            pool.wait_ge(slab_used, SL_O2)
            pool.dma_start(lora2[:, :, :], A["lora2"]).then_inc(s_lora, 16)
            pool.wait_ge(slab_used, SL_MOE)
            pool.dma_start(router[:, :, :], A["router"]).then_inc(s_router, 16)
            pool.dma_start(before[:, :, :], A["before"]).then_inc(s_router, 16)
            pool.dma_start(places, A["places"]).then_inc(s_router, 16)

        @block.tensor
        def _(pe):
            def products(n, b, width, pieces, tokens_stay=False, before=None):
                def mm(out, w, x, start, stop):
                    return pe.matmul(out, x, w, start=start, stop=stop) if tokens_stay else \
                        pe.matmul(out, w, x, start=start, stop=stop)

                pe.wait_ge(hi_set, n + 1)
                for i, (c, hi, lo, out, start, stop) in enumerate(pieces):
                    if before is not None:
                        before(i)
                    w = w_hi[:, b, width * c:width * (c + 1)]
                    mm(out, w, hi, start, False)
                    last = mm(out, w, lo, False, False)
                last.then_inc(hi_free, 1)
                pe.wait_ge(slab_taken, n + 1)
                for c, hi, lo, out, start, stop in pieces:
                    last = mm(out, w_lo[:, b, width * c:width * (c + 1)], hi, False, stop)
                last.then_inc(slab_used, 1)

            def linear(base, outs, chunks, x_hi, x_lo, ready, kept=None, before_out=0):
                for n in range(base, base + outs * chunks // TILES):
                    tiles = [divmod((n - base) * TILES + t, chunks) for t in range(TILES)]

                    def before(t):
                        m, k = tiles[t]
                        if k == 0 and kept is not None and m + before_out >= 8:
                            pe.wait_ge(kept, m + before_out - 7)
                        if m == 0:
                            pe.wait_ge(ready[0], ready[1] + k)

                    products(n, n % 2, P, [(t, x_hi(k), x_lo(k), PS[:, m, 0:T], k == 0, k == chunks - 1)
                                           for t, (m, k) in enumerate(tiles)], before=before)

            def layer_norm(l):
                if l == 3:
                    pe.wait_ge(z_whole, 1)
                for k in range(KC):
                    if l < 3:
                        pe.wait_ge(zsum[l], k + 1)
                    mm = pe.matmul(PS[:, 0, 0:T], ones_d[:, :], z[:, k, :], start=k == 0, stop=k == KC - 1)
                    if l == 0 and k == 0:
                        mm.then_inc(gu_free, 2)
                mm.then_inc(ln_pe[l], 1)
                for k in range(KC):
                    pe.wait_ge(ln_act[l], k + 1)
                    mm = pe.matmul(PS[:, 1, 0:T], ones_d[:, :], sq[:, k, :], start=k == 0, stop=k == KC - 1)
                mm.then_inc(ln_pe[l], 1)

            pe.wait_ge(s_attn, 32)
            for i in range(3):
                n = min(512, 2 * LINE - 512 * i)
                pe.matmul(PS[0:HEADS, i, 0:n], rbias[0:33, :], onehot[0:33, 512 * i:512 * i + n],
                          start=True, stop=True).then_inc(s_line_ps, 1)
            pe.wait_ge(s_line, 3)
            for n in range(SL_QK, SL_V):
                def before(t):
                    m, k = 2 * n + t // 8, t % 8
                    if k == 0 and m >= 8:
                        pe.wait_ge(qkv_kept, m - 7)
                    if m == 0:
                        pe.wait_ge(h_split, k + 1)

                products(n, n % 2, P, [(t, sq_r[:, t % 8, :], z_r[:, t % 8, :], PS[:, (2 * n + t // 8) % 8, 0:T],
                                        t % 8 == 0, t % 8 == 7) for t in range(TILES)], before=before)
            pe.wait_ge(s_ones, 1)
            pe.wait_ge(s_bv, 16)
            pe.wait_ge(qkv_kept, 5)
            tokens = [(t, min(P, T - P * t)) for t in range(3)]
            for t, n in tokens:
                pe.matmul(PS[0:n, 2 + t, 0:256], ones_row[0:1, 0:n], bv[0:1, :], start=True, stop=False)
            products(SL_V, SL_V % 2, 256,
                     [(k, sq_r[:, k, P * t:P * t + n], z_r[:, k, P * t:P * t + n], PS[0:n, 2 + t, 0:256],
                       False, k == KC - 1) for t, n in tokens for k in range(KC)], tokens_stay=True)
            pe.wait_ge(qkv_kept, 13)
            pe.wait_ge(s_const, 128)

            units = [(t, m) for t in range(3) for m in range(8)]

            def scores(u):
                t, m = units[u]
                q0, qn, kn = Q_TILES[t]
                if u >= 2:
                    pe.wait_ge(sc_dve, 4 * (u - 1))
                for p in range(2):
                    o = slice(64 * p, 64 * p + 64)
                    mm = pe.matmul(PS[0:qn, 2 * (u % 2) + p, 0:kn], qk[o, m, q0:q0 + qn],
                                   qk[o, 8 + m // 4, 0:kn], start=True, stop=True)
                mm.then_inc(sc_ps, 1)

            def parts(u):
                kn = Q_TILES[units[u][0]][2]
                return [(i, min(P, kn - P * i)) for i in range(-(-kn // P))]

            def probs_times_values(u):
                t, m = units[u]
                qn = Q_TILES[t][1]
                pe.wait_ge(pT_kept, u + 1)
                if u >= 2:
                    pe.wait_ge(o_split, u - 1)
                for p in range(2):
                    g = 2 * (m // 4) + p
                    for i, n in parts(u):
                        mm = pe.matmul(PS[64 * p:64 * p + 64, 6 + u % 2, 0:qn], vn[0:n, i, 64 * g:64 * g + 64],
                                       prT[0:n, u % 2, p, i, 0:qn], start=i == 0, stop=i == len(parts(u)) - 1)
                mm.then_inc(o_ps, 1)

            scores(0)
            scores(1)
            for u, (t, m) in enumerate(units):
                qn = Q_TILES[t][1]
                if u + 2 < len(units):
                    scores(u + 2)
                pe.wait_ge(sc_norm, u + 1)
                if u:
                    pe.wait_ge(pT_kept, u)
                for p in range(2):
                    for i, n in parts(u):
                        mm = pe.transpose(PS[0:n, 4 + p, 96 * i:96 * i + qn], pr[0:qn, u % 2, p, P * i:P * i + n],
                                          eye[0:qn, 0:qn])
                mm.then_inc(pT_ps, 1)
                if u:
                    probs_times_values(u - 1)
            probs_times_values(len(units) - 1)
            pe.wait_ge(o_split, len(units))
            linear(SL_WO, 8, KC, lambda k: o_hi[:, k, :], lambda k: o_lo[:, k, :], (o_split, 1))
            layer_norm(0)

            with pe.Fori(0, FT // 2) as j:
                for f in range(2):
                    def before(t):
                        if t == 0:
                            pe.wait_ge(gu_free, 2 * j + (f + 1))
                        if f == 0 and t < 8:
                            pe.wait_ge(h_split, KC + t + 1)

                    products(2 * j + (SL_GU + f), (SL_GU + f) % 2, P,
                             [(t, h_hi[:, t % 8, :], h_lo[:, t % 8, :], PS[:, 2 * f + t // 8, 0:T], t % 8 == 0, t % 8 == 7)
                              for t in range(TILES)], before=before)
            pe.wait_ge(gu_free, FT + 2)
            linear(SL_DN, 8, FT, lambda k: dh_hi[:, k, :], lambda k: dh_lo[:, k, :], (dense_split, 1))
            layer_norm(1)

            for i in range(3):
                linear(SL_RKV + 4 * i, 8, KC, lambda k: mix_hi[:, k, :], lambda k: mix_lo[:, k, :],
                       (mix_split, 8 * i + 1), rkv_kept, before_out=8 * i)
            pe.wait_ge(s_lora, 32)
            pe.wait_ge(rkv_kept, 24)
            for i, c0, n, b in ((3, 0, 64, 0), (4, 64, 64, 1), (5, 128, 128, 2), (5, 256, 32, 3)):
                pe.wait_ge(mixed, 8 * (i + 1))
                for k in range(KC):
                    mm = pe.matmul(PS[0:n, b, 0:T], lora1[:, k, c0:c0 + n], mix[:, i % 2, k, :],
                                   start=k == 0, stop=k == KC - 1)
                mm.then_inc(l1_ps, 1)
            pe.wait_ge(l1_kept, 4)
            for i in range(24):
                j, m = i // 8, i % 8
                if i >= 8:
                    pe.wait_ge(l2_kept, i - 7)
                if j < 2:
                    mm = pe.matmul(PS[:, i % 8, 0:T], lora2[0:64, j, m * P:(m + 1) * P], sq[0:64, j, :],
                                   start=True, stop=True)
                else:
                    pe.matmul(PS[:, i % 8, 0:T], lora2[:, 2, m * P:(m + 1) * P], sq[:, 2, :],
                              start=True, stop=False)
                    mm = pe.matmul(PS[:, i % 8, 0:T], lora2[0:32, 3, m * P:(m + 1) * P], sq[0:32, 3, :],
                                   start=False, stop=True)
                mm.then_inc(l2_ps, 1)

            def head_sums(square, x, wait, value, done):
                pe.wait_ge(wait, value)
                for m in range(KC):
                    mm = pe.matmul(PS[:, m, 0:T], square, x(m), start=True, stop=True)
                mm.then_inc(done, 1)

            def head_rows(wait, value, done):
                pe.wait_ge(wait, value)
                for m in range(KC):
                    mm = pe.matmul(PS[0:HEADS, 0, 0:T], to_head[:, m, :], sq[:, m, :], start=m == 0, stop=m == KC - 1)
                mm.then_inc(done, 1)

            def rows_to_features(wait, value, done):
                pe.wait_ge(wait, value)
                for m in range(KC):
                    mm = pe.matmul(PS[:, m, 0:T], from_head[:, m, :], rstd[0:HEADS, :], start=True, stop=True)
                mm.then_inc(done, 1)

            pe.wait_ge(l2_kept, 24)
            head_rows(pre_act, 1, pre_pe)
            rows_to_features(pre_dve, PRE_KN, pre_pe)
            head_sums(same_head[:, :], lambda m: t1[:, m, :], pre_dve, PRE_KK, pre_pe)

            def per_head(g, b, n_out, width, *pairs, col=0):
                for m in range(4 * g, 4 * g + 4):
                    at = col + CH * (m - 4 * g)
                    for i, (lhsT, rhs) in enumerate(pairs):
                        for p in range(2):
                            mm = pe.matmul(PS[64 * p:64 * p + n_out, b + g, at:at + width],
                                           lhsT(m, p), rhs(m, p), start=i == 0, stop=i == len(pairs) - 1)
                mm.then_inc(c_pe, 1)

            def by_feature(x, c):
                return lambda m, p: x[64 * p:64 * p + 64, m, CH * c:CH * c + tokens_of(c)]

            def by_token(x, c, width):
                return lambda m, p: x[64 * p:64 * p + tokens_of(c), m, 0:width]

            def with_r_kk(x, c, g, b):
                n = tokens_of(c)
                for m in range(4 * g, 4 * g + 4):
                    out = PS[:, b + g, 2 * CH * (m % 4):2 * CH * (m % 4 + 1)].rearrange("p (k t) -> p k t", k=2)
                    for p in range(2):
                        mm = pe.matmul(out[64 * p:64 * p + n, :, 0:n], by_feature(x, c)(m, p),
                                       r_kk[64 * p:64 * p + 64, :, T * m + CH * c:T * m + CH * c + n],
                                       start=True, stop=True)
                mm.then_inc(c_pe, 1)

            def transposed(g, b, col, x, n):
                for m in range(4 * g, 4 * g + 4):
                    for p in range(2):
                        mm = pe.matmul(PS[64 * p:64 * p + n, b + g, col + CH * (m % 4):col + CH * (m % 4 + 1)],
                                       x(m, p), masks[64 * p:64 * p + 64, MASKS.index("eye64"), :],
                                       start=True, stop=True)
                return mm

            state = lambda m, p: st[64 * p:64 * p + 64, m, :]
            order, _, DV = recurrence_order()

            def dv(g, name, c, i=0):
                pe.wait_ge(c_dve, DV[name, c, i, g])

            pe.wait_ge(pre_dve, PRE_LAST)
            for part, c, *level in order:
                n, q = tokens_of(c), c % 2
                last = len(levels_of(c)) - 1
                if part == "first":
                    A, B, K, V = (by_feature(x, c) for x in (kk, a_, k_, v_))
                    for g in range(2):
                        if c:
                            dv(g, "t+", c - 1, len(levels_of(c - 1)) - 1)
                        with_r_kk(a_, c, g, 0)
                    for g in range(2):
                        with_r_kk(k_, c, g, 2)
                    for g in range(2):
                        dv(g, "b_ra", c)
                        transposed(g, 0, 256, V, n)
                        per_head(g, 0, n, n, (A, B))
                    if c < N_CH - 1:
                        for g in range(2):
                            dv(g, "k_ra", c)
                            transposed(g, 2, 0, B, n)
                            transposed(g, 2, 256, K, n).then_inc(c_pe, 1)
                elif part == "level":
                    i = level[0]
                    ttc = by_token(ttm[q], c, n)
                    for g in range(2):
                        dv(g, "otm", c, i)
                        per_head(g, 0, n, n, (by_token(otm, c, n), by_token(tm[q], c, n)))
                    for g in range(2):
                        dv(g, "um", c, i)
                        per_head(g, 2, n, n, (ttc, by_token(um, c, n)))
                        per_head(g, 2, n, n, (by_token(um, c, n), ttc), col=256)
                elif part == "x":
                    pairs = [(by_token(mak[q], c, n), by_token(vnat[q], c, CH))]
                    if c:
                        pairs.append((by_feature(kk, c), state))
                    for g in range(2):
                        dv(g, "vnat", c)
                        if c:
                            dv(g, "st", c - 1)
                            dv(g, "y", c - 1)
                        per_head(g, 4, n, CH, *pairs)
                elif part == "sa":
                    for g in range(2):
                        dv(g, "xm", c)
                        dv(g, "t+", c, last)
                        per_head(g, 6, n, CH, (by_token(ttm[q], c, n), by_token(xm, c, CH)))
                elif part == "y":
                    pairs = [(by_token(sam, c, CH), by_token(mrb[q], c, n)),
                             (by_token(vnat[q], c, CH), by_token(mrk[q], c, n))]
                    if c:
                        pairs.append((state, by_feature(r_, c)))
                    for g in range(2):
                        dv(g, "sam", c)
                        per_head(g, 4, 64, n, *pairs)
                else:
                    for g in range(2):
                        per_head(g, 6, 64, CH, (by_token(bnat[q], c, CH), by_token(sam, c, CH)),
                                 (by_token(knat[q], c, CH), by_token(vnat[q], c, CH)))

            head_sums(mean_head[:, :], lambda m: r_[:, m, :], c_dve, len(DV), gn_pe)
            head_rows(gn_act, 1, gn_pe)
            rows_to_features(gn_dve, 3, gn_pe)
            linear(SL_O2, 8, KC, lambda k: out_hi[:, k, :], lambda k: out_lo[:, k, :], (out_split, 1))
            layer_norm(2)

            pe.wait_ge(ln_act[2], LN_READY + 7)
            pe.wait_ge(s_router, 48)
            for t, n in tokens:
                for k in range(KC):
                    mm = pe.matmul(PS[0:n, 6, EXPERTS * t:EXPERTS * (t + 1)], h[:, k, P * t:P * t + n],
                                   router[:, k, :], start=k == 0, stop=k == KC - 1)
            mm.then_inc(rt_pe, 1)
            for t, n in tokens:
                for k in range(KC):
                    mm = pe.transpose(PS[0:n, 2 * t + k // 4, P * (k % 4):P * (k % 4) + P],
                                      h[:, k, P * t:P * t + n], eye[:, :])
            mm.then_inc(rt_pe, 1)
            pe.wait_ge(rt_dve, RT_SEL)
            for t, n in tokens:
                for i in range(t + 1):
                    k = tokens[i][1]
                    mm = pe.matmul(PS[0:n, 7, EXPERTS * t:EXPERTS * (t + 1)], (ones if i < t else tri)[0:k, 0:n],
                                   sel[0:k, i, :], start=i == 0, stop=i == t)
            for t, n in tokens:
                mm = pe.matmul(PS[0:1, 7, 32:32 + EXPERTS], ones[0:n, 0:1], sel[0:n, t, :], start=t == 0, stop=t == 2)
            mm.then_inc(rt_pe, 1)
            pe.wait_ge(rt_act, 1)

            def gather(o, first=False):
                pe.wait_ge(picked, 3 * o + 3)
                if not first:
                    pe.wait_ge(x_split, o)
                for k in range(KC):
                    for t, n in tokens:
                        mm = pe.matmul(PS[:, 4 + k // 4, CAP * (k % 4):CAP * (k % 4 + 1)],
                                       hn[0:n, t, P * k:P * k + P], pick[0:n, t, :], start=t == 0, stop=t == 2)
                mm.then_inc(gathered, 1)

            def expert(q, o, gather_ahead):
                def hidden_transposed(g):
                    pe.wait_ge(rows_set, GROUPS * q + (g + 1))
                    if g >= 2:
                        pe.wait_ge(hid_split, GROUPS * q + (g - 1))
                    for j in range(GROUP // P):
                        mm = pe.transpose(PS[:, 4 + g % 2, CAP * j:CAP * (j + 1)],
                                          hid_rows[0:CAP, g % 2, P * j:P * (j + 1)], eye[0:CAP, 0:CAP])
                    mm.then_inc(hidT_ps, 1)

                pe.wait_ge(x_split, o + 1)
                pe.wait_ge(zsum[3], 8 * q + 1)
                for i in range(SL_EXPERT):
                    g, part = i // SL_GROUP, i % SL_GROUP
                    if g < GROUPS:
                        if part == 0 and g >= 2:
                            pe.wait_ge(rows_set, GROUPS * q + (g - 1))
                        out = PS[0:CAP, 2 * (g % 2) + part // 2, :]
                        pieces = [(k % 4, x_hi[:, k, :], x_lo[:, k, :], out, k == 0, k == KC - 1)
                                  for k in range(4 * (part % 2), 4 * (part % 2) + 4)]
                    else:
                        f = 2 * (i - GROUPS * SL_GROUP)
                        pe.wait_ge(hid_split, GROUPS * q + ((f + 1) * P // GROUP + 1))
                        pieces = [(2 * (k - f) + c, hid_hi[:, k, :], hid_lo[:, k, :], PS[0:CAP, 6 + c, :], k == 0, k == FTE - 1)
                                  for k in (f, f + 1) for c in range(2)]
                    products(SL_EXPERT * q + (SL_MOE + i), (SL_MOE + i) % 2, GROUP, pieces, tokens_stay=True)
                    if i >= 5 and (i - 5) % SL_GROUP == 0 and (i - 5) // SL_GROUP < GROUPS:
                        hidden_transposed((i - 5) // SL_GROUP)
                    if gather_ahead and i == GATHER_AT:
                        pe.wait_ge(hid_split, GROUPS * q + GROUPS)
                        gather(o + 1)
                    if i == PUT_AT:
                        pe.wait_ge(gated_set, 3 * q + 3)
                        pe.wait_ge(hid_split, GROUPS * q + GROUPS)
                        pe.wait_ge(x_split, o + 2 if gather_ahead else o + 1)
                        for t, n in tokens:
                            mm = pe.transpose(PS[0:CAP, 4, P * t:P * t + n], gated_pick[0:n, t, :], eye[0:n, 0:n])
                        mm.then_inc(put_ps, 1)

            def scatter(q):
                pe.wait_ge(put_kept, q + 1)
                for m in range(KC):
                    if m % 4 == 0:
                        pe.wait_ge(yn_kept, 2 * q + 1 + m // 4)
                    if m >= 4:
                        pe.wait_ge(zsum[3], 8 * q + (m - 2))
                    pe.matmul(PS[:, m % 4, 0:T], yn[0:CAP, P * m:P * m + P], put[0:CAP, :],
                              start=True, stop=True).then_inc(scattered, 1)

            gather(0, first=True)
            with pe.Fori(0, EXPERTS) as e:
                expert(e, e, gather_ahead=True)
                scatter(e)
            with pe.If(pe.value_load(flag[0:1, 0:1]) > 0):
                with pe.Fori(1, PASSES) as i:
                    with pe.Fori(0, EXPERTS) as e:
                        q = EXPERTS * i + e
                        gather(q + 1)
                        expert(q, q + 1, gather_ahead=False)
                        scatter(q)
            layer_norm(3)

        @block.scalar
        def _(act):
            def round_slab(n):
                act.wait_ge(loaded[n % SLOTS], 16 * (n // SLOTS + 1))
                if n >= 2:
                    act.wait_ge(hi_free, n - 1)
                    act.wait_ge(slab_taken, n - 1)
                act.activation(w_hi[:, n % 2, :], ring[:, n % SLOTS, :], ACT.Copy).then_inc(hi_set, 1)

            def layer_norm(l):
                for k in range(KC):
                    act.wait_ge(ln_dve[l], k + 1)
                    act.activation(sq[:, k, :], z[:, k, :], ACT.Square).then_inc(ln_act[l], 1)
                act.wait_ge(ln_dve[l], 9)
                act.activation(rstd[:, :], rstd[:, :], ACT.Sqrt).then_inc(ln_act[l], 1)
                for k in range(KC):
                    act.wait_ge(ln_dve[l], 11 + k)
                    act.activation(h[:, k, :], z[:, k, :], ACT.Identity, bias=v_of(f"b{l}", k))\
                       .then_inc(ln_act[l], 1)
                    if l == 0:
                        act.activation(h_hi[:, k, :], z[:, k, :], ACT.Identity, bias=v_of(f"b{l}", k))\
                           .then_inc(h_hi_set, 1)

            act.wait_ge(s_h0, 16)
            for k in range(KC):
                act.activation(sq_r[:, k, :], h[:, k, :], ACT.Copy).then_inc(h_hi_set, 1)
            round_slab(0)
            round_slab(1)
            act.wait_ge(s_const, 128)
            for m in range(10):
                if m % 2 == 0:
                    round_slab(m // 2 + 2)
                act.wait_ge(slab_used, m // 2 + 1)
                b = v_of("b_q", m) if m < 8 else v_of("b_k", m - 8)
                act.activation(qk[:, m, :], PS[:, m % 8, 0:T], ACT.Identity, bias=b).then_inc(qkv_kept, 1)
            round_slab(SL_V + 2)
            act.wait_ge(slab_used, SL_V + 1)
            for t in range(3):
                n = min(P, T - P * t)
                act.activation(vn[0:n, t, :], PS[0:n, 2 + t, 0:256], ACT.Copy).then_inc(qkv_kept, 1)

            units = [(t, m) for t in range(3) for m in range(8)]

            def exps(u):
                q0, qn, kn = Q_TILES[units[u][0]]
                act.wait_ge(sc_dve, 4 * (u + 1))
                for p in range(2):
                    a = act.activation(pr[0:qn, u % 2, p, 0:kn + 1], sb_[0:qn, u % 2, p, 0:kn + 1], ACT.Exp,
                                       bias=negm[0:qn, u % 2, p:p + 1], accum_out=den[0:qn, u % 2, p:p + 1])
                a.then_inc(sc_exp, 1)

            def keep_out(u):
                t, m = units[u]
                q0, qn, kn = Q_TILES[t]
                act.wait_ge(o_ps, u + 1)
                act.activation(o_hi[:, m, q0:q0 + qn], PS[:, 6 + u % 2, 0:qn], ACT.Copy).then_inc(o_kept, 1)

            exps(0)
            for u, (t, m) in enumerate(units):
                q0, qn, kn = Q_TILES[t]
                if u + 1 < len(units):
                    exps(u + 1)
                act.wait_ge(pT_ps, u + 1)
                full, part = kn // P, kn % P
                src = PS[:, 4:6, 0:288].rearrange("p b (i q) -> p b i q", i=3)
                if full:
                    a = act.activation(prT[:, u % 2, :, 0:full, 0:qn], src[:, :, 0:full, 0:qn], ACT.Copy)
                if part:
                    a = act.activation(prT[0:part, u % 2, :, full, 0:qn], src[0:part, :, full, 0:qn], ACT.Copy)
                a.then_inc(pT_kept, 1)
                if u >= 1:
                    keep_out(u - 1)
            keep_out(len(units) - 1)
            for n in range(SL_WO, SL_GU):
                round_slab(n + 2)
            layer_norm(0)

            def round_hidden(f):
                act.wait_ge(gu_free, f + 3)
                act.activation(dh_hi[:, f, :], dh[:, f % 2, :], ACT.Copy).then_inc(dense_hi, 1)

            for f in range(FT):
                round_slab(SL_GU + f + 2)
                act.wait_ge(slab_used, SL_GU + f + 1)
                if f:
                    act.wait_ge(dense_gate, f)
                act.activation(sg[:, :], PS[:, 2 * (f % 2), 0:T], ACT.Sigmoid).then_inc(dense_sig, 1)
                if f:
                    round_hidden(f - 1)
            round_hidden(FT - 1)
            for n in range(SL_DN, SL_RKV):
                round_slab(n + 2)
            layer_norm(1)

            def round_mix(i):
                if i:
                    act.wait_ge(slab_used, SL_RKV + 4 * i)
                for k in range(KC):
                    act.wait_ge(mixed, 8 * i + k + 1)
                    act.activation(mix_hi[:, k, :], mix[:, i % 2, k, :], ACT.Copy).then_inc(mix_hi_set, 1)

            for i in range(3):
                round_mix(i)
                for n in range(SL_RKV + 4 * i, SL_RKV + 4 * (i + 1)):
                    if n + 2 < SL_O2:
                        round_slab(n + 2)
                    act.wait_ge(slab_used, n + 1)
                    for m in (2 * (n - SL_RKV) % 8, 2 * (n - SL_RKV) % 8 + 1):
                        act.activation((r_, k_, v_)[i][:, m, 0:T], PS[:, m, 0:T], ACT.Copy).then_inc(rkv_kept, 1)
            for i, (n, f) in enumerate(((64, ACT.Tanh), (64, ACT.Copy), (128, ACT.Sigmoid), (32, ACT.Sigmoid))):
                act.wait_ge(l1_ps, i + 1)
                act.activation(sq[0:n, i, :], PS[0:n, i, 0:T], f).then_inc(l1_kept, 1)
            for i in range(24):
                j, m = i // 8, i % 8
                act.wait_ge(l2_ps, i + 1)
                if j < 2:
                    a = act.activation((cum, a_)[j][:, m, 0:T], PS[:, m, 0:T], ACT.Sigmoid,
                                       bias=v_of(("w0", "a0")[j], m))
                else:
                    a = act.activation(g_[:, m, :], PS[:, m, 0:T], ACT.Copy)
                a.then_inc(l2_kept, 1)
            act.wait_ge(pre_dve, 1)
            act.activation(sq[:, :, :], kk[:, :, :], ACT.Square).then_inc(pre_act, 1)
            act.wait_ge(pre_dve, PRE_SCAN)
            act.activation(e1[:, :, :], cum[:, :, :], ACT.Exp, scale=-DECAY).then_inc(pre_act, 1)
            act.activation(em[:, :, :], cum[:, :, :], ACT.Exp, scale=DECAY).then_inc(pre_act, 1)
            act.wait_ge(pre_dve, PRE_KN - 1)
            act.activation(rstd[0:HEADS, :], rstd[0:HEADS, :], ACT.Sqrt).then_inc(pre_act, 1)

            act.wait_ge(c_dve, len(recurrence_order()[2]))
            act.wait_ge(c_pe, len(recurrence_order()[1]))
            round_slab(SL_O2)
            act.wait_ge(gn_dve, 1)
            act.activation(sq[:, :, :], r_[:, :, 0:T], ACT.Square).then_inc(gn_act, 1)
            act.wait_ge(gn_dve, 2)
            act.activation(rstd[0:HEADS, :], rstd[0:HEADS, :], ACT.Sqrt).then_inc(gn_act, 1)
            round_slab(SL_O2 + 1)
            for k in range(KC):
                act.wait_ge(gn_dve, GN_OUT + 3 * (k + 1))
                act.activation(out_hi[:, k, :], r_[:, k, 0:T], ACT.Copy).then_inc(out_hi_set, 1)
            for n in range(SL_O2 + 2, SL_MOE):
                round_slab(n)
            layer_norm(2)
            act.wait_ge(rt_pe, 2)
            for t in range(3):
                n = min(P, T - P * t)
                a = act.activation(hn[0:n, t, :].rearrange("p (b c) -> p b c", b=2), PS[0:n, 2 * t:2 * t + 2, :],
                                   ACT.Copy)
            a.then_inc(rt_act, 1)
            act.wait_ge(rt_dve, RT_EXP)
            act.activation(ex[:, :, :], ex[:, :, :], ACT.Exp).then_inc(rt_act, 1)

            def keep_tokens(o):
                act.wait_ge(gathered, o + 1)
                act.activation(x_hi[:, :, :].rearrange("p (i k) c -> p i (k c)", i=2), PS[:, 4:6, 0:4 * CAP],
                               ACT.Copy).then_inc(x_hi_set, 1)

            def expert(q, gather_ahead):
                for i in range(SL_EXPERT):
                    n = SL_MOE + i
                    act.wait_ge(loaded[n % SLOTS], 96 * q + 16 * (n // SLOTS + 1))
                    act.wait_ge(hi_free, SL_EXPERT * q + (n - 1))
                    act.wait_ge(slab_taken, SL_EXPERT * q + (n - 1))
                    act.activation(w_hi[:, n % 2, :], ring[:, n % SLOTS, :], ACT.Copy).then_inc(hi_set, 1)
                    if i % SL_GROUP == 3 and i // SL_GROUP < GROUPS:
                        g = i // SL_GROUP
                        act.wait_ge(slab_used, SL_EXPERT * q + (SL_MOE + SL_GROUP * g + 2))
                        act.wait_ge(gate_used, GROUPS * q + g)
                        act.activation(sge[0:CAP, :], PS[0:CAP, 2 * (g % 2), :], ACT.Sigmoid).then_inc(gated, 1)
                    if i % SL_GROUP == 3 and 1 <= i // SL_GROUP <= GROUPS:
                        g = i // SL_GROUP - 1
                        act.wait_ge(hidT_ps, GROUPS * q + (g + 1))
                        act.activation(hid_hi[:, 4 * g:4 * g + 4, :].rearrange("p k c -> p (k c)"),
                                       PS[:, 4 + g % 2, 0:4 * CAP], ACT.Copy).then_inc(hid_hi_set, 1)
                    if gather_ahead is not None and i == GATHER_AT + 2:
                        keep_tokens(gather_ahead)
                    if i == PUT_AT + 2:
                        act.wait_ge(put_ps, q + 1)
                        act.activation(put[0:CAP, :], PS[0:CAP, 4, 0:T], ACT.Copy).then_inc(put_kept, 1)
                act.wait_ge(slab_used, SL_EXPERT * q + (SL_MOE + SL_EXPERT))
                for i in range(2):
                    act.activation(yn[0:CAP, GROUP * i:GROUP * (i + 1)], PS[0:CAP, 6 + i, :], ACT.Copy)\
                       .then_inc(yn_kept, 1)

            keep_tokens(0)
            with act.Fori(0, EXPERTS) as e:
                expert(e, gather_ahead=e + 1)
            act.wait_ge(rt_dve, RT_FLAG)
            with act.If(act.value_load(flag[0:1, 0:1]) > 0):
                with act.Fori(1, PASSES) as i:
                    with act.Fori(0, EXPERTS) as e:
                        q = EXPERTS * i + e
                        keep_tokens(q + 1)
                        expert(q, gather_ahead=None)
            layer_norm(3)

        @block.vector
        def _(dve):
            class Steps:
                def __init__(self, s, n=0):
                    self.s, self.n = s, n

                def step(self, ins):
                    self.n = self.n + 1
                    ins.then_inc(self.s, 1)
                    dve.wait_ge(self.s, self.n)

                def mark(self, ins):
                    self.n = self.n + 1
                    ins.then_inc(self.s, 1)

            tt = lambda o, a, b, op=ALU.mult: dve.tensor_tensor(out=o, in0=a, in1=b, op=op)

            def split_slab(n):
                dve.wait_ge(hi_set, n + 1)
                if n >= 2:
                    dve.wait_ge(slab_used, n - 1)
                tt(w_lo[:, n % 2, :], ring[:, n % SLOTS, :], w_hi[:, n % 2, :].bitcast(F32), ALU.subtract)\
                    .then_inc(slab_taken, 1)

            def left(lo, x, hi, wait, value, done):
                dve.wait_ge(wait, value)
                tt(lo, x, hi.bitcast(F32), ALU.subtract).then_inc(done, 1)

            def residual(l, base, chunks):
                slabs = KC * chunks // TILES
                for n in range(slabs):
                    dve.wait_ge(slab_used, base + n + 1)
                    for m in range(KC):
                        if (chunks * (m + 1) - 1) // TILES == n:
                            dve.scalar_tensor_tensor(out=z[:, m, :], in0=h[:, m, :], scalar=ALPHA, in1=PS[:, m, 0:T],
                                                     op0=ALU.mult, op1=ALU.add).then_inc(zsum[l], 1)
                    if base + n + 2 < SL_MOE:
                        split_slab(base + n + 2)

            def layer_norm(l):
                s = Steps(ln_dve[l])
                dve.wait_ge(ln_pe[l], 1)
                dve.wait_ge(zsum[l] if l < 3 else z_whole, 8 if l < 3 else 1)
                for k in range(KC):
                    s.mark(dve.tensor_tensor(out=z[:, k, :], in0=z[:, k, :], in1=PS[:, 0, 0:T], op=ALU.subtract))
                dve.wait_ge(ln_pe[l], 2)
                s.mark(dve.tensor_scalar(rstd[:, :], PS[:, 1, 0:T], LN_EPS, None, ALU.add))
                dve.wait_ge(ln_act[l], 9)
                s.step(dve.reciprocal(rstd[:, :], rstd[:, :]))
                for k in range(KC):
                    s.mark(dve.scalar_tensor_tensor(out=z[:, k, :], in0=z[:, k, :], scalar=v_of(f"g{l}", k),
                                                    in1=rstd[:, :], op0=ALU.mult, op1=ALU.mult))

            for i in range(3):
                n = min(512, 2 * LINE - 512 * i)
                dve.wait_ge(s_line_ps, i + 1)
                dve.tensor_copy(line[0:HEADS, 512 * i:512 * i + n], PS[0:HEADS, i, 0:n]).then_inc(s_line, 1)
            for k in range(KC):
                left(z_r[:, k, :], h[:, k, :], sq_r[:, k, :], h_hi_set, k + 1, h_split)
            for n in range(SL_WO + 2):
                split_slab(n)

            units = [(t, m) for t in range(3) for m in range(8)]
            sc, nr = Steps(sc_dve), Steps(nrm)

            def biased(u):
                t, m = units[u]
                q0, qn, kn = Q_TILES[t]
                if m == 0:
                    dve.wait_ge(s_bias[t], 32)
                dve.wait_ge(sc_ps, u + 1)
                if u >= 2:
                    dve.wait_ge(sc_exp, u - 1)
                sc.mark(dve.scalar_tensor_tensor(
                    out=sb_[0:qn, u % 2, :, 0:kn], in0=PS[0:qn, 2 * (u % 2):2 * (u % 2) + 2, 0:kn],
                    scalar=HD ** -0.5, in1=bias_of(t)[0:qn, 2 * m:2 * m + 2, :], op0=ALU.mult, op1=ALU.add))
                sc.step(dve.tensor_copy(sb_[0:qn, u % 2, :, kn:kn + 1],
                                        sinks[0:qn, 2 * m:2 * m + 2].unsqueeze(2)))
                sc.step(dve.tensor_reduce(out=mx[0:qn, :], in_=sb_[0:qn, u % 2, :, 0:kn + 1], axis=AX.X, op=ALU.max))
                sc.mark(dve.tensor_scalar(negm[0:qn, u % 2, :], mx[0:qn, :], -1.0, None, ALU.mult))

            def split_out(u):
                t, m = units[u]
                q0, qn, kn = Q_TILES[t]
                left(o_lo[:, m, q0:q0 + qn], PS[:, 6 + u % 2, 0:qn], o_hi[:, m, q0:q0 + qn], o_kept, u + 1, o_split)

            dve.wait_ge(s_sinks, 16)
            biased(0)
            biased(1)
            for u, (t, m) in enumerate(units):
                q0, qn, kn = Q_TILES[t]
                dve.wait_ge(sc_exp, u + 1)
                if u:
                    dve.wait_ge(sc_norm, u)
                nr.step(dve.reciprocal(rden[0:qn, :], den[0:qn, u % 2, :]))
                for p in range(2):
                    i = dve.tensor_scalar(pr[0:qn, u % 2, p, 0:kn], pr[0:qn, u % 2, p, 0:kn],
                                          rden[0:qn, p:p + 1], None, ALU.mult)
                i.then_inc(sc_norm, 1)
                if u + 2 < len(units):
                    biased(u + 2)
                if u >= 2:
                    split_out(u - 2)
            split_out(len(units) - 2)
            split_out(len(units) - 1)
            residual(0, SL_WO, KC)
            layer_norm(0)
            for k in range(KC):
                dve.wait_ge(ln_act[0], LN_READY + k)
                left(h_lo[:, k, :], h[:, k, :], h_hi[:, k, :], h_hi_set, KC + k + 1, h_split)

            def split_hidden(f):
                left(dh_lo[:, f, :], dh[:, f % 2, :], dh_hi[:, f, :], dense_hi, f + 1, dense_split)

            for f in range(FT):
                split_slab(SL_GU + f + 2)
                dve.wait_ge(dense_sig, f + 1)
                if f:
                    dve.wait_ge(gu_free, f + 2)
                tt(gu[:, :], sg[:, :], PS[:, 2 * (f % 2), 0:T]).then_inc(dense_gate, 1)
                dve.wait_ge(dense_gate, f + 1)
                tt(dh[:, f % 2, :], gu[:, :], PS[:, 2 * (f % 2) + 1, 0:T]).then_inc(gu_free, 1)
                if f:
                    split_hidden(f - 1)
            split_hidden(FT - 1)
            residual(1, SL_DN, FT)
            layer_norm(1)

            dve.wait_ge(ln_act[1], LN_READY + 7)
            s = Steps(xx_steps)
            s.mark(dve.tensor_tensor(out=z[:, :, 1:T], in0=h[:, :, 0:T - 1], in1=h[:, :, 1:T], op=ALU.subtract))
            s.step(dve.tensor_scalar(z[:, :, 0:1], h[:, :, 0:1], -1.0, None, ALU.mult))
            def mixture(i, k):
                name = ("mu_r", "mu_k", "mu_v", "mu_w", "mu_a", "mu_g")[i]
                dve.scalar_tensor_tensor(out=mix[:, i % 2, k, :], in0=z[:, k, :], scalar=v_of(name, k),
                                         in1=h[:, k, :], op0=ALU.mult, op1=ALU.add).then_inc(mixed, 1)

            def split_mix(i, k):
                dve.wait_ge(mixed, 8 * i + k + 1)
                left(mix_lo[:, k, :], mix[:, i % 2, k, :], mix_hi[:, k, :], mix_hi_set, 8 * i + k + 1, mix_split)

            mixture(0, 0)
            for k in range(KC):
                if k + 1 < KC:
                    mixture(0, k + 1)
                split_mix(0, k)
            for i in range(3):
                for n in range(SL_RKV + 4 * i, SL_RKV + 4 * (i + 1)):
                    if n + 2 < SL_O2:
                        split_slab(n + 2)
                    if n == SL_RKV + 4 * i:
                        for k in range(KC):
                            mixture(i + 1, k)
                if i < 2:
                    for k in range(KC):
                        split_mix(i + 1, k)
            for k in range(KC):
                mixture(4, k)
            dve.wait_ge(l1_ps, 1)
            for k in range(KC):
                mixture(5, k)
            s = Steps(pre_dve)
            flat = lambda x: x.rearrange("p a b -> p (a b)")
            dve.wait_ge(rkv_kept, 24)
            s.step(tt(kk[:, :, :], k_[:, :, :], v_all("k_k")))
            s.step(dve.memset(restart[:, :, :], 1.0))
            for c in range(N_CH):
                i = dve.memset(restart[:, :, CH * c:CH * c + 1], 0.0)
            s.step(i)
            dve.wait_ge(l2_kept, 16)
            s.step(dve.scalar_tensor_tensor(out=t1[:, :, :], in0=a_[:, :, :], scalar=-1.0, in1=v_all("k_a"),
                                            op0=ALU.add, op1=ALU.mult))
            s.step(dve.scalar_tensor_tensor(out=k_[:, :, :], in0=t1[:, :, :], scalar=1.0, in1=k_[:, :, :],
                                            op0=ALU.add, op1=ALU.mult))
            s.step(dve.tensor_tensor_scan(flat(cum), flat(restart), flat(cum), 0.0, ALU.mult, ALU.add))
            assert s.n == PRE_SCAN
            dve.wait_ge(pre_pe, 1)
            s.mark(dve.tensor_scalar(rstd[0:HEADS, :], PS[0:HEADS, 0, 0:T], 1e-24, None, ALU.max))
            dve.wait_ge(pre_act, 4)
            s.step(dve.reciprocal(rstd[0:HEADS, :], rstd[0:HEADS, :]))
            assert s.n == PRE_KN
            s.step(tt(t1[:, :, :], r_[:, :, :], k_[:, :, :]))
            s.step(tt(t1[:, :, :], t1[:, :, :], v_all("r_k")))
            dve.wait_ge(pre_pe, 2)
            s.step(tt(kk[:, :, :], kk[:, :, :], PS[:, :, 0:T]))
            assert s.n == PRE_KK
            s.step(dve.scalar_tensor_tensor(out=a_[:, :, :], in0=a_[:, :, :], scalar=-1.0, in1=kk[:, :, :],
                                            op0=ALU.mult, op1=ALU.mult))
            s.step(tt(r_[:, :, :], r_[:, :, :], e1[:, :, :]))
            s.step(tt(a_[:, :, :], a_[:, :, :], em[:, :, :]))
            s.step(tt(k_[:, :, :], k_[:, :, :], em[:, :, :]))
            for c in range(N_CH):
                i = tt(kk[:, :, CH * c + 1:CH * c + tokens_of(c)], kk[:, :, CH * c + 1:CH * c + tokens_of(c)],
                       e1[:, :, CH * c:CH * c + tokens_of(c) - 1])
            s.step(i)
            s.step(dve.tensor_copy(wc[:, :, 0:N_CH - 1], e1[:, :, CH - 1:CH * (N_CH - 1):CH]))
            dve.wait_ge(pre_pe, 3)
            s.step(tt(z[:, :, :], PS[:, :, 0:T], v_[:, :, :]))
            s.step(dve.memset(st[:, :, :], 0.0))
            assert s.n == PRE_LAST

            order, PT, DV = recurrence_order()
            steps = []

            def step(ins):
                ins.then_inc(c_dve, 1)
                steps.append(ins)

            def begin():
                if len(steps) > 1:
                    dve.wait_ge(c_dve, len(steps) - 1)

            def mask(name, n):
                i = MASKS.index(name)
                return masks[:, i:i + 1, 0:n].broadcast_to([P, KC // 2, n])

            for part, c, *level in order:
                n, q = tokens_of(c), c % 2
                i = level[0] if level else 0

                def both(product, out, a, b=None, op=ALU.mult, width=n):
                    for g in range(2):
                        one(g, product, out, a, b, op, width)

                def one(g, product, out, a, b=None, op=ALU.mult, width=n):
                    def half(x):
                        if isinstance(x, int):
                            return PS[:, x + g, 0:256].rearrange("p (m t) -> p m t", m=4)[:, :, 0:width]
                        return x if x.shape[1] == KC // 2 else x[:, 4 * g:4 * g + 4, 0:width]

                    if product:
                        dve.wait_ge(c_pe, PT[product, c, i, g])
                    begin()
                    step(dve.tensor_copy(half(out), half(a)) if b is None else tt(half(out), half(a), half(b), op))

                if part == "first":
                    at = MASKS.index("upper_eq")
                    wide = [P, 2, KC // 2, n]
                    for x, out, b in (("b_ra", b_ra[q], 0), ("k_ra", k_ra[q], 2)):
                        for g in range(2):
                            dve.wait_ge(c_pe, PT[x, c, 0, g])
                            begin()
                            step(tt(out[:, :, 4 * g:4 * g + 4, 0:n],
                                    PS[:, b + g, :].rearrange("p (m k t) -> p k m t", k=2, m=4)[:, :, :, 0:n],
                                    masks[:, at:at + 2, 0:n].unsqueeze(2).broadcast_to(wide)))
                    both(None, ttm[q], ltm[q], mask("low2T", n))
                    both(None, ttm[q], ttm[q], mask("eye64", n), ALU.add)
                    both("l_v", tm[q], 0, mask("low2", n))
                    both(None, tm[q], tm[q], mask("eye64", n), ALU.add)
                    for g in range(2):
                        begin()
                        step(dve.tensor_copy(vnat[q][:, 4 * g:4 * g + 4, :],
                                             PS[:, g, 256:512].rearrange("p (m t) -> p m t", m=4)))
                    if c < N_CH - 1:
                        for g in range(2):
                            dve.wait_ge(c_pe, PT["bk", c, 0, g])
                            begin()
                            step(dve.tensor_copy(bk_nat[q][:, :, 4 * g:4 * g + 4, :],
                                                 PS[:, 2 + g, :].rearrange("p (k m t) -> p k m t", k=2, m=4)))
                elif part == "level":
                    both(None, otm, ltm[q], mask(f"off{LEVELS[i]}", n))
                    both("u", um, 0)
                    for g in range(2):
                        dve.wait_ge(c_pe, PT["tut", c, i, g])
                        begin()
                        t = t_both[q][:, :, 4 * g:4 * g + 4, 0:n]
                        step(tt(t, t, PS[:, 2 + g, :].rearrange("p (k m t) -> p k m t", k=2, m=4)[:, :, :, 0:n], ALU.add))
                elif part == "x":
                    both("x", xm, 4, width=CH)
                elif part == "sa":
                    both("sa", sam, 6, width=CH)
                elif part == "y":
                    both("y", r_[:, :, CH * c:CH * c + n], 4)
                else:
                    both("s", st, st, 6, ALU.add, width=CH)
                    both(None, st, st, wc[:, :, c:c + 1].broadcast_to([P, KC, CH]), width=CH)
            assert len(steps) == len(DV)
            dve.wait_ge(c_dve, len(DV))

            s = Steps(gn_dve)
            y = r_[:, :, :]
            dve.wait_ge(c_pe, len(PT))
            split_slab(SL_O2)
            dve.wait_ge(gn_pe, 1)
            s.step(tt(y, y, PS[:, :, 0:T], ALU.subtract))
            dve.wait_ge(gn_pe, 2)
            s.mark(dve.tensor_scalar(rstd[0:HEADS, :], PS[0:HEADS, 0, 0:T], 1.0 / HD, GN_EPS, ALU.mult, ALU.add))
            dve.wait_ge(gn_act, 2)
            s.step(dve.reciprocal(rstd[0:HEADS, :], rstd[0:HEADS, :]))
            split_slab(SL_O2 + 1)
            dve.wait_ge(gn_pe, 3)
            assert s.n == GN_OUT
            for k in range(KC):
                yk = r_[:, k, 0:T]
                s.step(dve.scalar_tensor_tensor(out=yk, in0=yk, scalar=v_of("lnx_g", k), in1=PS[:, k, 0:T],
                                                op0=ALU.mult, op1=ALU.mult))
                s.step(dve.scalar_tensor_tensor(out=yk, in0=yk, scalar=v_of("lnx_b", k), in1=z[:, k, :],
                                                op0=ALU.add, op1=ALU.add))
                s.mark(tt(yk, yk, g_[:, k, :]))
                if k:
                    dve.wait_ge(gn_dve, s.n - 3)
                    left(out_lo[:, k - 1, :], r_[:, k - 1, 0:T], out_hi[:, k - 1, :], out_hi_set, k, out_split)
            dve.wait_ge(gn_dve, s.n)
            left(out_lo[:, KC - 1, :], r_[:, KC - 1, 0:T], out_hi[:, KC - 1, :], out_hi_set, KC, out_split)
            residual(2, SL_O2, KC)
            layer_norm(2)

            dve.wait_ge(ln_act[2], LN_READY + 7)
            dve.wait_ge(s_router, 48)
            dve.wait_ge(rt_pe, 1)
            s = Steps(rt_dve)
            s.step(dve.memset(lg[:, :, :], 0.0))
            for t in range(3):
                n = min(P, T - P * t)
                s.step(dve.tensor_copy(lg[0:n, t, :], PS[0:n, 6, EXPERTS * t:EXPERTS * (t + 1)]))
            four = [P, 3, EXPERTS, EXPERTS]
            other, own = lg[:, :, :].unsqueeze(2).broadcast_to(four), lg[:, :, :].unsqueeze(3).broadcast_to(four)
            s.step(tt(cmp_a[:, :, :, :], other, own, ALU.is_gt))
            s.step(tt(cmp_b[:, :, :, :], other, own, ALU.is_equal))
            s.step(tt(cmp_b[:, :, :, :], cmp_b[:, :, :, :], before[:, :, :].unsqueeze(1).broadcast_to(four)))
            s.step(tt(cmp_a[:, :, :, :], cmp_a[:, :, :, :], cmp_b[:, :, :, :], ALU.add))
            s.step(dve.tensor_reduce(out=sel[:, :, :], in_=cmp_a[:, :, :, :], axis=AX.X, op=ALU.add))
            s.step(dve.tensor_scalar(sel[:, :, :], sel[:, :, :], 2.0, None, ALU.is_lt))
            assert s.n == RT_SEL
            s.step(dve.tensor_reduce(out=top[:, :], in_=lg[:, :, :], axis=AX.X, op=ALU.max))
            s.step(tt(ex[:, :, :], lg[:, :, :], top[:, :].unsqueeze(2).broadcast_to([P, 3, EXPERTS]), ALU.subtract))
            assert s.n == RT_EXP
            dve.wait_ge(rt_act, 2)
            s.step(tt(gates[:, :, :], ex[:, :, :], sel[:, :, :]))
            s.step(dve.tensor_reduce(out=top[:, :], in_=gates[:, :, :], axis=AX.X, op=ALU.add))
            s.step(dve.reciprocal(top[:, :], top[:, :]))
            s.step(tt(gates[:, :, :], gates[:, :, :], top[:, :].unsqueeze(2).broadcast_to([P, 3, EXPERTS])))
            dve.wait_ge(rt_pe, 3)
            for t in range(3):
                n = min(P, T - P * t)
                s.step(dve.scalar_tensor_tensor(out=place[0:n, t, 0:EXPERTS], in0=PS[0:n, 7, EXPERTS * t:EXPERTS * (t + 1)],
                                                scalar=1.0, in1=sel[0:n, t, :], op0=ALU.add, op1=ALU.mult))
            s.step(dve.tensor_scalar(place[:, 0:2, 0:EXPERTS], place[:, 0:2, 0:EXPERTS], -1.0, None, ALU.add))
            n = T - 2 * P
            s.step(dve.tensor_scalar(place[0:n, 2, 0:EXPERTS], place[0:n, 2, 0:EXPERTS], -1.0, None, ALU.add))
            assert s.n == RT_POS
            s.step(dve.tensor_reduce(out=most[0:1, :], in_=PS[0:1, 7, 32:32 + EXPERTS], axis=AX.X, op=ALU.max))
            s.step(dve.tensor_scalar(flag[0:1, :], most[0:1, :], CAP + 1.0, None, ALU.is_ge))
            assert s.n == RT_FLAG
            dve.memset(place[:, :, EXPERTS:], -1.0).then_inc(pads, 1)
            dve.wait_ge(pads, 1)

            def build_pick(e, first):
                for t in range(3):
                    n = min(P, T - P * t)
                    dve.tensor_scalar(pick[0:n, t:t + 1, :], first[0:n].unsqueeze(1), place[0:n, t, bass.ds(e, 1)]
                                      if e is not None else place[0:n, t, 0:1], None, ALU.is_equal)\
                       .then_inc(picked, 1)

            def build_put(e, first):
                for t in range(3):
                    n = min(P, T - P * t)
                    dve.tensor_scalar(gated_pick[0:n, t:t + 1, :], first[0:n].unsqueeze(1), place[0:n, t, bass.ds(e, 1)],
                                      gates[0:n, t, bass.ds(e, 1)], ALU.is_equal, ALU.mult).then_inc(gated_set, 1)

            def split_tokens(o):
                dve.wait_ge(x_hi_set, o + 1)
                tt(x_lo[:, :, :].rearrange("p (i k) c -> p i (k c)", i=2), PS[:, 4:6, 0:4 * CAP],
                   x_hi[:, :, :].rearrange("p (i k) c -> p i (k c)", i=2).bitcast(F32), ALU.subtract)\
                    .then_inc(x_split, 1)

            def expert(q, gather_ahead):
                for i in range(SL_EXPERT):
                    n = SL_MOE + i
                    dve.wait_ge(hi_set, SL_EXPERT * q + (n + 1))
                    dve.wait_ge(slab_used, SL_EXPERT * q + (n - 1))
                    tt(w_lo[:, n % 2, :], ring[:, n % SLOTS, :], w_hi[:, n % 2, :].bitcast(F32), ALU.subtract)\
                        .then_inc(slab_taken, 1)
                    g = i // SL_GROUP - 1
                    if i % SL_GROUP == 0 and 0 <= g < GROUPS:
                        dve.wait_ge(gated, GROUPS * q + (g + 1))
                        tt(gue[0:CAP, :], sge[0:CAP, :], PS[0:CAP, 2 * (g % 2), :]).then_inc(gate_used, 1)
                    if i % SL_GROUP == 1 and 0 <= g < GROUPS:
                        dve.wait_ge(gate_used, GROUPS * q + (g + 1))
                        dve.wait_ge(slab_used, SL_EXPERT * q + (SL_MOE + SL_GROUP * g + 4))
                        tt(hid_rows[0:CAP, g % 2, :], gue[0:CAP, :], PS[0:CAP, 2 * (g % 2) + 1, :])\
                            .then_inc(rows_set, 1)
                    if i % SL_GROUP == 3 and 0 <= g < GROUPS:
                        dve.wait_ge(hid_hi_set, GROUPS * q + (g + 1))
                        tt(hid_lo[:, 4 * g:4 * g + 4, :].rearrange("p k c -> p (k c)"), PS[:, 4 + g % 2, 0:4 * CAP],
                           hid_hi[:, 4 * g:4 * g + 4, :].rearrange("p k c -> p (k c)").bitcast(F32), ALU.subtract)\
                            .then_inc(hid_split, 1)
                    if gather_ahead is not None and i == GATHER_AT + 2:
                        split_tokens(gather_ahead)
                for m in range(KC):
                    dve.wait_ge(scattered, 8 * q + (m + 1))
                    tt(z[:, m, :], z[:, m, :], PS[:, m % 4, 0:T], ALU.add).then_inc(zsum[3], 1)

            build_pick(None, numbers[:, 0:CAP])
            dve.tensor_scalar(z[:, :, :], h[:, :, :], ALPHA, None, ALU.mult).then_inc(zsum[3], 1)
            split_tokens(0)
            with dve.Fori(0, EXPERTS) as e:
                dve.wait_ge(gathered, e + 1)
                build_pick(e + 1, numbers[:, 0:CAP])
                build_put(e, numbers[:, 0:CAP])
                expert(e, gather_ahead=e + 1)
            with dve.If(dve.value_load(flag[0:1, 0:1]) > 0):
                with dve.Fori(1, PASSES) as i:
                    with dve.Fori(0, EXPERTS) as e:
                        q = EXPERTS * i + e
                        dve.wait_ge(gathered, q + 1)
                        build_pick(e, numbers[:, bass.ds(CAP * i, CAP)])
                        build_put(e, numbers[:, bass.ds(CAP * i, CAP)])
                        split_tokens(q + 1)
                        expert(q, gather_ahead=None)
            dve.memset(most[:, :], 0.0).then_inc(z_whole, 1)
            dve.wait_ge(z_whole, 1)
            layer_norm(3)


def slabs_of(tiles):
    n = tiles.shape[0] // TILES
    return tiles.reshape(n, TILES, P, P).transpose(0, 2, 1, 3).reshape(n, P, TILES * P)


def tiles_of(w):
    k, m = w.shape
    return w.reshape(k // P, P, m // P, P).transpose(2, 0, 1, 3).reshape(-1, P, P)


def gate_up_tiles(w):
    k, f = w.shape
    t = w.reshape(k // P, P, 2, f // 2 // P, P).transpose(3, 2, 0, 1, 4)
    return t.reshape(-1, P, P)


def chunked(v):
    return v.reshape(-1, P).T


def t5_buckets():
    n = np.arange(T)
    f = np.maximum(n, 1).astype(np.float32)
    large = 16 + (np.log(f / np.float32(16)) / np.float32(np.log(8.0)) * np.float32(16)).astype(np.int32)
    return np.where(n < 16, n, np.minimum(large, 31))


def constants():
    onehot = np.zeros((33, 2, LINE), np.float32)
    buckets = t5_buckets()
    for x in range(LINE):
        d = T - 1 - x
        for s in range(2):
            ok = d >= 0 and (s == 0 or d < WINDOW)
            onehot[buckets[d] if ok else 32, s, x] = 1.0
    i = np.arange(P)
    eye = np.eye(P, dtype=np.float32)
    same = (i[:, None] // 64 == i[None, :] // 64).astype(np.float32)
    squares = np.concatenate([eye, np.full((P, P), 1.0 / D, np.float32), same, same / 64], 1).astype(np.float32)
    r, c = np.arange(CH)[:, None], np.arange(CH)[None, :]
    m = {"low2": (c < r) & (c // 2 == r // 2), "low2T": (r < c) & (c // 2 == r // 2),
         "upper": r < c, "upper_eq": r <= c, "eye64": r == c}
    for b in LEVELS:
        m[f"off{b}"] = (r // b != c // b) & (r // (2 * b) == c // (2 * b)) & (r < c)
    masks = np.stack([np.concatenate([m[n], m[n]], 0) for n in MASKS], 1).astype(np.float32)
    before = np.broadcast_to((np.arange(8)[None, :] < np.arange(8)[:, None]).astype(np.float32), (P, 8, 8))
    places = np.zeros((P, PASSES * CAP + 2 * P), np.float32)
    places[:, :PASSES * CAP] = np.arange(PASSES * CAP)
    places[:, -2 * P:-P] = i[:, None] < i[None, :]
    places[:, -P:] = 1.0
    to_head = np.zeros((P, KC, HEADS), np.float32)
    from_head = np.zeros((HEADS, KC, P), np.float32)
    for m in range(KC):
        to_head[i, m, 2 * m + i // 64] = 1.0
        from_head[2 * m + i // 64, m, i] = 1.0
    return {"to_head": to_head, "from_head": from_head, "places": places, "onehot": onehot.reshape(33, 2 * LINE), "squares": squares, "masks": masks,
            "before": np.ascontiguousarray(before)}


def head_order():
    return [4 * (2 * (m // 4) + p) + m % 4 for m in range(8) for p in range(2)]


def layout(x, meta_tokens, rel_bias, ln_mix_g, ln_mix_b, ln_ffn_g, ln_ffn_b, attn_w_qkv, attn_b_qkv, attn_sinks,
           attn_w_o, rwkv_mu, rwkv_w0, rwkv_w1, rwkv_w2, rwkv_a0, rwkv_a1, rwkv_a2, rwkv_g1, rwkv_g2, rwkv_k_k,
           rwkv_k_a, rwkv_r_k, rwkv_w_rkv, rwkv_lnx_g, rwkv_lnx_b, rwkv_w_o, ffn_w_gu, ffn_w_down, moe_router,
           moe_w_gu, moe_w_down):
    order = head_order()
    feats = np.concatenate([np.arange(64 * q, 64 * q + 64) for q in order])
    wqkv, bqkv = attn_w_qkv[0], attn_b_qkv[0]
    wq, wk, wv = wqkv[:, :D][:, feats], wqkv[:, D:D + 256], wqkv[:, D + 256:]
    v_slab = wv.reshape(KC, P, 256).transpose(1, 0, 2).reshape(1, P, KC * 256)
    parts = [slabs_of(tiles_of(np.concatenate([wq, wk], 1))), v_slab, slabs_of(tiles_of(attn_w_o[0][feats])),
             slabs_of(gate_up_tiles(ffn_w_gu[0])), slabs_of(tiles_of(ffn_w_down[0]))]
    parts += [slabs_of(tiles_of(rwkv_w_rkv[0, i])) for i in range(3)] + [slabs_of(tiles_of(rwkv_w_o[0]))]
    for e in range(EXPERTS):
        down = moe_w_down[0, e].reshape(FTE // 2, 2, P, D).transpose(0, 2, 1, 3).reshape(FTE // 2, P, 2 * D)
        gate_up = moe_w_gu[0, e].reshape(2, KC // 2, P, 2, GROUPS, GROUP).transpose(4, 3, 0, 2, 1, 5)
        parts += [gate_up.reshape(GROUPS * SL_GROUP, P, TILES * P), down]
    vecs = [ln_mix_g[0], ln_mix_b[0], ln_ffn_g[0], ln_ffn_b[0], ln_mix_g[1], ln_mix_b[1], ln_ffn_g[1], ln_ffn_b[1],
            *rwkv_mu[0][[0, 2, 3, 1, 4, 5]], rwkv_w0[0], rwkv_a0[0], rwkv_k_k[0], rwkv_k_a[0],
            rwkv_r_k[0].reshape(-1), rwkv_lnx_g[0], rwkv_lnx_b[0], bqkv[:D][feats], bqkv[D:D + 256]]
    lora1 = np.concatenate([rwkv_w1[0], rwkv_a1[0], rwkv_g1[0]], 1).reshape(KC, P, 288).transpose(1, 0, 2)
    lora2 = np.zeros((P, 4, D), np.float32)
    lora2[0:64, 0], lora2[0:64, 1] = rwkv_w2[0], rwkv_a2[0]
    lora2[:, 2], lora2[0:32, 3] = rwkv_g2[0][0:P], rwkv_g2[0][P:]
    h0 = np.concatenate([meta_tokens, x[0]], 0)
    return {
        "h0": h0.T.reshape(KC, P, T).transpose(1, 0, 2),
        "slabs": np.concatenate(parts, 0),
        "vecs": np.concatenate([chunked(v) for v in vecs], 1),
        "rel_bias": np.concatenate([rel_bias[:, order], np.full((1, HEADS), NEG, np.float32)], 0),
        "b_v": bqkv[None, D + 256:],
        "sinks": attn_sinks[:, order],
        "lora1": lora1, "lora2": lora2,
        "router": moe_router[0].reshape(KC, P, EXPERTS).transpose(1, 0, 2),
        **constants(),
    }


def kernel(**inputs):
    import concourse.bacc as bacc
    from concourse.bass_utils import run_bass_kernel_spmd

    nc = bacc.Bacc("TRN2", target_bir_lowering=False, num_devices=1)
    arrays = {f"in_{n}": np.ascontiguousarray(a) for n, a in
              layout(**{n: np.asarray(a) for n, a in inputs.items()}).items()}
    A = {n[3:]: nc.dram_tensor(n, a.shape, F32, kind="ExternalInput").ap() for n, a in arrays.items()}
    out = nc.dram_tensor("out", (P, KC, SEQ), F32, kind="ExternalOutput").ap()
    build(nc, A, out)
    got = run_bass_kernel_spmd(nc, [arrays], core_ids=[0]).results[0]["out"]
    return np.ascontiguousarray(got.transpose(2, 1, 0).reshape(1, SEQ, D))
```
